# Optimizing a Trainium2 kernel written in Bass

```python
import math
import jax
import jax.numpy as jnp
from jax import lax
import numpy as np
import jax, jax.numpy as jnp

D_MODEL = 1024
BATCH = 1
SEQ = 512
DEPTH = 2

HEAD_DIM = 64
MOBA_HEADS = 8
SB_HEADS = 8
MOBA_WIDTH = MOBA_HEADS * HEAD_DIM
SB_WIDTH = SB_HEADS * HEAD_DIM
ATTN_IN = 3 * (MOBA_WIDTH + SB_WIDTH)
ATTN_OUT = MOBA_WIDTH + SB_WIDTH
MOBA_BLOCK = 256
MOBA_TOPK = 3
MOBA_Q_CHUNK = 32
SB_Q_BLOCK = 128
ROPE_THETA = 500000.0
ROPE_DIMS = HEAD_DIM // 4
GDN_HEADS = 8
GDN_HEAD_DIM = 128
GDN_WIDTH = GDN_HEADS * GDN_HEAD_DIM
GDN_IN = 4 * GDN_WIDTH + 2 * GDN_HEADS
GDN_CONV = 4
GDN_CHUNK = 64
FFN_HIDDEN = -(-8 * D_MODEL // (3 * 256)) * 256
N_EVEN = (DEPTH + 1) // 2
N_ODD = DEPTH // 2
EPS = 1e-6


def rmsnorm(x, g):
    xf = x.astype(jnp.float32)
    y = xf * lax.rsqrt(jnp.mean(xf * xf, axis=-1, keepdims=True) + EPS)
    return (y * g.astype(jnp.float32)).astype(x.dtype)

def l2norm(x):
    xf = x.astype(jnp.float32)
    return xf * lax.rsqrt(jnp.sum(xf * xf, axis=-1, keepdims=True) + EPS)

def partial_rope(x, positions):
    half = ROPE_DIMS // 2
    inv_freq = ROPE_THETA ** (-jnp.arange(half, dtype=jnp.float32) * 2.0 / ROPE_DIMS)
    ang = positions.astype(jnp.float32)[:, :, None] * inv_freq
    cos = jnp.cos(ang)[:, :, None, :].astype(x.dtype)
    sin = jnp.sin(ang)[:, :, None, :].astype(x.dtype)
    x1 = x[..., :half]
    x2 = x[..., half:ROPE_DIMS]
    return jnp.concatenate([x1 * cos - x2 * sin, x2 * cos + x1 * sin, x[..., ROPE_DIMS:]], axis=-1)

def moba_attention(q, k, v):
    B, H, T, dh = q.shape
    scale = dh ** -0.5
    n_blk = -(-T // MOBA_BLOCK)
    pad = n_blk * MOBA_BLOCK - T
    kp = jnp.pad(k, ((0, 0), (0, 0), (0, pad), (0, 0)))
    vp = jnp.pad(v, ((0, 0), (0, 0), (0, pad), (0, 0)))
    k_blocks = kp.reshape(B, H, n_blk, MOBA_BLOCK, dh)
    v_blocks = vp.reshape(B, H, n_blk, MOBA_BLOCK, dh)
    k_mean = jnp.mean(k_blocks.astype(jnp.float32), axis=3)
    q_blk = jnp.arange(T) // MOBA_BLOCK
    past = jnp.arange(n_blk)[None, :] < q_blk[:, None]
    gate = jnp.einsum('bhtd,bhnd->bhtn', q.astype(jnp.float32), k_mean)
    gate = jnp.where(past, gate, -jnp.inf)
    n_sel = min(MOBA_TOPK, max(n_blk - 1, 1))
    _, sel = lax.top_k(gate, n_sel)
    sel_valid = sel < q_blk[:, None]

    n_qc = T // MOBA_Q_CHUNK
    def to_chunks(t):
        return jnp.moveaxis(t.reshape((B, H, n_qc, MOBA_Q_CHUNK) + t.shape[3:]), 2, 0)
    b_idx = jnp.arange(B)[:, None, None, None]
    h_idx = jnp.arange(H)[None, :, None, None]
    q_offs = jnp.arange(MOBA_Q_CHUNK)
    k_offs = jnp.arange(MOBA_BLOCK)

    def chunk(args):
        ci, q_c, sel_c, valid_c = args
        t0 = ci * MOBA_Q_CHUNK
        k_sel = k_blocks[b_idx, h_idx, sel_c]
        v_sel = v_blocks[b_idx, h_idx, sel_c]
        s_sel = jnp.einsum('bhqd,bhqnkd->bhqnk', q_c, k_sel).astype(jnp.float32) * scale
        s_sel = jnp.where(valid_c[..., None], s_sel, -jnp.inf)
        s_sel = s_sel.reshape(B, H, MOBA_Q_CHUNK, n_sel * MOBA_BLOCK)
        blk_start = (t0 // MOBA_BLOCK) * MOBA_BLOCK
        k_own = lax.dynamic_slice_in_dim(kp, blk_start, MOBA_BLOCK, axis=2)
        v_own = lax.dynamic_slice_in_dim(vp, blk_start, MOBA_BLOCK, axis=2)
        s_own = jnp.einsum('bhqd,bhkd->bhqk', q_c, k_own).astype(jnp.float32) * scale
        causal = (blk_start + k_offs)[None, :] <= (t0 + q_offs)[:, None]
        s_own = jnp.where(causal, s_own, -jnp.inf)
        p = jax.nn.softmax(jnp.concatenate([s_sel, s_own], axis=-1), axis=-1).astype(v.dtype)
        p_sel = p[..., :n_sel * MOBA_BLOCK].reshape(B, H, MOBA_Q_CHUNK, n_sel, MOBA_BLOCK)
        p_own = p[..., n_sel * MOBA_BLOCK:]
        return (jnp.einsum('bhqnk,bhqnkd->bhqd', p_sel, v_sel)
                + jnp.einsum('bhqk,bhkd->bhqd', p_own, v_own))

    out = lax.map(chunk, (jnp.arange(n_qc), to_chunks(q), to_chunks(sel), to_chunks(sel_valid)))
    return jnp.moveaxis(out, 0, 2).reshape(B, H, T, dh)

def stick_breaking_attention(q, k, v):
    B, H, T, dh = q.shape
    scale = dh ** -0.5
    outs = []
    for t0 in range(0, T, SB_Q_BLOCK):
        t1 = t0 + SB_Q_BLOCK
        z = jnp.einsum('bhqd,bhkd->bhqk', q[:, :, t0:t1], k[:, :, :t1]).astype(jnp.float32) * scale
        causal = jnp.arange(t1)[None, :] < jnp.arange(t0, t1)[:, None]
        log_1m = jnp.where(causal, jax.nn.log_sigmoid(-z), 0.0)
        log_after = lax.cumsum(log_1m, axis=3, reverse=True) - log_1m
        w = jnp.where(causal, jnp.exp(jax.nn.log_sigmoid(z) + log_after), 0.0)
        outs.append(jnp.einsum('bhqk,bhkd->bhqd', w.astype(v.dtype), v[:, :, :t1]))
    return jnp.concatenate(outs, axis=2)

def attention_head_groups(h, positions, w_in, w_out):
    B, T, _ = h.shape
    proj = h @ w_in
    cuts = [MOBA_WIDTH, 2 * MOBA_WIDTH, 3 * MOBA_WIDTH,
            3 * MOBA_WIDTH + SB_WIDTH, 3 * MOBA_WIDTH + 2 * SB_WIDTH]
    qa, ka, va, qb, kb, vb = (t.reshape(B, T, -1, HEAD_DIM) for t in jnp.split(proj, cuts, axis=-1))
    qa = partial_rope(qa, positions)
    ka = partial_rope(ka, positions)
    def bhtd(t):
        return t.transpose(0, 2, 1, 3)
    oa = moba_attention(bhtd(qa), bhtd(ka), bhtd(va))
    ob = stick_breaking_attention(bhtd(qb), bhtd(kb), bhtd(vb))
    o = jnp.concatenate([oa, ob], axis=1).transpose(0, 2, 1, 3).reshape(B, T, ATTN_OUT)
    return o @ w_out

def causal_depthwise_conv(x, w):
    ch = x.shape[-1]
    return lax.conv_general_dilated(
        x, w[:, None, :].astype(x.dtype), window_strides=(1,), padding=[(GDN_CONV - 1, 0)],
        dimension_numbers=('NWC', 'WIO', 'NWC'), feature_group_count=ch)

def chunk_gated_delta_rule(q, k, v, g, beta):
    B, T, H, dk = q.shape
    dv = v.shape[-1]
    C = GDN_CHUNK
    N = T // C
    def chunks(t):
        t = t.astype(jnp.float32).reshape((B, N, C, H) + t.shape[3:])
        return t.transpose((0, 3, 1, 2) + tuple(range(4, t.ndim)))
    q, k, v, g, beta = (chunks(t) for t in (q, k, v, g, beta))
    g = jnp.cumsum(g, axis=-1)
    idx = jnp.arange(C)
    incl = idx[:, None] >= idx[None, :]
    strict = idx[:, None] > idx[None, :]
    decay = jnp.exp(jnp.where(incl, g[..., :, None] - g[..., None, :], -jnp.inf))
    k_beta = k * beta[..., None]
    lower = jnp.where(strict, jnp.einsum('bhncd,bhnsd->bhncs', k_beta, k) * decay, 0.0)
    eye = jnp.eye(C, dtype=jnp.float32)
    rhs = jnp.concatenate([v * beta[..., None], k_beta * jnp.exp(g)[..., None]], axis=-1)
    sol = lax.linalg.triangular_solve(lower + eye, rhs, left_side=True, lower=True, unit_diagonal=True)
    u, w = sol[..., :dv], sol[..., dv:]
    attn = jnp.einsum('bhncd,bhnsd->bhncs', q, k) * decay

    def step(state, xs):
        q_c, k_c, u_c, w_c, g_c, a_c = xs
        v_new = u_c - jnp.einsum('bhcd,bhde->bhce', w_c, state)
        o = (jnp.einsum('bhcd,bhde->bhce', q_c * jnp.exp(g_c)[..., None], state)
             + jnp.einsum('bhcs,bhse->bhce', a_c, v_new))
        g_last = g_c[..., -1]
        k_dec = k_c * jnp.exp(g_last[..., None] - g_c)[..., None]
        state = state * jnp.exp(g_last)[..., None, None] + jnp.einsum('bhcd,bhce->bhde', k_dec, v_new)
        return state, o

    xs = tuple(jnp.moveaxis(t, 2, 0) for t in (q, k, u, w, g, attn))
    state0 = jnp.zeros((B, H, dk, dv), jnp.float32)
    _, o = lax.scan(step, state0, xs)
    return o.transpose(1, 0, 3, 2, 4).reshape(B, T, H, dv)

def gated_deltanet(h, w_in, conv_w, a_log, dt_bias, norm_g, w_out):
    B, T, _ = h.shape
    proj = h @ w_in
    qkv = jax.nn.silu(causal_depthwise_conv(proj[..., :3 * GDN_WIDTH], conv_w))
    z = proj[..., 3 * GDN_WIDTH:4 * GDN_WIDTH].reshape(B, T, GDN_HEADS, GDN_HEAD_DIM)
    a = proj[..., 4 * GDN_WIDTH:4 * GDN_WIDTH + GDN_HEADS].astype(jnp.float32)
    b = proj[..., 4 * GDN_WIDTH + GDN_HEADS:].astype(jnp.float32)
    q, k, v = (t.reshape(B, T, GDN_HEADS, GDN_HEAD_DIM) for t in jnp.split(qkv, 3, axis=-1))
    q = l2norm(q) * GDN_HEAD_DIM ** -0.5
    k = l2norm(k)
    beta = jax.nn.sigmoid(b)
    g = -jnp.exp(a_log.astype(jnp.float32)) * jax.nn.softplus(a + dt_bias.astype(jnp.float32))
    o = chunk_gated_delta_rule(q, k, v, g, beta)
    o = rmsnorm(o, norm_g) * jax.nn.silu(z.astype(jnp.float32))
    return o.reshape(B, T, GDN_WIDTH).astype(h.dtype) @ w_out

def swiglu(h, w_in, w_out):
    gate, up = jnp.split(h @ w_in, 2, axis=-1)
    return (jax.nn.silu(gate) * up) @ w_out

def first_inputs(seed: int = 0) -> dict:
    key = jax.random.key(seed)
    ks = jax.random.split(key, 18)
    f32 = jnp.float32
    def dense(k, shape, fan_in, s=1.0):
        return jax.random.normal(k, shape, f32) * (s * fan_in ** -0.5)
    def gain(k, shape):
        return 1.0 + 0.05 * jax.random.normal(k, shape, f32)
    x = jax.random.normal(ks[0], (BATCH, SEQ, D_MODEL), f32)
    c = jax.random.normal(ks[1], (BATCH, D_MODEL), f32)
    offset = jax.random.randint(ks[2], (BATCH, 1), 0, 1024, dtype=jnp.int32)
    positions = offset + jnp.arange(SEQ, dtype=jnp.int32)[None, :]
    ada_w = dense(ks[3], (DEPTH, D_MODEL, 6 * D_MODEL), D_MODEL, 0.5)
    ada_b = 0.02 * jax.random.normal(ks[4], (DEPTH, 6 * D_MODEL), f32)
    norm_mix_g = gain(ks[5], (DEPTH, D_MODEL))
    norm_ffn_g = gain(ks[6], (DEPTH, D_MODEL))
    attn_w_in = dense(ks[7], (N_EVEN, D_MODEL, ATTN_IN), D_MODEL)
    attn_w_out = dense(ks[8], (N_EVEN, ATTN_OUT, D_MODEL), ATTN_OUT)
    gdn_w_in = dense(ks[9], (N_ODD, D_MODEL, GDN_IN), D_MODEL)
    gdn_conv_w = dense(ks[10], (N_ODD, GDN_CONV, 3 * GDN_WIDTH), GDN_CONV)
    gdn_a_log = jnp.log(jax.random.uniform(ks[11], (N_ODD, GDN_HEADS), f32, 1.0, 16.0))
    dt = jnp.exp(jax.random.uniform(ks[12], (N_ODD, GDN_HEADS), f32, math.log(1e-3), math.log(1e-1)))
    gdn_dt_bias = dt + jnp.log(-jnp.expm1(-dt))
    gdn_norm_g = gain(ks[13], (N_ODD, GDN_HEAD_DIM))
    gdn_w_out = dense(ks[14], (N_ODD, GDN_WIDTH, D_MODEL), GDN_WIDTH)
    ffn_w_in = dense(ks[15], (DEPTH, D_MODEL, 2 * FFN_HIDDEN), D_MODEL)
    ffn_w_out = dense(ks[16], (DEPTH, FFN_HIDDEN, D_MODEL), FFN_HIDDEN)
    final_norm_g = gain(ks[17], (D_MODEL,))
    return {'x': x, 'c': c, 'positions': positions, 'ada_w': ada_w, 'ada_b': ada_b,
            'norm_mix_g': norm_mix_g, 'norm_ffn_g': norm_ffn_g,
            'attn_w_in': attn_w_in, 'attn_w_out': attn_w_out,
            'gdn_w_in': gdn_w_in, 'gdn_conv_w': gdn_conv_w, 'gdn_a_log': gdn_a_log,
            'gdn_dt_bias': gdn_dt_bias, 'gdn_norm_g': gdn_norm_g, 'gdn_w_out': gdn_w_out,
            'ffn_w_in': ffn_w_in, 'ffn_w_out': ffn_w_out, 'final_norm_g': final_norm_g}

def first_block(x, c, positions, ada_w, ada_b, norm_mix_g, norm_ffn_g, attn_w_in, attn_w_out,
              gdn_w_in, gdn_conv_w, gdn_a_log, gdn_dt_bias, gdn_norm_g, gdn_w_out,
              ffn_w_in, ffn_w_out, final_norm_g):
    cond = jax.nn.silu(c)
    for layer in range(DEPTH):
        mod = (cond @ ada_w[layer] + ada_b[layer])[:, None, :]
        shift_m, scale_m, gate_m, shift_f, scale_f, gate_f = jnp.split(mod, 6, axis=-1)
        h = rmsnorm(x, norm_mix_g[layer]) * (1.0 + scale_m) + shift_m
        i = layer // 2
        if layer % 2 == 0:
            mixed = attention_head_groups(h, positions, attn_w_in[i], attn_w_out[i])
        else:
            mixed = gated_deltanet(h, gdn_w_in[i], gdn_conv_w[i], gdn_a_log[i], gdn_dt_bias[i],
                                   gdn_norm_g[i], gdn_w_out[i])
        x = x + gate_m * mixed
        h = rmsnorm(x, norm_ffn_g[layer]) * (1.0 + scale_f) + shift_f
        x = x + gate_f * swiglu(h, ffn_w_in[layer], ffn_w_out[layer])
    return rmsnorm(x, final_norm_g)


GRID_W = 64
CTX_LEN = 256
N_GROUPS = 4
GROUP_W = D_MODEL // N_GROUPS
A_HEADS = GROUP_W // HEAD_DIM
A_KV_HEADS = A_HEADS // 2
A_WINDOW = 128
BLK = 128
CONV_CH = GROUP_W
CONV_K = 31
C_HEADS = GROUP_W // HEAD_DIM
C_QK_DIM = HEAD_DIM // 2
C_V_DIM = HEAD_DIM
D_HEADS = GROUP_W // HEAD_DIM
NA_KH = 8
NA_KW = 16
FFN_HIDDEN_2 = -(-8 * D_MODEL // (3 * 256)) * 256

PROJ_SIZES = (A_HEADS * HEAD_DIM, A_KV_HEADS * HEAD_DIM, A_KV_HEADS * HEAD_DIM,
              2 * CONV_CH,
              C_HEADS * 2 * C_QK_DIM, C_HEADS * 2 * C_QK_DIM, C_HEADS * C_V_DIM,
              D_HEADS * HEAD_DIM, D_HEADS * HEAD_DIM, D_HEADS * HEAD_DIM)
IN_WIDTH = sum(PROJ_SIZES)
SPLIT_IDX = tuple(int(v) for v in np.cumsum(PROJ_SIZES)[:-1])
MIX_WIDTH = A_HEADS * HEAD_DIM + CONV_CH + C_HEADS * C_V_DIM + D_HEADS * HEAD_DIM
ROPE_BASE = 10000.0
NEG_INF = -1e30


def rmsnorm_2(x, g):
    xf = x.astype(jnp.float32)
    r = lax.rsqrt(jnp.mean(xf * xf, axis=-1, keepdims=True) + EPS)
    return (xf * r).astype(x.dtype) * g

def layernorm(x, g, b):
    xf = x.astype(jnp.float32)
    mu = jnp.mean(xf, axis=-1, keepdims=True)
    var = jnp.mean(jnp.square(xf - mu), axis=-1, keepdims=True)
    return ((xf - mu) * lax.rsqrt(var + EPS)).astype(x.dtype) * g + b

def modulate(h, shift, scale):
    return h * (1 + scale) + shift

def axial_rope(n_tok, dim):
    t = jnp.arange(n_tok)
    row = (t // GRID_W).astype(jnp.float32)
    col = (t % GRID_W).astype(jnp.float32)
    nf = dim // 4
    inv = ROPE_BASE ** (-jnp.arange(nf, dtype=jnp.float32) / nf)
    ang = jnp.concatenate([row[:, None] * inv, col[:, None] * inv], axis=-1)
    return jnp.cos(ang), jnp.sin(ang)

def apply_rope(x, cos, sin):
    half = x.shape[-1] // 2
    shape = (1, x.shape[1]) + (1,) * (x.ndim - 3) + (half,)
    cs = cos.reshape(shape).astype(x.dtype)
    sn = sin.reshape(shape).astype(x.dtype)
    x1, x2 = x[..., :half], x[..., half:]
    return jnp.concatenate([x1 * cs - x2 * sn, x1 * sn + x2 * cs], axis=-1)

def project(h, w_in):
    b, n = h.shape[:2]
    qa, ka, va, ub, qc, kc, vc, qd, kd, vd = jnp.split(h @ w_in, SPLIT_IDX, axis=-1)
    return (qa.reshape(b, n, A_HEADS, HEAD_DIM), ka.reshape(b, n, A_KV_HEADS, HEAD_DIM),
            va.reshape(b, n, A_KV_HEADS, HEAD_DIM), ub,
            qc.reshape(b, n, C_HEADS, 2, C_QK_DIM), kc.reshape(b, n, C_HEADS, 2, C_QK_DIM),
            vc.reshape(b, n, C_HEADS, C_V_DIM),
            qd.reshape(b, n, D_HEADS, HEAD_DIM), kd.reshape(b, n, D_HEADS, HEAD_DIM),
            vd.reshape(b, n, D_HEADS, HEAD_DIM))

def ctx_attn(q, k, v, sink=None):
    b, l, h, d = q.shape
    g = k.shape[2]
    r = h // g
    qg = q.reshape(b, l, g, r, d)
    s = jnp.einsum('blgrd,bmgd->bgrlm', qg, k).astype(jnp.float32) * (d ** -0.5)
    if sink is not None:
        s_sink = jnp.broadcast_to(sink.astype(jnp.float32).reshape(1, g, r, 1, 1), s.shape[:-1] + (1,))
        s = jnp.concatenate([s, s_sink], axis=-1)
    p = jax.nn.softmax(s, axis=-1)[..., :l].astype(v.dtype)
    return jnp.einsum('bgrlm,bmgd->blgrd', p, v).reshape(b, l, h * d)

def window_gqa(q, k, v, kc, vc, sink):
    b, s_len, h, d = q.shape
    g = k.shape[2]
    r = h // g
    nb = s_len // BLK
    qb = q.reshape(b, nb, BLK, g, r, d)

    def band(t):
        tp = jnp.pad(t, ((0, 0), (BLK, BLK), (0, 0), (0, 0))).reshape(b, nb + 2, BLK, g, d)
        return jnp.concatenate([tp[:, :-2], tp[:, 1:-1], tp[:, 2:]], axis=2)

    kb, vb = band(k), band(v)
    scale = d ** -0.5
    s_loc = jnp.einsum('bnqgrd,bnkgd->bgrnqk', qb, kb).astype(jnp.float32) * scale
    s_ctx = jnp.einsum('bnqgrd,blgd->bgrnql', qb, kc).astype(jnp.float32) * scale
    blocks = jnp.arange(nb)[:, None, None] * BLK
    qpos = blocks + jnp.arange(BLK)[None, :, None]
    kpos = blocks + jnp.arange(3 * BLK)[None, None, :] - BLK
    valid = (jnp.abs(qpos - kpos) <= A_WINDOW) & (kpos >= 0) & (kpos < s_len)
    s_loc = jnp.where(valid, s_loc, NEG_INF)
    s_sink = jnp.broadcast_to(sink.astype(jnp.float32).reshape(1, g, r, 1, 1, 1), s_ctx.shape[:-1] + (1,))
    p = jax.nn.softmax(jnp.concatenate([s_loc, s_ctx, s_sink], axis=-1), axis=-1).astype(v.dtype)
    nk = 3 * BLK
    l = kc.shape[1]
    out = (jnp.einsum('bgrnqk,bnkgd->bnqgrd', p[..., :nk], vb)
           + jnp.einsum('bgrnql,blgd->bnqgrd', p[..., nk:nk + l], vc))
    return out.reshape(b, s_len, h * d)

def conformer_conv(u, w_dw, b_dw, ln_g, ln_b):
    a, gate = jnp.split(u, 2, axis=-1)
    h = a * jax.nn.sigmoid(gate)
    h = lax.conv_general_dilated(h, w_dw, window_strides=(1,),
                                 padding=((CONV_K // 2, CONV_K // 2),),
                                 dimension_numbers=('NWC', 'WIO', 'NWC'),
                                 feature_group_count=CONV_CH) + b_dw
    return jax.nn.silu(layernorm(h, ln_g, ln_b))

def diff_weights(q, k, v, lam):
    s = jnp.einsum('bqhmd,bkhmd->bhmqk', q, k).astype(jnp.float32) * (C_QK_DIM ** -0.5)
    p = jax.nn.softmax(s, axis=-1)
    w = (p[:, :, 0] - lam * p[:, :, 1]).astype(v.dtype)
    return jnp.einsum('bhqk,bkhd->bqhd', w, v)

def diff_out(o, subln_g, lambda_init):
    b, n, h, dv = o.shape
    return (rmsnorm_2(o, subln_g) * (1.0 - lambda_init)).reshape(b, n, h * dv)

def diff_attention_latent(q, k, v, kc, vc, lam):
    b, s_len = q.shape[:2]
    nb = s_len // BLK
    keys = jnp.concatenate([k, kc], axis=1)
    vals = jnp.concatenate([v, vc], axis=1)
    qb = jnp.moveaxis(q.reshape(b, nb, BLK, C_HEADS, 2, C_QK_DIM), 1, 0)
    o = lax.map(lambda qi: diff_weights(qi, keys, vals, lam), qb)
    return jnp.moveaxis(o, 0, 1).reshape(b, s_len, C_HEADS, C_V_DIM)

def neighbourhood_attn(q, k, v, kc, vc, rpb):
    b, s_len, h, d = q.shape
    rows = s_len // GRID_W
    kh = min(NA_KH, rows)
    qg = q.reshape(b, rows, GRID_W, h, d)
    kg = k.reshape(b, rows, GRID_W, h, d)
    vg = v.reshape(b, rows, GRID_W, h, d)
    r = jnp.arange(rows)
    rs = jnp.clip(r - kh // 2, 0, rows - kh)
    rows_idx = rs[:, None] + jnp.arange(kh)[None, :]
    kw_ = kg[:, rows_idx]
    vw_ = vg[:, rows_idx]
    cq = jnp.arange(GRID_W)
    cs = jnp.clip(cq - NA_KW // 2, 0, GRID_W - NA_KW)
    col_valid = (cq[None, :] >= cs[:, None]) & (cq[None, :] < cs[:, None] + NA_KW)
    dr = rows_idx - r[:, None] + (NA_KH - 1)
    dc = jnp.clip(cq[None, :] - cq[:, None], -(NA_KW - 1), NA_KW - 1) + (NA_KW - 1)
    bias = rpb.astype(jnp.float32)[:, dr[:, None, :, None], dc[None, :, None, :]]
    scale = d ** -0.5
    s_loc = jnp.einsum('brqhd,brkwhd->bhrqkw', qg, kw_).astype(jnp.float32) * scale + bias[None]
    s_loc = jnp.where(col_valid[:, None, :], s_loc, NEG_INF).reshape(b, h, rows, GRID_W, kh * GRID_W)
    s_ctx = jnp.einsum('brqhd,blhd->bhrql', qg, kc).astype(jnp.float32) * scale
    p = jax.nn.softmax(jnp.concatenate([s_loc, s_ctx], axis=-1), axis=-1).astype(v.dtype)
    nk = kh * GRID_W
    p_loc = p[..., :nk].reshape(b, h, rows, GRID_W, kh, GRID_W)
    out = (jnp.einsum('bhrqkw,brkwhd->brqhd', p_loc, vw_)
           + jnp.einsum('bhrql,blhd->brqhd', p[..., nk:], vc))
    return out.reshape(b, s_len, h * d)

def hybrid_mixer(hx, hc, w_in, w_out, sink, conv_w, conv_b, conv_ln_g, conv_ln_b,
                 lam, subln_g, lambda_init, rpb, rope_a, rope_c, ctx_out):
    qa, ka, va, ub, qc, kc, vc, qd, kd, vd = project(hx, w_in)
    qa_c, ka_c, va_c, ub_c, qc_c, kc_c, vc_c, qd_c, kd_c, vd_c = project(hc, w_in)
    qa, ka = apply_rope(qa, *rope_a), apply_rope(ka, *rope_a)
    qc, kc = apply_rope(qc, *rope_c), apply_rope(kc, *rope_c)
    y_a = window_gqa(qa, ka, va, ka_c, va_c, sink)
    y_b = conformer_conv(ub, conv_w, conv_b, conv_ln_g, conv_ln_b)
    y_c = diff_out(diff_attention_latent(qc, kc, vc, kc_c, vc_c, lam), subln_g, lambda_init)
    y_d = neighbourhood_attn(qd, kd, vd, kd_c, vd_c, rpb)
    yx = jnp.concatenate([y_a, y_b, y_c, y_d], axis=-1) @ w_out
    if not ctx_out:
        return yx, None
    yc_a = ctx_attn(qa_c, ka_c, va_c, sink)
    yc_b = conformer_conv(ub_c, conv_w, conv_b, conv_ln_g, conv_ln_b)
    yc_c = diff_out(diff_weights(qc_c, kc_c, vc_c, lam), subln_g, lambda_init)
    yc_d = ctx_attn(qd_c, kd_c, vd_c)
    yc = jnp.concatenate([yc_a, yc_b, yc_c, yc_d], axis=-1) @ w_out
    return yx, yc

def swiglu_2(h, w_gate, w_up, w_down):
    return (jax.nn.silu(h @ w_gate) * (h @ w_up)) @ w_down

def second_inputs(seed: int = 0) -> dict:
    key = jax.random.key(seed)
    ks = jax.random.split(key, 25)
    nrm = lambda k, shape, s: jax.random.normal(k, shape, jnp.float32) * s
    D, F = D_MODEL, FFN_HIDDEN_2
    return {
        'x': nrm(ks[0], (BATCH, SEQ, D), 1.0),
        'c': nrm(ks[1], (BATCH, D), 1.0),
        'ctx': nrm(ks[2], (BATCH, CTX_LEN, D), 1.0),
        'c_ctx': nrm(ks[3], (D,), 1.0),
        'norm1_g': 1.0 + nrm(ks[4], (DEPTH, D), 0.1),
        'norm2_g': 1.0 + nrm(ks[5], (DEPTH, D), 0.1),
        'w_ada': nrm(ks[6], (DEPTH, D, 6 * D), 0.5 * D ** -0.5),
        'b_ada': nrm(ks[7], (DEPTH, 6 * D), 0.02),
        'w_in': nrm(ks[8], (DEPTH, D, IN_WIDTH), D ** -0.5),
        'w_out': nrm(ks[9], (DEPTH, MIX_WIDTH, D), MIX_WIDTH ** -0.5),
        'attn_sink': nrm(ks[10], (DEPTH, A_HEADS), 1.0),
        'conv_w': nrm(ks[11], (DEPTH, CONV_K, 1, CONV_CH), CONV_K ** -0.5),
        'conv_b': nrm(ks[12], (DEPTH, CONV_CH), 0.02),
        'conv_ln_g': 1.0 + nrm(ks[13], (DEPTH, CONV_CH), 0.1),
        'conv_ln_b': nrm(ks[14], (DEPTH, CONV_CH), 0.02),
        'diff_lq1': nrm(ks[15], (DEPTH, C_QK_DIM), 0.1),
        'diff_lk1': nrm(ks[16], (DEPTH, C_QK_DIM), 0.1),
        'diff_lq2': nrm(ks[17], (DEPTH, C_QK_DIM), 0.1),
        'diff_lk2': nrm(ks[18], (DEPTH, C_QK_DIM), 0.1),
        'diff_subln_g': 1.0 + nrm(ks[19], (DEPTH, C_V_DIM), 0.1),
        'na_rpb': nrm(ks[20], (DEPTH, D_HEADS, 2 * NA_KH - 1, 2 * NA_KW - 1), 0.1),
        'w_gate': nrm(ks[21], (DEPTH, D, F), D ** -0.5),
        'w_up': nrm(ks[22], (DEPTH, D, F), D ** -0.5),
        'w_down': nrm(ks[23], (DEPTH, F, D), F ** -0.5),
        'final_g': 1.0 + nrm(ks[24], (D,), 0.1),
    }

def second_block(x, c, ctx, c_ctx, norm1_g, norm2_g, w_ada, b_ada, w_in, w_out, attn_sink,
              conv_w, conv_b, conv_ln_g, conv_ln_b, diff_lq1, diff_lk1, diff_lq2, diff_lk2,
              diff_subln_g, na_rpb, w_gate, w_up, w_down, final_g):
    s_len = x.shape[1]
    rope_a = axial_rope(s_len, HEAD_DIM)
    rope_c = axial_rope(s_len, C_QK_DIM)
    sc = jax.nn.silu(c)
    scc = jax.nn.silu(c_ctx)
    for l in range(DEPTH):
        ctx_needed = l < DEPTH - 1
        mx = sc @ w_ada[l] + b_ada[l]
        mc = scc @ w_ada[l] + b_ada[l]
        sh1, sc1, g1, sh2, sc2, g2 = jnp.split(mx[:, None, :], 6, axis=-1)
        csh1, csc1, cg1, csh2, csc2, cg2 = jnp.split(mc, 6, axis=-1)
        lambda_init = 0.8 - 0.6 * math.exp(-0.3 * l)
        lam = (jnp.exp(jnp.sum(diff_lq1[l].astype(jnp.float32) * diff_lk1[l].astype(jnp.float32)))
               - jnp.exp(jnp.sum(diff_lq2[l].astype(jnp.float32) * diff_lk2[l].astype(jnp.float32)))
               + lambda_init)
        hx = modulate(rmsnorm_2(x, norm1_g[l]), sh1, sc1)
        hc = modulate(rmsnorm_2(ctx, norm1_g[l]), csh1, csc1)
        yx, yc = hybrid_mixer(hx, hc, w_in[l], w_out[l], attn_sink[l], conv_w[l], conv_b[l],
                              conv_ln_g[l], conv_ln_b[l], lam, diff_subln_g[l], lambda_init,
                              na_rpb[l], rope_a, rope_c, ctx_needed)
        x = x + g1 * yx
        x = x + g2 * swiglu_2(modulate(rmsnorm_2(x, norm2_g[l]), sh2, sc2), w_gate[l], w_up[l], w_down[l])
        if ctx_needed:
            ctx = ctx + cg1 * yc
            ctx = ctx + cg2 * swiglu_2(modulate(rmsnorm_2(ctx, norm2_g[l]), csh2, csc2),
                                     w_gate[l], w_up[l], w_down[l])
    return rmsnorm_2(x, final_g)


def setup_inputs(seed=0):
    out = dict(first_inputs(seed))
    for name, value in second_inputs(seed + 1).items():
        if name != "x":
            out[name + "_2"] = value
    return out


def reference(
    x, c, positions, ada_w, ada_b, norm_mix_g, norm_ffn_g, attn_w_in, attn_w_out, gdn_w_in,
    gdn_conv_w, gdn_a_log, gdn_dt_bias, gdn_norm_g, gdn_w_out, ffn_w_in, ffn_w_out,
    final_norm_g, c_2, ctx_2, c_ctx_2, norm1_g_2, norm2_g_2, w_ada_2, b_ada_2, w_in_2, w_out_2,
    attn_sink_2, conv_w_2, conv_b_2, conv_ln_g_2, conv_ln_b_2, diff_lq1_2, diff_lk1_2,
    diff_lq2_2, diff_lk2_2, diff_subln_g_2, na_rpb_2, w_gate_2, w_up_2, w_down_2, final_g_2,
):
    x = first_block(
        x, c, positions, ada_w, ada_b, norm_mix_g, norm_ffn_g, attn_w_in, attn_w_out, gdn_w_in,
        gdn_conv_w, gdn_a_log, gdn_dt_bias, gdn_norm_g, gdn_w_out, ffn_w_in, ffn_w_out,
        final_norm_g,
    )
    return second_block(
        x, c_2, ctx_2, c_ctx_2, norm1_g_2, norm2_g_2, w_ada_2, b_ada_2, w_in_2, w_out_2,
        attn_sink_2, conv_w_2, conv_b_2, conv_ln_g_2, conv_ln_b_2, diff_lq1_2, diff_lk1_2,
        diff_lq2_2, diff_lk2_2, diff_subln_g_2, na_rpb_2, w_gate_2, w_up_2, w_down_2, final_g_2,
    )


_drawn_inputs = setup_inputs


def setup_inputs(seed=0):
    import zlib

    import numpy as np

    out = dict(_drawn_inputs(seed))
    spreads = {}
    factors = {'norm_mix_g': 2.925,
     'gdn_norm_g': 5.172,
     'attn_sink_2': 8.0,
     'conv_b_2': 8.0,
     'conv_ln_g_2': 3.568,
     'conv_ln_b_2': 21.39,
     'diff_lq1_2': 8.0,
     'diff_lk1_2': 8.0,
     'diff_lq2_2': 8.0,
     'diff_lk2_2': 8.0,
     'diff_subln_g_2': 4.237,
     'na_rpb_2': 44.154,
     'norm_ffn_g': 3.169}
    for name, (base, spread) in spreads.items():
        noise = np.random.default_rng([zlib.crc32(name.encode()), seed]).standard_normal(out[name].shape)
        drawn = base * np.exp(spread * noise) if base else spread * noise
        out[name] = jnp.asarray(drawn.astype(out[name].dtype))
    for name, factor in factors.items():
        out[name] = (out[name] * factor).astype(out[name].dtype)
    return out
```

```python
from contextlib import ExitStack

import numpy as np
import concourse.bass as bass
from concourse import mybir

F32 = mybir.dt.float32
I32 = mybir.dt.int32
ALU = mybir.AluOpType
ACT = mybir.ActivationFunctionType
AX_X = mybir.AxisListType.X

P = 128
D = 1024
DC = D // P
T = 512
TC = 256
TA = T + TC
NT = T // P
F = 2816
FC = F // P
EPS = 1e-6
NEG = -1e30
SLOTS = 4
TILE = DC * 256
DOWN = FC // 2 * P
GH = 8
GC = 24
TWO_PI = 2 * np.pi
PI_A, PI_B = 6.28125, 0.0019350051879882812
PI_C = TWO_PI - PI_A - PI_B
ROUND = 12582912.0

CONST = {}
_at = 0
for _name, _w in [("ident", P), ("ones", P), ("tri", P), ("negtri", P), ("negones", P), ("perm_a1", P),
                  ("perm_64", P), ("perm_32", P), ("causal", P), ("band_lo", P), ("band_hi", P),
                  ("level", 7 * P), ("onehot", P), ("colmask", 64), ("half64", P), ("freq", 1), ("sign", 1)]:
    CONST[_name] = (_at, _w)
    _at += _w
CONST_W = _at

PARAM = {}
_at = 0
for _name, _w in [("c1", DC), ("c2", 2 * DC), ("ada_b", 4 * 48), ("mix_g", 4 * DC), ("ffn_g", 4 * DC),
                  ("fin_g", 2 * DC), ("gconv", 4 * GC), ("gnorm", 1), ("alog", GH), ("dtb", GH),
                  ("sink", 2 * 4), ("cw", 2 * 2 * 31), ("cb", 2 * 2), ("lng", 2 * 2), ("lnb", 2 * 2),
                  ("lq", 2 * 4 * 32), ("subg", 2), ("rpb", 2 * 4 * 15)]:
    PARAM[_name] = (_at, _w)
    _at += _w
PARAM_W = _at


def linear_plan():
    plan = []
    for layer in range(2):
        plan.append((f"ada{layer}", "w", 24))
        plan += [("attn_in", "w", 12), ("attn_out", "w", 4)] if layer == 0 else [("gdn_in", "w", 17), ("gdn_out", "w", 4)]
        plan += [(f"up{layer}", "w", FC), (f"down{layer}", "d", 2 * DC)]
    for layer in (2, 3):
        plan += [(f"ada{layer}", "w", 24), (f"in{layer}", "w", 11), (f"out{layer}", "w", 4),
                 (f"up{layer}", "w", FC), (f"down{layer}", "d", 2 * DC)]
    return plan


def build_program(nc, w_tiles, d_tiles, xT, ctxT, positions, consts, params, rope_tables, outT):
    G0, E0, at, read = {}, {}, 0, 8
    FROM = {}
    seen = {"w": 0, "d": 0}
    for name, kind, n in linear_plan():
        G0[name], FROM[name] = at, seen[kind]
        E0[name] = read
        at += n
        read += 0 if name.startswith("ada") else n // 2 if kind == "d" else n
        seen[kind] += n

    ctx = ExitStack()
    with ctx:
        def sb(name, shape, dt=F32):
            return ctx.enter_context(nc.sbuf_tensor(name, shape, dt))

        def sem(name):
            return ctx.enter_context(nc.semaphore(name))

        ring = sb("ring", [P, SLOTS, TILE])
        X = sb("X", [P, DC, TA])
        H = sb("H", [P, DC, TA])
        BIG = sb("BIG", [P, FC * TA])
        WORK = sb("WORK", [P, 9216])
        CN = sb("CN", [P, CONST_W])
        PR = sb("PR", [P, PARAM_W])
        MOD = sb("MOD", [P, 48, 2])
        GAIN = sb("GAIN", [P, 2, DC, 2])
        SC = sb("SC", [P, 3 * DC])
        SM = sb("SM", [P, 64])
        PS = ctx.enter_context(nc.psum_tensor("PS", [P, 4096], F32))

        def const(name):
            a, w = CONST[name]
            return CN[:, a:a + w]

        def par(name):
            a, w = PARAM[name]
            return PR[:, a:a + w]

        ident, ones = const("ident"), const("ones")

        loaded = sem("loaded")
        tile_loaded = [sem(f"tile_loaded{s}") for s in range(SLOTS)]
        tile_done = sem("tile_done")
        evac_done = sem("evac_done")
        phase_done = sem("phase_done")
        dve_chain = sem("dve_chain")
        act_chain = sem("act_chain")
        pool_chain = sem("pool_chain")
        stored = sem("stored")
        tables_loaded = sem("tables_loaded")
        scratch = {}

        def sig(name):
            if name not in scratch:
                scratch[name] = sem(name)
            return scratch[name]

        class Chain:

            def __init__(self, eng, s):
                self.eng, self.s, self.n = eng, s, 0

            def __call__(self, ins):
                ins.then_inc(self.s, 1)
                self.n = self.n + 1
                self.eng.wait_ge(self.s, self.n)

        def over_tiles(eng, n, body, chain=None, g0=0):
            rounds = n // SLOTS
            if rounds > 1:
                base = chain.n if chain else 0
                per = 0
                with eng.Fori(0, rounds) as i:
                    if chain:
                        per = body.steps * SLOTS
                        chain.n = i * per + base
                    for u in range(SLOTS):
                        body(i * SLOTS + u, u, i)
                if chain:
                    chain.n = base + per * rounds
            else:
                for i in range(rounds):
                    for u in range(SLOTS):
                        body(i * SLOTS + u, u, i)
            for u in range(n - rounds * SLOTS):
                body(rounds * SLOTS + u, u, rounds)

        class Phase:
            def __init__(self):
                self.n = 0

            def end(self, eng):
                self.n += 1
                eng.drain().then_inc(phase_done, 1)
                eng.wait_ge(phase_done, 4 * self.n)

        BASE = {}

        def base(who, name, count):
            key = (who, name)
            at = BASE.get(key, 0)
            BASE[key] = at + count
            return at

        SEG1 = [(0, T)]
        SEG2 = [(0, T), (T, TC)]

        def wait_tile(pe, name, u, i):
            g = G0[name] + u
            pe.wait_ge(tile_loaded[g % SLOTS], (i + g // SLOTS + 1) * 16)
            return g % SLOTS

        def pe_feature_tiles(pe, name, src, segs, n, first=0, chunks=2, nb=None):
            e0 = E0[name] + first
            nb = nb or 4 // len(segs)
            W = 4096 // nb

            def body(t, u, i):
                slot = wait_tile(pe, name, u + first, i)
                pe.wait_ge(evac_done, t + (e0 - nb + 1))
                buf = (u + first) % nb
                for j in range(chunks):
                    for s, (c0, w) in enumerate(segs):
                        o = buf * W + j * W // 2 + s * 512
                        for k in range(DC):
                            mm = pe.matmul(PS[:, o:o + w], ring[:, slot, k * 256 + j * P:k * 256 + (j + 1) * P],
                                           src[:, k, c0:c0 + w], start=k == 0, stop=k == DC - 1)
                mm.then_inc(tile_done, 1)
            over_tiles(pe, n, body)

        def act_copy_tiles(act, name, dst, segs, n, first=0, chunks=2, nb=None):
            g0 = G0[name] + first
            nb = nb or 4 // len(segs)
            W = 4096 // nb
            width = sum(w for _, w in segs)

            def body(t, u, i):
                act.wait_ge(tile_done, t + (g0 + 1))
                buf = (u + first) % nb
                act.activation(dst[:, bass.ds((t + first) * 2, chunks), 0:width],
                               PS[:, buf * W:buf * W + W].rearrange("p (j c) -> p j c", j=2)[:, 0:chunks, 0:width],
                               ACT.Copy).then_inc(evac_done, 1)
            over_tiles(act, n, body)

        def pe_token_tiles(pe, name, tokens, n, first, cols=256, nb=4):
            e0 = E0[name] + first
            W = 4096 // nb
            for t in range(n):
                slot = wait_tile(pe, name, first + t, 0)
                pe.wait_ge(evac_done, e0 + t - nb + 1)
                o = (first + t) % nb * W
                for a in range(tokens // P):
                    for k in range(DC):
                        mm = pe.matmul(PS[:, o + a * 256:o + a * 256 + cols], H[:, k, a * P:(a + 1) * P],
                                       ring[:, slot, k * 256:k * 256 + cols], start=k == 0, stop=k == DC - 1)
                mm.then_inc(tile_done, 1)

        def act_token_tiles(act, name, dst, tokens, n, first, cols=256, nb=4, col0=0):
            g0 = G0[name] + first
            W = 4096 // nb
            A = tokens // P
            for t in range(n):
                act.wait_ge(tile_done, g0 + t + 1)
                o = (first + t) % nb * W
                act.activation(dst[:, :, col0 + t * 256:col0 + t * 256 + cols],
                               PS[:, o:o + A * 256].rearrange("p (a c) -> p a c", a=A)[:, :, 0:cols],
                               ACT.Copy).then_inc(evac_done, 1)

        def dve_residual_tiles(dve, name, gate, segs, n):
            g0 = G0[name]
            nb = 4 // len(segs)
            W = 4096 // nb

            def body(t, u, i):
                dve.wait_ge(tile_done, t + (g0 + 1))
                buf = u % nb
                for j in range(2):
                    for s, (c0, w) in enumerate(segs):
                        o = buf * W + j * W // 2 + s * 512
                        m = t * 2 + j
                        ins = dve.scalar_tensor_tensor(
                            out=X[:, bass.ds(m, 1), c0:c0 + w], in0=PS[:, o:o + w].rearrange("p (a c) -> p a c", a=1),
                            scalar=gate[:, bass.ds(m, 1), s], in1=X[:, bass.ds(m, 1), c0:c0 + w],
                            op0=ALU.mult, op1=ALU.add)
                ins.then_inc(evac_done, 1)
            over_tiles(dve, n, body)

        HID = BIG[:, :].rearrange("p (k t) -> p k t", k=FC)

        def pe_down(pe, name, segs):
            e0 = E0[name]

            def body(t, u, i):
                slot = wait_tile(pe, name, u, i)
                if u % 2 == 0:
                    pe.wait_ge(evac_done, i * 2 + (e0 + u // 2 - 1))
                buf = (u // 2) % 2
                for s, (c0, w) in enumerate(segs):
                    o = buf * 1024 + s * 512
                    for k in range(FC // 2):
                        kk = (u % 2) * (FC // 2) + k
                        mm = pe.matmul(PS[:, o:o + w], ring[:, slot, k * P:(k + 1) * P], HID[:, kk, c0:c0 + w],
                                       start=kk == 0, stop=kk == FC - 1, skip_group_check=True)
                mm.then_inc(tile_done, 1)
            over_tiles(pe, 2 * DC, body)

        def dve_down(dve, name, gate, segs):
            e0 = E0[name]
            g0 = G0[name]

            def body(t, u, i):
                if u % 2 == 0:
                    return
                dve.wait_ge(tile_done, t + (g0 + 1))
                buf = (u // 2) % 2
                m = i * 2 + u // 2
                for s, (c0, w) in enumerate(segs):
                    o = buf * 1024 + s * 512
                    ins = dve.scalar_tensor_tensor(
                        out=X[:, bass.ds(m, 1), c0:c0 + w], in0=PS[:, o:o + w].rearrange("p (a c) -> p a c", a=1),
                        scalar=gate[:, bass.ds(m, 1), s], in1=X[:, bass.ds(m, 1), c0:c0 + w],
                        op0=ALU.mult, op1=ALU.add)
                ins.then_inc(evac_done, 1)
            over_tiles(dve, 2 * DC, body)

        def act_up(act, name, segs):
            n = FC
            e0 = E0[name]
            g0 = G0[name]
            nb = 4 // len(segs)
            W = 4096 // nb
            width = sum(w for _, w in segs)

            def body(t, u, i):
                act.wait_ge(tile_done, t + (g0 + 1))
                act.wait_ge(evac_done, t + (e0 - 1))
                o = (u % nb) * W
                act.activation(WORK[:, (u % 2) * TA:(u % 2) * TA + width], PS[:, o:o + width], ACT.Exp,
                               scale=-1.0).then_inc(sig("gate_exp"), 1)
            over_tiles(act, n, body)

        def dve_up(dve, name, segs, chain):
            n = FC
            b = base("dve", "gate_exp", n)
            nb = 4 // len(segs)
            W = 4096 // nb
            width = sum(w for _, w in segs)

            def body(t, u, i):
                dve.wait_ge(sig("gate_exp"), t + (b + 1))
                E = WORK[:, (u % 2) * TA:(u % 2) * TA + width]
                o = (u % nb) * W
                chain(dve.tensor_scalar(E, E, 1.0, None, ALU.add))
                chain(dve.reciprocal(E, E))
                chain(dve.tensor_tensor(E, E, PS[:, o:o + width], ALU.mult))
                dve.tensor_tensor(HID[:, bass.ds(t, 1), 0:width], E.rearrange("p (a c) -> p a c", a=1),
                                  PS[:, o + W // 2:o + W // 2 + width].rearrange("p (a c) -> p a c", a=1),
                                  ALU.mult).then_inc(evac_done, 1)
            body.steps = 3
            over_tiles(dve, n, body, chain)

        def pe_ada(pe, layer):
            name = f"ada{layer}"
            nv = 1 if layer < 2 else 2
            src = SC[:, 0:DC].rearrange("p (k v) -> p k v", v=1) if layer < 2 else \
                SC[:, DC:3 * DC].rearrange("p (k v) -> p k v", v=2)
            acc = PS[:, 0:96].rearrange("p (n v) -> p n v", v=2)

            def body(t, u, i):
                slot = wait_tile(pe, name, u, i)
                for j in range(2):
                    for k in range(DC):
                        mm = pe.matmul(acc[:, bass.ds(t * 2 + j, 1), 0:nv].rearrange("p a v -> p (a v)"),
                                       ring[:, slot, k * 256 + j * P:k * 256 + (j + 1) * P],
                                       src[:, k, :], start=k == 0, stop=k == DC - 1)
                mm.then_inc(tile_done, 1)
            over_tiles(pe, 24, body)

        def dve_ada(dve, layer, chain):
            nv = 1 if layer < 2 else 2
            dve.wait_ge(tile_done, G0[f"ada{layer}"] + 24)
            acc = PS[:, 0:96].rearrange("p (n v) -> p n v", v=2)
            bias = par("ada_b").rearrange("p (l n) -> p l n", l=4)[:, layer, :]
            for v in range(nv):
                chain(dve.tensor_tensor(MOD[:, :, v], acc[:, :, v], bias, ALU.add))
                for which, row in ((0, DC), (1, 4 * DC)):
                    g = par("mix_g" if which == 0 else "ffn_g").rearrange("p (l k) -> p l k", l=4)[:, layer, :]
                    dve.scalar_tensor_tensor(out=GAIN[:, which, :, v], in0=MOD[:, row:row + DC, v], scalar=1.0,
                                             in1=g, op0=ALU.add, op1=ALU.mult)

        SQ = [WORK[:, 0:TA], WORK[:, TA:2 * TA]]
        RSTD = WORK[:, 2 * TA:3 * TA]

        def act_norm(act, segs, chain, shift=None):
            width = sum(w for _, w in segs)
            b_mm = base("act", "norm_summed", DC)
            b_h = base("act", "norm_scaled", DC)
            for k in range(DC):
                if k >= 2:
                    act.wait_ge(sig("norm_summed"), b_mm + k - 1)
                act.activation(SQ[k % 2][:, 0:width], X[:, k, 0:width], ACT.Square).then_inc(sig("norm_squared"), 1)
            act.wait_ge(sig("norm_summed"), b_mm + DC)
            chain(act.activation(RSTD[:, 0:width], PS[:, 0:width], ACT.Ln, scale=1.0 / D, bias=SM[:, 0:1]))
            act.activation(RSTD[:, 0:width], RSTD[:, 0:width], ACT.Exp, scale=-0.5).then_inc(sig("norm_rstd"), 1)
            for k in range(DC):
                act.wait_ge(sig("norm_scaled"), b_h + k + 1)
                if shift is not None:
                    for s, (c0, w) in enumerate(segs):
                        act.activation(H[:, k, c0:c0 + w], H[:, k, c0:c0 + w], ACT.Identity, bias=shift[:, k, s:s + 1])

        def pe_norm(pe, segs):
            b = base("pe", "norm_squared", DC)
            for k in range(DC):
                pe.wait_ge(sig("norm_squared"), b + k + 1)
                for c0, w in segs:
                    mm = pe.matmul(PS[:, c0:c0 + w], ones, SQ[k % 2][:, c0:c0 + w], start=k == 0, stop=k == DC - 1)
                mm.then_inc(sig("norm_summed"), 1)

        def dve_norm(dve, segs, gain):
            b = base("dve", "norm_rstd", 1)
            dve.wait_ge(sig("norm_rstd"), b + 1)
            for k in range(DC):
                for s, (c0, w) in enumerate(segs):
                    ins = dve.scalar_tensor_tensor(out=H[:, k, c0:c0 + w], in0=X[:, k, c0:c0 + w],
                                                   scalar=gain[:, k, s:s + 1], in1=RSTD[:, c0:c0 + w],
                                                   op0=ALU.mult, op1=ALU.mult)
                ins.then_inc(sig("norm_scaled"), 1)

        S_SB = [WORK[:, n * TA:(n + 1) * TA] for n in range(4)]
        PT = [WORK[:, (4 + n) * TA:(5 + n) * TA] for n in range(2)]

        def map_list(jobs):
            return [(n, m) for n, job in enumerate(jobs) for m in range(len(job["q"]))]

        def pe_attention(pe, jobs):
            maps = map_list(jobs)
            b_read = base("pe", "scores_read", len(maps))
            b_p = base("pe", "weights_ready", len(jobs))
            b_pt = base("pe", "turned_copied", len(jobs))
            b_o = base("pe", "heads_copied", len(jobs))

            def scores(s):
                n, m = maps[s]
                job = jobs[n]
                if s >= 2:
                    pe.wait_ge(sig("scores_read"), b_read + s - 1)
                for o, k in job["k"][m]:
                    a = (s % 2) * 1024 + o
                    mm = pe.matmul(PS[:, a:a + k.shape[-1]], job["q"][m], k, start=True, stop=True)
                mm.then_inc(sig("scores_ready"), 1)

            def turn(n):
                s = max(x for x, (j, _) in enumerate(maps) if j == n)
                pe.wait_ge(sig("weights_ready"), b_p + n + 1)
                if n >= 1:
                    pe.wait_ge(sig("turned_copied"), b_pt + n)
                for x in range(len(jobs[n]["v"])):
                    mm = pe.transpose(PS[:, 2048 + x * P:2048 + (x + 1) * P], S_SB[s % 4][:, x * P:(x + 1) * P], ident)
                mm.then_inc(sig("turned"), 1)

            def outputs(n):
                job = jobs[n]
                pe.wait_ge(sig("turned_copied"), b_pt + n + 1)
                if n >= 2:
                    pe.wait_ge(sig("heads_copied"), b_o + n - 1)
                off = job["off"]
                o = 3072 + (n % 2) * 512
                for x, v in enumerate(job["v"]):
                    mm = pe.matmul(PS[off:off + 64, o:o + P], v, PT[n % 2][:, x * P:(x + 1) * P],
                                   start=x == 0, stop=x == len(job["v"]) - 1)
                mm.then_inc(sig("heads_ready"), 1)

            per = len(jobs[0]["q"])
            for s in range(per):
                scores(s)
            for n in range(len(jobs)):
                if n + 1 < len(jobs):
                    for s in range((n + 1) * per, (n + 2) * per):
                        scores(s)
                if n >= 1:
                    outputs(n - 1)
                turn(n)
            outputs(len(jobs) - 1)

        def dve_attention(dve, jobs, chain):
            maps = map_list(jobs)
            b_s = base("dve", "scores_ready", len(maps))
            b_t = base("dve", "turned", len(jobs))
            b_e = base("dve", "exps_ready", len(maps))

            def score_part(s):
                n, m = maps[s]
                job = jobs[n]
                per = len(job["q"])
                nk = len(job["v"]) * P
                S = S_SB[s % 4]
                dve.wait_ge(sig("scores_ready"), b_s + s + 1)
                if s >= 4:
                    dve.wait_ge(sig("turned"), b_t + (s - 4) // per + 1)
                pieces = job["pieces"]
                for x, (o, p0, w, mask) in enumerate(pieces):
                    src = PS[:, (s % 2) * 1024 + p0:(s % 2) * 1024 + p0 + w]
                    if mask is None:
                        ins = dve.tensor_scalar(S[:, o:o + w], src, job["scale"], None, ALU.mult)
                    else:
                        ins = dve.scalar_tensor_tensor(out=S[:, o:o + w], in0=src, scalar=job["scale"], in1=mask,
                                                       op0=ALU.mult, op1=ALU.add)
                    if x < len(pieces) - 1:
                        chain(ins)
                ins.then_inc(sig("scores_read"), 1)
                dve.wait_ge(sig("scores_read"), b_read + s + 1)
                if job["sink"] is None:
                    dve.tensor_reduce(SM[:, 8 + s % 4:9 + s % 4], S[:, 0:nk], AX_X, ALU.max,
                                      negate=True).then_inc(sig("max_ready"), 1)
                else:
                    chain(dve.tensor_reduce(SM[:, 8 + s % 4:9 + s % 4], S[:, 0:nk], AX_X, ALU.max, negate=True))
                    dve.scalar_tensor_tensor(out=SM[:, 8 + s % 4:9 + s % 4], in0=job["sink"], scalar=-1.0,
                                             in1=SM[:, 8 + s % 4:9 + s % 4], op0=ALU.mult,
                                             op1=ALU.min).then_inc(sig("max_ready"), 1)

            def weight_part(s):
                n, m = maps[s]
                job = jobs[n]
                nk = len(job["v"]) * P
                S = S_SB[s % 4]
                dve.wait_ge(sig("exps_ready"), b_e + s + 1)
                total, inv = SM[:, 12 + s % 4:13 + s % 4], SM[:, 16 + s % 4:17 + s % 4]
                if job["sink"] is not None:
                    chain(dve.tensor_tensor(total, total, SM[:, 20 + s % 4:21 + s % 4], ALU.add))
                chain(dve.reciprocal(inv, total))
                if m == 1:
                    chain(dve.tensor_scalar(inv, inv, job["neg_lam"], None, ALU.mult))
                    dve.scalar_tensor_tensor(out=S[:, 0:nk], in0=S[:, 0:nk], scalar=inv,
                                             in1=S_SB[(s - 1) % 4][:, 0:nk], op0=ALU.mult,
                                             op1=ALU.add).then_inc(sig("weights_ready"), 1)
                elif len(job["q"]) == 2:
                    chain(dve.tensor_scalar(S[:, 0:nk], S[:, 0:nk], inv, None, ALU.mult))
                else:
                    dve.tensor_scalar(S[:, 0:nk], S[:, 0:nk], inv, None, ALU.mult).then_inc(sig("weights_ready"), 1)

            b_read = base("dve", "scores_read", len(maps))
            score_part(0)
            for s in range(len(maps)):
                if s + 1 < len(maps):
                    score_part(s + 1)
                weight_part(s)

        def act_attention(act, jobs, chain):
            maps = map_list(jobs)
            b_m = base("act", "max_ready", len(maps))
            b_t = base("act", "turned", len(jobs))
            b_h = base("act", "heads_ready", len(jobs))

            def exps(s):
                n, m = maps[s]
                job = jobs[n]
                nk = len(job["v"]) * P
                S = S_SB[s % 4]
                act.wait_ge(sig("max_ready"), b_m + s + 1)
                if job["sink"] is not None:
                    chain(act.activation(SM[:, 20 + s % 4:21 + s % 4], job["sink"], ACT.Exp, bias=SM[:, 8 + s % 4:9 + s % 4]))
                act.activation(S[:, 0:nk], S[:, 0:nk], ACT.Exp, bias=SM[:, 8 + s % 4:9 + s % 4],
                               accum_out=SM[:, 12 + s % 4:13 + s % 4]).then_inc(sig("exps_ready"), 1)

            def copy_turned(n):
                act.wait_ge(sig("turned"), b_t + n + 1)
                if n >= 2:
                    act.wait_ge(sig("heads_ready"), b_h + n - 1)
                nk = len(jobs[n]["v"]) * P
                act.activation(PT[n % 2][:, 0:nk], PS[:, 2048:2048 + nk], ACT.Copy).then_inc(sig("turned_copied"), 1)

            def copy_heads(n):
                act.wait_ge(sig("heads_ready"), b_h + n + 1)
                job = jobs[n]
                off = job["off"]
                o = 3072 + (n % 2) * 512
                act.activation(job["out"], PS[off:off + 64, o:o + P], ACT.Copy).then_inc(sig("heads_copied"), 1)

            per = len(jobs[0]["q"])
            for s in range(per):
                exps(s)
            for n in range(len(jobs)):
                if n + 1 < len(jobs):
                    for s in range((n + 1) * per, (n + 2) * per):
                        exps(s)
                copy_turned(n)
                if n >= 1:
                    copy_heads(n - 1)
            copy_heads(len(jobs) - 1)

        def pe_rope(pe, chunks):
            b = base("pe", "rotated", len(chunks))
            for n, (c, perm, _, _) in enumerate(chunks):
                if n >= 4:
                    pe.wait_ge(sig("rotated"), b + n - 3)
                pe.matmul(PS[:, (n % 4) * 512:(n % 4) * 512 + T], perm, c, start=True, stop=True).then_inc(sig("swapped"), 1)

        def dve_rope(dve, chunks, chain):
            b = base("dve", "swapped", len(chunks))
            for n, (c, _, cos, sin) in enumerate(chunks):
                dve.wait_ge(sig("swapped"), b + n + 1)
                tmp = ROPE_TMP[:, (n % 2) * T:(n % 2) * T + T]
                dve.tensor_tensor(tmp, PS[:, (n % 4) * 512:(n % 4) * 512 + T], sin, ALU.mult)
                chain(dve.tensor_tensor(c, c, cos, ALU.mult))
                dve.tensor_tensor(c, c, tmp, ALU.add).then_inc(sig("rotated"), 1)

        ROPE_TMP = WORK[:, 8192:9216]

        QK1 = BIG[:, 0:16 * T].rearrange("p (k t) -> p k t", k=16)
        V1 = BIG[:, 16 * T:24 * T].rearrange("p (a c) -> p a c", a=NT)
        COS1, SIN1 = WORK[:, 0:T], WORK[:, T:2 * T]
        POS = WORK[:, 5 * T:6 * T]
        TMP1, TMP2 = WORK[:, 3 * T:4 * T], WORK[:, 4 * T:5 * T]

        def dve_angles(dve, chain):
            dve.wait_ge(tables_loaded, 16)
            chain(dve.tensor_copy(POS, POS.bitcast(I32)))
            chain(dve.tensor_scalar(POS, POS, const("freq"), None, ALU.mult))
            for dst, ahead in ((COS1, 0.25), (SIN1, 0.0)):
                chain(dve.tensor_scalar(TMP1, POS, 1 / TWO_PI, ahead, ALU.mult, ALU.add))
                chain(dve.tensor_scalar(TMP1, TMP1, ROUND, ROUND, ALU.add, ALU.subtract))
                chain(dve.scalar_tensor_tensor(out=dst, in0=TMP1, scalar=-PI_A, in1=POS, op0=ALU.mult, op1=ALU.add))
                chain(dve.scalar_tensor_tensor(out=dst, in0=TMP1, scalar=-PI_B, in1=dst, op0=ALU.mult, op1=ALU.add))
                chain(dve.scalar_tensor_tensor(out=dst, in0=TMP1, scalar=-PI_C, in1=dst, op0=ALU.mult, op1=ALU.add))
                if ahead:
                    chain(dve.tensor_scalar(dst, dst, np.pi / 2, None, ALU.add))
                chain(dve.tensor_scalar(dst, dst, 3.1415925, -3.1415925, ALU.min, ALU.max))

        def act_angles(act, chain):
            chain(act.activation(COS1, COS1, ACT.Sin))
            chain(act.activation(SIN1, SIN1, ACT.Sin))
            act.activation(SIN1, SIN1, ACT.Copy, scale=const("sign"))

        def causal_jobs():
            jobs = []
            for h in range(8):
                r = slice((h % 2) * 64, (h % 2) * 64 + 64)
                for i in range(NT):
                    pieces = [(0, 0, i * P, None)] if i else []
                    pieces.append((i * P, i * P, P, const("causal")))
                    jobs.append(dict(q=[QK1[r, h // 2, i * P:(i + 1) * P]],
                                     k=[[(0, QK1[r, 4 + h // 2, 0:(i + 1) * P])]],
                                     v=[V1[:, a, h * 64:(h + 1) * 64] for a in range(i + 1)],
                                     pieces=pieces, scale=0.125, sink=None, off=(h % 2) * 64,
                                     out=H[r, h // 2, i * P:(i + 1) * P]))
            return jobs

        OFFS = [0, 512, 1024, 896]
        SBW = 1280
        SP_ = [WORK[:, n * SBW:(n + 1) * SBW] for n in range(2)]
        SW = [WORK[:, (2 + n) * SBW:(3 + n) * SBW] for n in range(2)]

        def sb_bank(h, i):
            return (h % 2) * 1536 + OFFS[i]

        def pe_stick(pe):
            def z(h):
                if h >= 2:
                    pe.wait_ge(sig("sticks_read"), h - 1)
                r = slice((h % 2) * 64, (h % 2) * 64 + 64)
                for i in (0, 1, 3, 2):
                    a, w = sb_bank(h, i), T - i * P
                    mm = pe.matmul(PS[:, a:a + w], QK1[r, 12 + h // 2, i * P:(i + 1) * P],
                                   QK1[r, 8 + h // 2, i * P:T], start=i != 3, stop=True, skip_group_check=True)
                mm.then_inc(sig("z_ready"), 1)

            def sums(h):
                pe.wait_ge(sig("softplus_masked"), h + 1)
                for i in (0, 1, 3, 2):
                    for j in range(i, NT):
                        a = sb_bank(h, i) + (j - i) * P
                        w = T - j * P
                        mm = pe.matmul(PS[:, a:a + w], const("negtri") if j == i else const("negones"),
                                       SP_[h % 2][:, OFFS[j]:OFFS[j] + w], start=False, stop=True, skip_group_check=True)
                mm.then_inc(sig("sticks_ready"), 1)

            def outputs(h):
                pe.wait_ge(sig("sticks_masked"), h + 1)
                if h >= 2:
                    pe.wait_ge(sig("stick_heads_copied"), h - 1)
                off = (h % 2) * 64
                for i in range(NT):
                    o = 3072 + (h % 2) * 512
                    mm = pe.matmul(PS[off:off + 64, o + i * P:o + T], V1[:, i, 512 + h * 64:512 + (h + 1) * 64],
                                   SW[h % 2][:, OFFS[i]:OFFS[i] + T - i * P], start=i == 0, stop=i == NT - 1,
                                   skip_group_check=True)
                mm.then_inc(sig("stick_heads_ready"), 1)

            z(0)
            for h in range(8):
                if h + 1 < 8:
                    z(h + 1)
                sums(h)
                if h >= 1:
                    outputs(h - 1)
            outputs(7)

        def act_stick(act, chain):
            def softplus(h):
                act.wait_ge(sig("z_ready"), h + 1)
                if h >= 2:
                    act.wait_ge(sig("sticks_ready"), h - 1)
                L, a = SP_[h % 2], (h % 2) * 1536
                chain(act.activation(L, PS[:, a:a + SBW], ACT.Abs))
                chain(act.activation(L, L, ACT.Exp, scale=-1.0))
                act.activation(L, L, ACT.Ln, bias=SM[:, 1:2]).then_inc(sig("log_ready"), 1)

            def weights(h):
                act.wait_ge(sig("sticks_ready"), h + 1)
                if h >= 2:
                    act.wait_ge(sig("stick_heads_ready"), h - 1)
                a = (h % 2) * 1536
                act.activation(SW[h % 2], PS[:, a:a + SBW], ACT.Exp).then_inc(sig("sticks_read"), 1)

            def copy(h):
                off = (h % 2) * 64
                act.wait_ge(sig("stick_heads_ready"), h + 1)
                act.activation(H[off:off + 64, 4 + h // 2, 0:T], PS[off:off + 64, 3072 + (h % 2) * 512:3072 + (h % 2) * 512 + T],
                               ACT.Copy).then_inc(sig("stick_heads_copied"), 1)

            softplus(0)
            for h in range(8):
                if h + 1 < 8:
                    softplus(h + 1)
                weights(h)
                if h >= 1:
                    copy(h - 1)
            copy(7)

        def dve_stick(dve):
            for h in range(8):
                dve.wait_ge(sig("log_ready"), h + 1)
                a = (h % 2) * 1536
                dve.scalar_tensor_tensor(out=SP_[h % 2], in0=PS[:, a:a + SBW], scalar=0.0, in1=SP_[h % 2],
                                         op0=ALU.max, op1=ALU.add).then_inc(sig("softplus_ready"), 1)

        def pool_stick(pool):
            def keep_past(buf):
                for i in range(NT):
                    v = buf[:, OFFS[i]:OFFS[i] + P]
                    ins = pool.affine_select(out=v, in_=v, compare_op=ALU.is_gt, fill=0.0, base=0,
                                             pattern=[[1, P]], channel_multiplier=-1)
                return ins
            def soft(h):
                pool.wait_ge(sig("softplus_ready"), h + 1)
                keep_past(SP_[h % 2]).then_inc(sig("softplus_masked"), 1)
            soft(0)
            for h in range(8):
                if h + 1 < 8:
                    soft(h + 1)
                pool.wait_ge(sig("sticks_read"), h + 1)
                keep_past(SW[h % 2]).then_inc(sig("sticks_masked"), 1)
        def rope1_chunks():
            return [(QK1[:, x, :], const("perm_a1"), COS1, SIN1) for x in range(8)]

        FIN_G = [par("fin_g").rearrange("p (l k v) -> p l k v", l=2, v=1)[:, n, :, :] for n in range(2)]
        GQ = BIG[:, 0:32 * T].rearrange("p (k t) -> p k t", k=32)
        CONV_IN = [WORK[:, n * 1030:n * 1030 + 1030].rearrange("p (j t) -> p j t", j=2) for n in range(2)]
        CONV_E = [WORK[:, 2080 + n * 1024:3104 + n * 1024] for n in range(2)]
        HF = H[:, :, :].rearrange("p k t -> p (k t)")
        KTOK = HF[:, 0:8 * T].rearrange("p (h c d) -> p h c d", h=GH, c=NT)
        VTOK = BIG[:, 16 * T:24 * T].rearrange("p (h c d) -> p h c d", h=GH, c=NT)
        GS0 = 4096 + 4 * P + 1024
        AB = HF[:, GS0:GS0 + 64].rearrange("p (c n) -> p c n", c=NT)

        def gate_vec(n):
            return HF[:, GS0 + 64 + 32 * n:GS0 + 96 + 32 * n]
        GRAW, BETA, GCUM, NCOEF, EG, EKD, EGL, GTMP = [gate_vec(n) for n in range(8)]
        STATE = HF[:, 4096:4096 + 4 * P].rearrange("p (h e) -> p h e", h=4)
        VNEW = HF[:, 4096 + 4 * P:4096 + 8 * P]
        QEXP = HF[:, 4096 + 8 * P:4096 + 12 * P]
        SEL = lambda v, c, h: v[:, c * GH + h:c * GH + h + 1]

        def act_gdn_in(act, chain):
            g0, e0 = G0["gdn_in"], E0["gdn_in"]
            b = base("act", "convolved", 12)

            def body(t, u, i):
                act.wait_ge(tile_done, t + (g0 + 1))
                act.wait_ge(sig("convolved"), t + (b + 7))
                act.activation(CONV_IN[u % 2][:, :, 3:3 + T], PS[:, (u % 4) * 1024:(u % 4 + 1) * 1024]
                               .rearrange("p (j c) -> p j c", j=2), ACT.Copy).then_inc(evac_done, 1)
                act.wait_ge(sig("convolved"), t + (b + 9))
                act.activation(CONV_E[u % 2], GQ[:, bass.ds(t * 2, 2), :], ACT.Exp, scale=-1.0).then_inc(sig("conv_exp"), 1)
            over_tiles(act, 12, body)
            for t in range(4):
                act.wait_ge(tile_done, g0 + 12 + t + 1)
                act.activation(GQ[:, 24 + 2 * t:26 + 2 * t, :], PS[:, t * 1024:(t + 1) * 1024]
                               .rearrange("p (j c) -> p j c", j=2), ACT.Copy).then_inc(evac_done, 1)
            act.wait_ge(tile_done, g0 + 17)
            act.activation(AB, PS[:, 0:64].rearrange("p (c n) -> p c n", c=NT), ACT.Copy).then_inc(evac_done, 1)

        def dve_gdn_in(dve, chain):
            e0 = E0["gdn_in"]
            b = base("dve", "conv_exp", 12)
            dve.memset(CONV_IN[0][:, :, 0:3], 0.0)
            dve.memset(CONV_IN[1][:, :, 0:3], 0.0).then_inc(sig("convolved"), 8)
            dve.wait_ge(sig("convolved"), 8)
            w = par("gconv").rearrange("p (k n) -> p k n", k=4)

            def body(t, u, i):
                dve.wait_ge(evac_done, t + (e0 + 1))
                src = CONV_IN[u % 2]
                for tap in range(4):
                    for j in range(2):
                        y = GQ[:, bass.ds(t * 2 + j, 1), :]
                        x = src[:, j:j + 1, tap:tap + T]
                        s = w[:, tap, bass.ds(t * 2 + j, 1)]
                        if tap == 0:
                            ins = dve.tensor_scalar(y, x, s, None, ALU.mult)
                        else:
                            ins = dve.scalar_tensor_tensor(out=y, in0=x, scalar=s, in1=y, op0=ALU.mult, op1=ALU.add)
                    if tap < 3:
                        chain(ins)
                    else:
                        ins.then_inc(sig("convolved"), 1)
                dve.wait_ge(sig("conv_exp"), t + (b + 1))
                E = CONV_E[u % 2]
                y = GQ[:, bass.ds(t * 2, 2), :]
                chain(dve.tensor_scalar(E, E, 1.0, None, ALU.add))
                chain(dve.reciprocal(E, E))
                dve.tensor_tensor(y, y, E.rearrange("p (j c) -> p j c", j=2), ALU.mult)
            body.steps = 5
            over_tiles(dve, 12, body, chain)

        def pe_gdn_in(pe):
            pe_feature_tiles(pe, "gdn_in", H, SEG1, 12)
            pe_feature_tiles(pe, "gdn_in", H, SEG1, 4, first=12)
            slot = wait_tile(pe, "gdn_in", 16, 0)
            pe.wait_ge(evac_done, E0["gdn_in"] + 13)
            for a in range(NT):
                for k in range(DC):
                    mm = pe.matmul(PS[:, a * 16:a * 16 + 16], H[:, k, a * P:(a + 1) * P], ring[:, slot, k * 256:k * 256 + 16],
                                   start=k == 0, stop=k == DC - 1)
            mm.then_inc(tile_done, 1)

        def act_gdn_prep(act, chain):
            for n in range(16):
                act.wait_ge(sig("l2_summed"), n + 1)
                if n >= 2:
                    act.wait_ge(sig("l2_scaled"), n - 1)
                R = WORK[:, (2 + n % 2) * T:(3 + n % 2) * T]
                s = float(P) if n < 8 else 1.0
                chain(act.activation(R, PS[:, (n % 2) * 512:(n % 2) * 512 + T], ACT.Ln, scale=s,
                                     bias=SM[:, 2:3] if n < 8 else SM[:, 0:1]))
                act.activation(R, R, ACT.Exp, scale=-0.5).then_inc(sig("l2_rstd"), 1)
            act.wait_ge(sig("dt_added"), 1)
            a = AB[:, :, 0:GH]
            t3 = GTMP.rearrange("p (c n) -> p c n", c=NT)
            chain(act.activation(t3, a, ACT.Abs))
            chain(act.activation(GTMP, GTMP, ACT.Exp, scale=-1.0))
            chain(act.activation(GTMP, GTMP, ACT.Ln, bias=SM[:, 1:2]))
            act.activation(BETA.rearrange("p (c n) -> p c n", c=NT), AB[:, :, GH:2 * GH], ACT.Exp, scale=-1.0)
            act.activation(SM[:, 24:32], par("alog"), ACT.Exp).then_inc(sig("gate_parts"), 1)
            act.wait_ge(sig("gcum_ready"), 1)
            act.activation(EG, GCUM, ACT.Exp)
            act.activation(EKD, GTMP, ACT.Exp)
            act.activation(EGL, PS[:, 2048 + 32:2048 + 64], ACT.Exp).then_inc(sig("gate_exps"), 1)

        def pool_gdn_prep(pool):
            for n in range(16):
                if n >= 2:
                    pool.wait_ge(sig("l2_summed"), n - 1)
                pool.tensor_tensor(WORK[:, (n % 2) * T:(n % 2 + 1) * T], GQ[:, n, :], GQ[:, n, :],
                                   ALU.mult).then_inc(sig("l2_squared"), 1)

        def pe_gdn_prep(pe):
            for n in range(16):
                pe.wait_ge(sig("l2_squared"), n + 1)
                if n >= 2:
                    pe.wait_ge(sig("l2_rstd"), n - 1)
                pe.matmul(PS[:, (n % 2) * 512:(n % 2) * 512 + T], ones, WORK[:, (n % 2) * T:(n % 2 + 1) * T],
                          start=True, stop=True).then_inc(sig("l2_summed"), 1)
            pe.wait_ge(sig("graw_ready"), 1)
            pe.matmul(PS[:, 2048:2048 + 32], const("tri"), GRAW, start=True, stop=True)
            pe.matmul(PS[:, 2048 + 32:2048 + 64], ones, GRAW, start=True, stop=True).then_inc(sig("gsums_ready"), 1)
            for n in range(16):
                h = n % 8
                if n < 8:
                    pe.wait_ge(sig("l2_scaled"), 9 + h)
                if n >= 2:
                    pe.wait_ge(sig("tokens_copied"), n - 1)
                for c in range(NT):
                    mm = pe.transpose(PS[:, 1024 + (n % 2) * 512 + c * P:1024 + (n % 2) * 512 + (c + 1) * P],
                                      GQ[:, 8 + n, c * P:(c + 1) * P], ident)
                mm.then_inc(sig("tokens_turned"), 1)

        def dve_gdn_prep(dve, chain):
            a = AB[:, :, 0:GH]
            for c in range(NT):
                ins = dve.tensor_tensor(AB[:, c, 0:GH], AB[:, c, 0:GH], par("dtb"), ALU.add)
            ins.then_inc(sig("dt_added"), 1)
            for n in range(16):
                dve.wait_ge(sig("l2_rstd"), n + 1)
                dve.tensor_tensor(GQ[:, n, :], GQ[:, n, :], WORK[:, (2 + n % 2) * T:(3 + n % 2) * T],
                                  ALU.mult).then_inc(sig("l2_scaled"), 1)
            dve.wait_ge(sig("gate_parts"), 1)
            t3 = GTMP.rearrange("p (c n) -> p c n", c=NT)
            chain(dve.scalar_tensor_tensor(out=t3, in0=a, scalar=0.0, in1=t3, op0=ALU.max, op1=ALU.add))
            for c in range(NT):
                ins = dve.scalar_tensor_tensor(out=GRAW[:, c * GH:(c + 1) * GH], in0=GTMP[:, c * GH:(c + 1) * GH],
                                               scalar=-1.0, in1=SM[:, 24:32], op0=ALU.mult, op1=ALU.mult)
            ins.then_inc(sig("graw_ready"), 1)
            chain(dve.tensor_scalar(BETA, BETA, 1.0, None, ALU.add))
            chain(dve.reciprocal(BETA, BETA))
            dve.wait_ge(sig("gsums_ready"), 1)
            chain(dve.tensor_copy(GCUM, PS[:, 2048:2048 + 32]))
            dve.scalar_tensor_tensor(out=GTMP, in0=GCUM, scalar=-1.0, in1=PS[:, 2048 + 32:2048 + 64], op0=ALU.mult,
                                     op1=ALU.add).then_inc(sig("gcum_ready"), 1)
            dve.wait_ge(sig("gate_exps"), 1)
            dve.scalar_tensor_tensor(out=NCOEF, in0=EG, scalar=-1.0, in1=BETA, op0=ALU.mult, op1=ALU.mult)
            for n in range(16):
                h = n % 8
                dve.wait_ge(sig("tokens_turned"), n + 1)
                src = PS[:, 1024 + (n % 2) * 512:1024 + (n % 2) * 512 + T].rearrange("p (c d) -> p c d", c=NT)
                dst, by = (KTOK, EKD) if n < 8 else (VTOK, BETA)
                for c in range(NT):
                    ins = dve.tensor_scalar(dst[:, h, c, :], src[:, c, :], SEL(by, c, h), None, ALU.mult)
                ins.then_inc(sig("tokens_copied"), 1)

        def gbuf(par_, n):
            o = 4096 + par_ * 2560 + n * T
            return WORK[:, o:o + T]
        XT = [WORK[:, n * T:(n + 1) * T] for n in range(4)]
        AT = [WORK[:, (4 + n) * T:(5 + n) * T] for n in range(4)]
        LEVELS = 7

        def gps(q, n, c=None):
            o = (q * 3 + n) * 512
            return PS[:, o:o + T] if c is None else PS[:, o + c * P:o + (c + 1) * P]

        def blk(v, c):
            return v[:, c * P:(c + 1) * P]

        def pe_gdn_inverse(pe, grp):
            kT = lambda h, c: GQ[:, 8 + h, c * P:(c + 1) * P]
            for n in range(0, 4, 2):
                for q in range(2):
                    h = grp * 4 + n + q
                    N = grp * 4 + n + q
                    pe.wait_ge(sig("tri_scaled"), N + 1)
                    if N >= 2:
                        pe.wait_ge(sig("inverse_step" + str(q)), (N // 2) * LEVELS)
                    pe.matmul(gps(q, 0), ones, gbuf(q, 4), start=True, stop=True)
                    for c in range(NT):
                        pe.matmul(gps(q, 1, c), kT(h, c), kT(h, c), start=True, stop=True)
                    for c in range(NT):
                        mm = pe.matmul(gps(q, 2, c), kT(h, c), GQ[:, h, c * P:(c + 1) * P], start=True, stop=True)
                    mm.then_inc(sig("products_ready"), 1)
                for q in range(2):
                    N = grp * 4 + n + q
                    pe.wait_ge(sig("level_masked" + str(q)), (N // 2) * LEVELS + 1)
                    for c in range(NT):
                        mm = pe.transpose(gps(q, 0, c), blk(gbuf(q, 1), c), ident)
                    mm.then_inc(sig("m0_turned"), 1)
                for lv in range(1, LEVELS):
                    for q in range(2):
                        N = grp * 4 + n + q
                        X_, T_, V_, M_ = XT[n + q], gbuf(q, 3), gbuf(q, 4), gbuf(q, 1 + lv % 2)
                        pe.wait_ge(sig("inverse_step" + str(q)), (N // 2) * LEVELS + lv)
                        pe.wait_ge(sig("level_masked" + str(q)), (N // 2) * LEVELS + lv + 1)
                        for c in range(NT):
                            mm = pe.matmul(gps(q, 0, c), blk(M_, c), blk(X_, c), start=True, stop=True)
                        mm.then_inc(sig("mx_ready" + str(q)), 1)
                    for q in range(2):
                        N = grp * 4 + n + q
                        X_, T_, V_ = XT[n + q], gbuf(q, 3), gbuf(q, 4)
                        pe.wait_ge(sig("mx_copied" + str(q)), (N // 2) * (LEVELS - 1) + lv)
                        for c in range(NT):
                            mm = pe.matmul(gps(q, 1, c), blk(T_, c), blk(V_, c), start=True, stop=True)
                        if lv < LEVELS - 1:
                            for c in range(NT):
                                mm = pe.matmul(gps(q, 2, c), blk(V_, c), blk(T_, c), start=True, stop=True)
                        mm.then_inc(sig("update_ready" + str(q)), 1)

        def dve_gdn_inverse(dve, grp, chain):
            for n in range(0, 4, 2):
                for q in range(2):
                    h = N = grp * 4 + n + q
                    if N >= 2:
                        dve.wait_ge(sig("update_ready" + str(q)), (N // 2) * (LEVELS - 1))
                    for c in range(NT):
                        ins = dve.tensor_scalar(blk(gbuf(q, 4), c), const("tri"), SEL(GRAW, c, h), None, ALU.mult)
                    ins.then_inc(sig("tri_scaled"), 1)
                for q in range(2):
                    h = N = grp * 4 + n + q
                    dve.wait_ge(sig("products_ready"), N + 1)
                    if N >= 2:
                        dve.wait_ge(sig("level_masked" + str(q)), (N // 2) * LEVELS)
                    for c in range(NT):
                        dve.tensor_scalar(blk(AT[n + q], c), gps(q, 0, c), SEL(GCUM, c, h), 0.0, ALU.subtract, ALU.min)
                        ins = dve.tensor_scalar(blk(gbuf(q, 0), c), gps(q, 0, c), SEL(GCUM, c, h), 0.0, ALU.subtract, ALU.max)
                    ins.then_inc(sig("gaps_ready"), 1)
                for q in range(2):
                    h = N = grp * 4 + n + q
                    dve.wait_ge(sig("decay_masked"), N + 1)
                    dve.tensor_tensor(AT[n + q], AT[n + q], gps(q, 2), ALU.mult)
                    for c in range(NT):
                        ins = dve.scalar_tensor_tensor(out=blk(gbuf(q, 0), c), in0=gps(q, 1, c), scalar=SEL(BETA, c, h),
                                                       in1=blk(gbuf(q, 0), c), op0=ALU.mult, op1=ALU.mult)
                    ins.then_inc(sig("lower_ready"), 1)
                for q in range(2):
                    N = grp * 4 + n + q
                    dve.wait_ge(sig("level_masked" + str(q)), (N // 2) * LEVELS + 1)
                    dve.wait_ge(sig("m0_turned"), N + 1)
                    for c in range(NT):
                        dve.tensor_tensor(blk(gbuf(q, 3), c), ident, blk(gbuf(q, 1), c), ALU.subtract)
                        ins = dve.tensor_tensor(blk(XT[n + q], c), ident, gps(q, 0, c), ALU.subtract)
                    ins.then_inc(sig("inverse_step" + str(q)), 1)
                for lv in range(1, LEVELS):
                    for q in range(2):
                        N = grp * 4 + n + q
                        dve.wait_ge(sig("update_ready" + str(q)), (N // 2) * (LEVELS - 1) + lv)
                        dve.wait_ge(sig("inverse_step" + str(q)), (N // 2) * LEVELS + lv)
                        if lv < LEVELS - 1:
                            dve.tensor_tensor(gbuf(q, 3), gbuf(q, 3), gps(q, 2), ALU.subtract)
                        dve.tensor_tensor(XT[n + q], XT[n + q], gps(q, 1), ALU.subtract).then_inc(sig("inverse_step" + str(q)), 1)

        def act_gdn_inverse(act, grp, chain):
            for n in range(0, 4, 2):
                for q in range(2):
                    N = grp * 4 + n + q
                    act.wait_ge(sig("gaps_ready"), N + 1)
                    act.activation(AT[n + q], AT[n + q], ACT.Exp)
                    act.activation(gbuf(q, 0), gbuf(q, 0), ACT.Exp, scale=-1.0).then_inc(sig("decay_ready"), 1)
                for lv in range(1, LEVELS):
                    for q in range(2):
                        N = grp * 4 + n + q
                        act.wait_ge(sig("mx_ready" + str(q)), (N // 2) * (LEVELS - 1) + lv)
                        act.activation(gbuf(q, 4), gps(q, 0), ACT.Copy).then_inc(sig("mx_copied" + str(q)), 1)

        def pool_gdn_inverse(pool, grp):
            for n in range(0, 4, 2):
                for q in range(2):
                    N = grp * 4 + n + q
                    pool.wait_ge(sig("decay_ready"), N + 1)
                    a3 = AT[n + q].rearrange("p (c s) -> p c s", c=NT)
                    l3 = gbuf(q, 0).rearrange("p (c s) -> p c s", c=NT)
                    pool.affine_select(out=a3, in_=a3, compare_op=ALU.is_ge, fill=0.0, base=0,
                                       pattern=[[0, NT], [1, P]], channel_multiplier=-1)
                    pool.affine_select(out=l3, in_=l3, compare_op=ALU.is_gt, fill=0.0, base=0,
                                       pattern=[[0, NT], [-1, P]], channel_multiplier=1).then_inc(sig("decay_masked"), 1)
                for lv in range(LEVELS):
                    mask = const("level")[:, lv * P:(lv + 1) * P]
                    for q in range(2):
                        N = grp * 4 + n + q
                        if lv == 0:
                            pool.wait_ge(sig("lower_ready"), N + 1)
                        if lv == 2:
                            pool.wait_ge(sig("inverse_step" + str(q)), (N // 2) * LEVELS + 1)
                        if lv > 2:
                            pool.wait_ge(sig("mx_ready" + str(q)), (N // 2) * (LEVELS - 1) + lv - 2)
                        for c in range(NT):
                            ins = pool.tensor_tensor(blk(gbuf(q, 1 + lv % 2), c), blk(gbuf(q, 0), c), mask, ALU.mult)
                        ins.then_inc(sig("level_masked" + str(q)), 1)
        def bank4(n, h=None):
            return PS[:, n * 512:n * 512 + 512] if h is None else PS[:, n * 512 + h * P:n * 512 + (h + 1) * P]

        def hs(v, h):
            return v[:, h * P:(h + 1) * P]
        RHS = [WORK[:, 8192:8704], WORK[:, 8704:9216]]

        def pe_scan(pe, grp):
            for c in range(NT):
                n = grp * NT + c
                ns = grp * (NT - 1) + c
                kT = lambda h: GQ[:, 8 + grp * 4 + h, c * P:(c + 1) * P]
                qT = lambda h: GQ[:, grp * 4 + h, c * P:(c + 1) * P]
                if c:
                    pe.wait_ge(sig("state_ready"), ns)
                    for h in range(4):
                        pe.matmul(bank4(0, h), kT(h), STATE[:, h, :], start=True, stop=True)
                    for h in range(4):
                        mm = pe.matmul(bank4(1, h), qT(h), STATE[:, h, :], start=True, stop=True)
                    mm.then_inc(sig("from_state"), 1)
                    pe.wait_ge(sig("rhs_ready"), ns)
                for h in range(4):
                    rhs = hs(RHS[0], h) if c else VTOK[:, grp * 4 + h, c, :]
                    mm = pe.matmul(bank4(2, h), blk(XT[h], c), rhs, start=True, stop=True)
                mm.then_inc(sig("vnew_ready"), 1)
                pe.wait_ge(sig("vnew_copied"), n + 1)
                if c < NT - 1:
                    for h in range(4):
                        mm = pe.matmul(bank4(3, h), KTOK[:, grp * 4 + h, c, :], hs(VNEW, h), start=True, stop=True)
                    mm.then_inc(sig("state_sums"), 1)
                if n:
                    pe.wait_ge(sig("out_stored"), n)
                for h in range(4):
                    mm = pe.matmul(bank4(4, h), blk(AT[h], c), hs(VNEW, h), start=True, stop=True)
                mm.then_inc(sig("out_ready"), 1)

        def dve_scan(dve, grp):
            for c in range(NT):
                n = grp * NT + c
                ns = grp * (NT - 1) + c
                if c:
                    dve.wait_ge(sig("from_state"), ns)
                    for h in range(4):
                        ins = dve.scalar_tensor_tensor(out=hs(RHS[0], h), in0=bank4(0, h), scalar=SEL(NCOEF, c, grp * 4 + h),
                                                       in1=VTOK[:, grp * 4 + h, c, :], op0=ALU.mult, op1=ALU.add)
                    ins.then_inc(sig("rhs_ready"), 1)
                if c < NT - 1:
                    dve.wait_ge(sig("state_sums"), ns + 1)
                    for h in range(4):
                        if c:
                            ins = dve.scalar_tensor_tensor(out=STATE[:, h, :], in0=STATE[:, h, :],
                                                           scalar=SEL(EGL, c, grp * 4 + h), in1=bank4(3, h),
                                                           op0=ALU.mult, op1=ALU.add)
                        else:
                            ins = dve.tensor_copy(STATE[:, h, :], bank4(3, h))
                    ins.then_inc(sig("state_ready"), 1)
                    dve.wait_ge(sig("state_ready"), ns + 1)
                dve.wait_ge(sig("out_ready"), n + 1)
                out = VTOK[:, grp * 4:grp * 4 + 4, c, :]
                o = bank4(4).rearrange("p (h e) -> p h e", h=4)
                if c:
                    dve.wait_ge(sig("q_state_scaled"), ns)
                    ins = dve.tensor_tensor(out, QEXP.rearrange("p (h e) -> p h e", h=4), o, ALU.add)
                else:
                    ins = dve.tensor_copy(out, o)
                ins.then_inc(sig("out_stored"), 1)

        def act_scan(act, grp):
            for c in range(NT):
                n = grp * NT + c
                ns = grp * (NT - 1) + c
                if c:
                    act.wait_ge(sig("from_state"), ns)
                    act.wait_ge(sig("out_stored"), n)
                    for h in range(4):
                        ins = act.activation(hs(QEXP, h), bank4(1, h), ACT.Copy, scale=SEL(EG, c, grp * 4 + h))
                    ins.then_inc(sig("q_state_scaled"), 1)
                act.wait_ge(sig("vnew_ready"), n + 1)
                if n:
                    act.wait_ge(sig("out_ready"), n)
                act.activation(VNEW, bank4(2), ACT.Copy).then_inc(sig("vnew_copied"), 1)

        ZS = [WORK[:, n * T:(n + 1) * T] for n in range(2)]
        OSQ = [WORK[:, (2 + n) * T:(3 + n) * T] for n in range(2)]

        def act_gdn_out(act, chain):
            for h in range(GH):
                if h >= 2:
                    act.wait_ge(sig("gated"), h - 1)
                act.activation(ZS[h % 2], GQ[:, 24 + h, :], ACT.Exp, scale=-1.0).then_inc(sig("z_exp"), 1)
                act.activation(OSQ[h % 2].rearrange("p (c e) -> p c e", c=NT), VTOK[:, h, :, :],
                               ACT.Square).then_inc(sig("o_squared"), 1)
                act.wait_ge(sig("o_summed"), h + 1)
                r = SM[:, 32 + (h % 2) * 4:36 + (h % 2) * 4]
                chain(act.activation(r, r, ACT.Ln, scale=1.0 / P, bias=SM[:, 0:1]))
                act.activation(r, r, ACT.Exp, scale=-0.5).then_inc(sig("o_rstd"), 1)

        def dve_gdn_out(dve, chain):
            for h in range(GH):
                dve.wait_ge(sig("o_squared"), h + 1)
                r = SM[:, 32 + (h % 2) * 4:36 + (h % 2) * 4]
                dve.tensor_reduce(r, OSQ[h % 2].rearrange("p (c e) -> p c e", c=NT), AX_X, ALU.add).then_inc(sig("o_summed"), 1)
                Z = ZS[h % 2]
                chain(dve.tensor_scalar(Z, Z, 1.0, None, ALU.add))
                chain(dve.reciprocal(Z, Z))
                chain(dve.tensor_tensor(Z, Z, GQ[:, 24 + h, :], ALU.mult))
                dve.wait_ge(sig("o_rstd"), h + 1)
                for c in range(NT):
                    ins = dve.tensor_scalar(VTOK[:, h, c, :], VTOK[:, h, c, :], r[:, c:c + 1], None, ALU.mult)
                ins.then_inc(sig("o_normed"), 1)
                dve.wait_ge(sig("o_turned"), h + 1)
                dve.scalar_tensor_tensor(out=H[:, h, 0:T], in0=PS[:, (h % 2) * 512:(h % 2) * 512 + T], scalar=par("gnorm"),
                                         in1=Z, op0=ALU.mult, op1=ALU.mult).then_inc(sig("gated"), 1)

        def pe_gdn_out(pe):
            for h in range(GH):
                pe.wait_ge(sig("o_normed"), h + 1)
                for c in range(NT):
                    mm = pe.transpose(PS[:, (h % 2) * 512 + c * P:(h % 2) * 512 + (c + 1) * P], VTOK[:, h, c, :], ident)
                mm.then_inc(sig("o_turned"), 1)

        Q2 = BIG[:, 0:15 * TA].rearrange("p (k t) -> p k t", k=15)
        V2 = BIG[:, 15 * TA:15 * TA + 6 * 640].rearrange("p (a c) -> p a c", a=6)
        UB, UG, QA, QC, KC, QD, KD, KA = 0, 2, 4, 6, 8, 10, 12, 14
        GW = 15 + T + 15 + 15 + TC + 15
        GLU = WORK[:, 0:2 * GW].rearrange("p (j t) -> p j t", j=2)
        YW = GW - 30
        YC = WORK[:, 2 * GW:2 * GW + 2 * YW].rearrange("p (j t) -> p j t", j=2)
        GE = WORK[:, 3300:3300 + 2 * TA].rearrange("p (j t) -> p j t", j=2)
        CTX0 = T + 30
        LAST = 3

        def in_tiles(layer):
            q = SEG1 if layer == LAST else SEG2
            return [(0, 4, 2, q), (4, 1, 2, SEG2), (5, 1, 2, q), (6, 1, 2, SEG2), (7, 1, 1, SEG2)]

        def pe_in(pe, layer):
            for first, n, chunks, segs in in_tiles(layer):
                pe_feature_tiles(pe, f"in{layer}", H, segs, n, first, chunks, nb=2)
            pe_token_tiles(pe, f"in{layer}", TA, 2, 8, nb=2)
            pe_token_tiles(pe, f"in{layer}", TA, 1, 10, cols=P, nb=2)

        def act_in(act, layer):
            for first, n, chunks, segs in in_tiles(layer):
                if first == 0:
                    act_copy_tiles(act, f"in{layer}", Q2, segs, 2, 0, chunks, nb=2)
                    act.wait_ge(evac_done, E0[f"in{layer}"] + 2)
                    w = sum(x for _, x in segs)
                    act.activation(GE[:, :, 0:w], Q2[:, UG:UG + 2, 0:w], ACT.Exp, scale=-1.0).then_inc(sig("glu_exp"), 1)
                    act_copy_tiles(act, f"in{layer}", Q2, segs, 2, 2, chunks, nb=2)
                else:
                    act_copy_tiles(act, f"in{layer}", Q2, segs, n, first, chunks, nb=2)
            act_token_tiles(act, f"in{layer}", V2, TA, 2, 8, nb=2)
            act_token_tiles(act, f"in{layer}", V2, TA, 1, 10, cols=P, nb=2, col0=512)

        def dve_in(dve, layer, chain):
            l = layer - 2
            segs = SEG1 if layer == LAST else SEG2
            w = sum(x for _, x in segs)
            chain(dve.memset(WORK[:, 0:2 * GW], 0.0))
            b = base("dve", "glu_exp", 1)
            dve.wait_ge(sig("glu_exp"), b + 1)
            chain(dve.tensor_scalar(GE[:, :, 0:w], GE[:, :, 0:w], 1.0, None, ALU.add))
            chain(dve.reciprocal(GE[:, :, 0:w], GE[:, :, 0:w]))
            for (c0, x), o in zip(segs, (15, T + 45)):
                ins = dve.tensor_tensor(GLU[:, :, o:o + x], Q2[:, UB:UB + 2, c0:c0 + x], GE[:, :, c0:c0 + x], ALU.mult)
            chain(ins)
            cw = par("cw").rearrange("p (l j k) -> p l j k", l=2, j=2)
            cb = par("cb").rearrange("p (l j) -> p l j", l=2)
            yw = T if layer == LAST else YW
            for tap in range(31):
                for j in range(2):
                    y, x = YC[:, j, 0:yw], GLU[:, j, tap:tap + yw]
                    if tap == 0:
                        ins = dve.tensor_scalar(y, x, cw[:, l, j, 0:1], cb[:, l, j:j + 1], ALU.mult, ALU.add)
                    else:
                        ins = dve.scalar_tensor_tensor(out=y, in0=x, scalar=cw[:, l, j, tap:tap + 1], in1=y,
                                                       op0=ALU.mult, op1=ALU.add)
                chain(ins)

        YSQ = WORK[:, 3300:3300 + 2 * TA].rearrange("p (j t) -> p j t", j=2)
        YR = WORK[:, 4900:4900 + TA]
        TAB = WORK[:, 5700:5700 + 4 * T].rearrange("p (n t) -> p n t", n=4)

        def yseg(layer):
            return [(0, 0, T)] if layer == LAST else [(0, 0, T), (CTX0, T, TC)]

        def rope2_chunks():
            return [(Q2[:, x, 0:T], const("perm_64"), TAB[:, 0, :], TAB[:, 1, :]) for x in (QA, QA + 1, KA)] + \
                   [(Q2[:, x, 0:T], const("perm_32"), TAB[:, 2, :], TAB[:, 3, :]) for x in (QC, QC + 1, KC, KC + 1)]

        def pe_conv_norm(pe, layer):
            b = base("pe", "centered", 1)
            b2 = base("pe", "y_squared", 1)
            for y0, o, w in yseg(layer):
                for j in range(2):
                    mm = pe.matmul(PS[:, 2048 + o:2048 + o + w], ones, YC[:, j, y0:y0 + w], start=j == 0, stop=j == 1)
            mm.then_inc(sig("y_summed"), 1)
            pe_rope(pe, rope2_chunks())
            pe.wait_ge(sig("y_squared"), b2 + 1)
            for y0, o, w in yseg(layer):
                for j in range(2):
                    mm = pe.matmul(PS[:, 3072 + o:3072 + o + w], ones, YSQ[:, j, o:o + w], start=j == 0, stop=j == 1)
            mm.then_inc(sig("y_squares_summed"), 1)

        def act_conv_norm(act, layer, chain):
            b = base("act", "centered", 1)
            bs = base("act", "y_squares_summed", 1)
            bn = base("act", "y_normed", 1)
            act.wait_ge(sig("centered"), b + 1)
            for y0, o, w in yseg(layer):
                ins = act.activation(YSQ[:, :, o:o + w], YC[:, :, y0:y0 + w], ACT.Square)
            ins.then_inc(sig("y_squared"), 1)
            act.wait_ge(sig("y_squares_summed"), bs + 1)
            w = T if layer == LAST else TA
            chain(act.activation(YR[:, 0:w], PS[:, 3072:3072 + w], ACT.Ln, scale=1.0 / 256, bias=SM[:, 0:1]))
            act.activation(YR[:, 0:w], YR[:, 0:w], ACT.Exp, scale=-0.5).then_inc(sig("y_rstd"), 1)
            act.wait_ge(sig("y_normed"), bn + 1)
            act.activation(YSQ[:, :, 0:w], H[:, 2:4, 0:w], ACT.Exp, scale=-1.0).then_inc(sig("y_exp"), 1)

        def dve_conv_norm(dve, layer, chain):
            l = layer - 2
            b1 = base("dve", "y_summed", 1)
            b2 = base("dve", "y_rstd", 1)
            b3 = base("dve", "y_exp", 1)
            bt = base("dve", "tables_loaded", 16)
            dve.wait_ge(sig("y_summed"), b1 + 1)
            for y0, o, w in yseg(layer):
                for j in range(2):
                    ins = dve.scalar_tensor_tensor(out=YC[:, j, y0:y0 + w], in0=PS[:, 2048 + o:2048 + o + w],
                                                   scalar=-1.0 / 256, in1=YC[:, j, y0:y0 + w], op0=ALU.mult, op1=ALU.add)
            ins.then_inc(sig("centered"), 1)
            dve.wait_ge(tables_loaded, 16 + bt + 16)
            dve_rope(dve, rope2_chunks(), chain)
            dve.wait_ge(sig("y_rstd"), b2 + 1)
            g = par("lng").rearrange("p (l j) -> p l j", l=2)
            be = par("lnb").rearrange("p (l j) -> p l j", l=2)
            for y0, o, w in yseg(layer):
                for j in range(2):
                    ins = dve.tensor_tensor(H[:, 2 + j, o:o + w], YC[:, j, y0:y0 + w], YR[:, o:o + w], ALU.mult)
            chain(ins)
            w = T if layer == LAST else TA
            for j in range(2):
                ins = dve.tensor_scalar(H[:, 2 + j, 0:w], H[:, 2 + j, 0:w], g[:, l, j:j + 1], be[:, l, j:j + 1],
                                        ALU.mult, ALU.add)
            ins.then_inc(sig("y_normed"), 1)
            dve.wait_ge(sig("y_exp"), b3 + 1)
            chain(dve.tensor_scalar(YSQ[:, :, 0:w], YSQ[:, :, 0:w], 1.0, None, ALU.add))
            chain(dve.reciprocal(YSQ[:, :, 0:w], YSQ[:, :, 0:w]))
            dve.tensor_tensor(H[:, 2:4, 0:w], H[:, 2:4, 0:w], YSQ[:, :, 0:w], ALU.mult)
            lq = par("lq").rearrange("p (l n d) -> p l n d", l=2, n=4)
            for m in range(2):
                dve.tensor_tensor(LTMP[:, m, :], lq[:, l, 2 * m, :], lq[:, l, 2 * m + 1, :], ALU.mult)
            chain(dve.memset(SM[:, 42:43], 0.0))
            dve.tensor_reduce(SM[:, 40:42], LTMP, AX_X, ALU.add).then_inc(sig("lam_sums"), 1)
            bl = base("dve", "lam_exps", 1)
            dve.wait_ge(sig("lam_exps"), bl + 1)
            chain(dve.tensor_tensor(SM[:, 42:43], SM[:, 41:42], SM[:, 40:41], ALU.subtract))
            dve.tensor_scalar(SM[:, 42:43], SM[:, 42:43], -lambda_init(l), None, ALU.add)

        LTMP = WORK[:, 7800:7864].rearrange("p (m d) -> p m d", m=2)

        def lambda_init(l):
            return 0.8 - 0.6 * float(np.exp(-0.3 * l))

        def act_lambda(act):
            b = base("act", "lam_sums", 1)
            act.wait_ge(sig("lam_sums"), b + 1)
            act.activation(SM[:, 40:42], SM[:, 40:42], ACT.Exp).then_inc(sig("lam_exps"), 1)

        SLOTN = 14
        BT = WORK[:, 6 * TA:6 * TA + 4 * SLOTN * 64].rearrange("p (h s c) -> p h s c", h=4, s=SLOTN)

        def pe_bias(pe, l):
            rpb = par("rpb").rearrange("p (l h r) -> p l h r", l=2, h=4)
            hot = const("onehot")
            for rnd in range(8):
                for cc in range(8):
                    c = rnd * 8 + cc
                    for p in range(2):
                        o = rnd * 512 + cc * 56
                        for h in range(4):
                            mm = pe.matmul(PS[p * 64:p * 64 + 64, o + h * SLOTN:o + (h + 1) * SLOTN], hot[0:31, 63 - c:127 - c],
                                           rpb[0:31, l, h, 1 - p:15 - p], start=True, stop=True)
                mm.then_inc(sig("bias_ready"), 1)

        def dve_bias(dve, l):
            b = base("dve", "bias_ready", 8)
            for rnd in range(8):
                dve.wait_ge(sig("bias_ready"), b + rnd + 1)
                src = PS[:, rnd * 512:rnd * 512 + 448].rearrange("p (c h s) -> p h s c", c=8, h=4)
                mask = const("colmask")[:, rnd * 8:rnd * 8 + 8]
                for h in range(4):
                    dve.tensor_tensor(BT[:, h, :, rnd * 8:rnd * 8 + 8], src[:, h, :, :],
                                      mask.rearrange("p (a c) -> p a c", a=1).to_broadcast([P, SLOTN, 8]), ALU.add)

        def mixer_jobs(layer):
            l = layer - 2
            singles, doubles = [], []
            sinks = par("sink").rearrange("p (l h) -> p l h", l=2)
            qtiles = range(NT if layer == LAST else TA // P)
            for h in range(4):
                g = h // 2
                r = slice(g * 64, g * 64 + 64)
                out_r = slice((h % 2) * 64, (h % 2) * 64 + 64)
                vs = lambda a: V2[:, a, 512 + g * 64:512 + g * 64 + 64]
                for i in qtiles:
                    q = Q2[r, QA + h % 2, i * P:(i + 1) * P]
                    if i < NT:
                        lo, hi = max(i - 1, 0), min(i + 1, NT - 1)
                        n1 = (hi - lo + 1) * P
                        ks = [(0, Q2[r, KA, lo * P:(hi + 1) * P]), (512, Q2[r, KA, T:TA])]
                        pieces = []
                        for x, blk_ in enumerate(range(lo, hi + 1)):
                            m = const("band_lo") if blk_ < i else const("band_hi") if blk_ > i else None
                            pieces.append((x * P, x * P, P, m))
                        pieces.append((n1, 512, TC, None))
                        v = [vs(a) for a in range(lo, hi + 1)] + [vs(4), vs(5)]
                    else:
                        ks = [(0, Q2[r, KA, T:TA])]
                        pieces = [(0, 0, TC, None)]
                        v = [vs(4), vs(5)]
                    singles.append(dict(q=[q], k=[ks], v=v, pieces=pieces, scale=0.125, sink=sinks[:, l, h:h + 1],
                                        off=(h % 2) * 64, out=H[out_r, h // 2, i * P:(i + 1) * P]))
            for h in range(4):
                r = slice((h % 2) * 64, (h % 2) * 64 + 64)
                vs = lambda a: V2[:, a, 256 + h * 64:256 + h * 64 + 64]
                for i in qtiles:
                    q = Q2[r, QD + h // 2, i * P:(i + 1) * P]
                    kv = lambda a, b: Q2[r, KD + h // 2, a:b]
                    if i < NT:
                        ks = [(0, kv(0, T)), (512, kv(T, TA))]
                        bias = BT[:, h, 6 - 2 * i:14 - 2 * i, :].rearrange("p s c -> p (s c)")
                        pieces = [(0, 0, T, bias), (T, 512, TC, None)]
                        v = [vs(a) for a in range(6)]
                    else:
                        ks, pieces, v = [(0, kv(T, TA))], [(0, 0, TC, None)], [vs(4), vs(5)]
                    singles.append(dict(q=[q], k=[ks], v=v, pieces=pieces, scale=0.125, sink=None,
                                        off=(h % 2) * 64, out=H[r, 6 + h // 2, i * P:(i + 1) * P]))
            for h in range(4):
                vs = lambda a: V2[:, a, h * 64:h * 64 + 64]
                for i in qtiles:
                    qs, ks = [], []
                    for m in range(2):
                        r = slice((h % 2) * 64 + m * 32, (h % 2) * 64 + m * 32 + 32)
                        qs.append(Q2[r, QC + h // 2, i * P:(i + 1) * P])
                        kv = lambda a, b: Q2[r, KC + h // 2, a:b]
                        ks.append([(0, kv(0, T)), (512, kv(T, TA))] if i < NT else [(0, kv(T, TA))])
                    full = i < NT
                    r = slice((h % 2) * 64, (h % 2) * 64 + 64)
                    doubles.append(dict(q=qs, k=ks, v=[vs(a) for a in (range(6) if full else (4, 5))],
                                        pieces=[(0, 0, TA if full else TC, None)], scale=32 ** -0.5, sink=None,
                                        neg_lam=SM[:, 42:43], off=(h % 2) * 64, out=H[r, 4 + h // 2, i * P:(i + 1) * P]))
            return singles, doubles

        def act_sub_norm(act, layer, chain):
            w = T if layer == LAST else TA
            b = base("act", "heads_summed", 2)
            for n in range(2):
                act.activation(WORK[:, n * TA:n * TA + w], H[:, 4 + n, 0:w], ACT.Square).then_inc(sig("heads_squared"), 1)
            for n in range(2):
                act.wait_ge(sig("heads_summed"), b + n + 1)
                R = WORK[:, (2 + n) * TA:(2 + n) * TA + w]
                chain(act.activation(R, PS[:, n * 1024:n * 1024 + w], ACT.Ln, scale=1.0 / 64, bias=SM[:, 0:1]))
                act.activation(R, R, ACT.Exp, scale=-0.5).then_inc(sig("heads_rstd"), 1)

        def pe_sub_norm(pe, layer):
            b = base("pe", "heads_squared", 2)
            for n in range(2):
                pe.wait_ge(sig("heads_squared"), b + n + 1)
                for c0, w in SEG1 if layer == LAST else SEG2:
                    mm = pe.matmul(PS[:, n * 1024 + c0:n * 1024 + c0 + w], const("half64"), WORK[:, n * TA + c0:n * TA + c0 + w],
                                   start=True, stop=True)
                mm.then_inc(sig("heads_summed"), 1)

        def dve_sub_norm(dve, layer, chain):
            l = layer - 2
            w = T if layer == LAST else TA
            b = base("dve", "heads_rstd", 2)
            chain(dve.tensor_scalar(SM[:, 43:44], par("subg")[:, l:l + 1], 1.0 - lambda_init(l), None, ALU.mult))
            for n in range(2):
                dve.wait_ge(sig("heads_rstd"), b + n + 1)
                dve.scalar_tensor_tensor(out=H[:, 4 + n, 0:w], in0=H[:, 4 + n, 0:w], scalar=SM[:, 43:44],
                                         in1=WORK[:, (2 + n) * TA:(2 + n) * TA + w], op0=ALU.mult, op1=ALU.mult)
        def store_order():
            return outT

        block = ctx.enter_context(nc.Block())

        @block.sync
        def _(sp):
            sp.dma_start(PR[:, :], params).then_inc(loaded, 16)
            sp.dma_start(CN[:, :], consts).then_inc(loaded, 16)
            sp.dma_start(X[:, :, 0:T], xT).then_inc(loaded, 16)
            sp.dma_start(X[:, :, T:TA], ctxT).then_inc(loaded, 16)
            sp.dma_start(POS.bitcast(I32), positions.to_broadcast([P, T])).then_inc(tables_loaded, 16)
            for name, kind, n in linear_plan():
                src, width = (w_tiles, TILE) if kind == "w" else (d_tiles, DOWN)

                def load(t, u, i, name=name, src=src, width=width):
                    g = G0[name] + u
                    if G0[name] + u >= SLOTS or not isinstance(i, int) or i > 0:
                        sp.wait_ge(tile_done, t + (G0[name] - SLOTS + 1))
                    at = t + FROM[name]
                    sp.dma_start(ring[:, g % SLOTS:g % SLOTS + 1, 0:width],
                                 src[bass.ds(at, 1), :, :].rearrange("a p c -> p a c")).then_inc(tile_loaded[g % SLOTS], 16)
                if G0[name] == 0:
                    for u in range(SLOTS):
                        load(u, u, 0)
                    rounds = n // SLOTS
                    with sp.Fori(1, rounds) as i:
                        for u in range(SLOTS):
                            load(i * SLOTS + u, u, i)
                else:
                    over_tiles(sp, n, load)
            sp.wait_ge(sig("out_normed"), 1)
            sp.dma_start(outT, H[:, :, 0:T]).then_inc(stored, 16)
            sp.wait_ge(stored, 16)

        @block.tensor
        def _(pe):
            ph = Phase()
            pe.wait_ge(loaded, 64)
            ph.end(pe)
            for layer in range(4):
                segs = SEG1 if layer < 2 or layer == LAST else SEG2
                pe_ada(pe, layer)
                ph.end(pe)
                pe_norm(pe, SEG2 if layer >= 2 else SEG1)
                ph.end(pe)
                if layer == 0:
                    pe_feature_tiles(pe, "attn_in", H, SEG1, 8)
                    pe_token_tiles(pe, "attn_in", T, 4, 8)
                    ph.end(pe)
                    pe_rope(pe, rope1_chunks())
                    ph.end(pe)
                    pe_attention(pe, causal_jobs())
                    ph.end(pe)
                    pe_stick(pe)
                    ph.end(pe)
                    pe_feature_tiles(pe, "attn_out", H, SEG1, 4)
                elif layer == 1:
                    pe_gdn_in(pe)
                    ph.end(pe)
                    pe_gdn_prep(pe)
                    ph.end(pe)
                    for grp in range(2):
                        pe_gdn_inverse(pe, grp)
                        ph.end(pe)
                        pe_scan(pe, grp)
                        ph.end(pe)
                    pe_gdn_out(pe)
                    ph.end(pe)
                    pe_feature_tiles(pe, "gdn_out", H, SEG1, 4)
                else:
                    pe_in(pe, layer)
                    ph.end(pe)
                    pe_conv_norm(pe, layer)
                    ph.end(pe)
                    pe_bias(pe, layer - 2)
                    ph.end(pe)
                    singles, doubles = mixer_jobs(layer)
                    pe_attention(pe, singles)
                    ph.end(pe)
                    pe_attention(pe, doubles)
                    ph.end(pe)
                    pe_sub_norm(pe, layer)
                    ph.end(pe)
                    pe_feature_tiles(pe, f"out{layer}", H, segs, 4)
                ph.end(pe)
                pe_norm(pe, segs)
                ph.end(pe)
                pe_feature_tiles(pe, f"up{layer}", H, segs, FC)
                ph.end(pe)
                pe_down(pe, f"down{layer}", segs)
                ph.end(pe)
                if layer in (1, 3):
                    pe_norm(pe, SEG1)
                    ph.end(pe)

        @block.scalar
        def _(act):
            ph = Phase()
            chain = Chain(act, act_chain)
            act.wait_ge(loaded, 64)
            act.activation(SC[:, :], PR[:, 0:3 * DC], ACT.Exp, scale=-1.0).then_inc(sig("c_exp"), 1)
            act.drain().then_inc(evac_done, 8)
            ph.end(act)
            for layer in range(4):
                segs = SEG1 if layer < 2 or layer == LAST else SEG2
                ph.end(act)
                act_norm(act, SEG2 if layer >= 2 else SEG1, chain, MOD[:, 0:DC, :])
                ph.end(act)
                if layer == 0:
                    act_copy_tiles(act, "attn_in", QK1, SEG1, 8)
                    act_token_tiles(act, "attn_in", V1, T, 4, 8)
                    ph.end(act)
                    act.wait_ge(sig("angles_ready"), 1)
                    act.activation(QK1[:, 8:12, :], QK1[:, 8:12, :], ACT.Copy, scale=0.125)
                    chain(act.activation(COS1, COS1, ACT.Sin))
                    chain(act.activation(SIN1, SIN1, ACT.Sin))
                    act.activation(SIN1, SIN1, ACT.Copy, scale=const("sign")).then_inc(sig("angles_done"), 1)
                    ph.end(act)
                    act_attention(act, causal_jobs(), chain)
                    ph.end(act)
                    act_stick(act, chain)
                    ph.end(act)
                elif layer == 1:
                    act_gdn_in(act, chain)
                    ph.end(act)
                    act_gdn_prep(act, chain)
                    ph.end(act)
                    for grp in range(2):
                        act_gdn_inverse(act, grp, chain)
                        ph.end(act)
                        act_scan(act, grp)
                        ph.end(act)
                    act_gdn_out(act, chain)
                    ph.end(act)
                else:
                    act_in(act, layer)
                    ph.end(act)
                    act.dma_start(TAB, rope_tables).then_inc(tables_loaded, 16)
                    act_conv_norm(act, layer, chain)
                    act_lambda(act)
                    ph.end(act)
                    ph.end(act)
                    singles, doubles = mixer_jobs(layer)
                    act_attention(act, singles, chain)
                    ph.end(act)
                    act_attention(act, doubles, chain)
                    ph.end(act)
                    act_sub_norm(act, layer, chain)
                    ph.end(act)
                ph.end(act)
                act_norm(act, segs, chain, MOD[:, 3 * DC:4 * DC, :])
                ph.end(act)
                act_up(act, f"up{layer}", segs)
                ph.end(act)
                ph.end(act)
                if layer in (1, 3):
                    act_norm(act, SEG1, chain)
                    ph.end(act)

        @block.vector
        def _(dve):
            ph = Phase()
            chain = Chain(dve, dve_chain)
            dve.memset(SM[:, 0:1], EPS)
            dve.memset(SM[:, 1:2], 1.0)
            dve.memset(SM[:, 2:3], P * EPS)
            dve.wait_ge(loaded, 64)
            dve.wait_ge(sig("c_exp"), 1)
            chain(dve.tensor_scalar(SC[:, :], SC[:, :], 1.0, None, ALU.add))
            chain(dve.reciprocal(SC[:, :], SC[:, :]))
            dve.tensor_tensor(SC[:, :], SC[:, :], PR[:, 0:3 * DC], ALU.mult)
            ph.end(dve)
            for layer in range(4):
                segs = SEG1 if layer < 2 or layer == LAST else SEG2
                dve_ada(dve, layer, chain)
                ph.end(dve)
                dve_norm(dve, SEG2 if layer >= 2 else SEG1, GAIN[:, 0, :, :])
                ph.end(dve)
                if layer == 0:
                    dve_angles(dve, chain)
                    dve.tensor_copy(SM[:, 44:45], SM[:, 0:1]).then_inc(sig("angles_ready"), 1)
                    ph.end(dve)
                    dve.wait_ge(sig("angles_done"), 1)
                    dve_rope(dve, rope1_chunks(), chain)
                    ph.end(dve)
                    dve_attention(dve, causal_jobs(), chain)
                    ph.end(dve)
                    dve_stick(dve)
                    ph.end(dve)
                    dve_residual_tiles(dve, "attn_out", MOD[:, 2 * DC:3 * DC, :], SEG1, 4)
                elif layer == 1:
                    dve_gdn_in(dve, chain)
                    ph.end(dve)
                    dve_gdn_prep(dve, chain)
                    ph.end(dve)
                    for grp in range(2):
                        dve_gdn_inverse(dve, grp, chain)
                        ph.end(dve)
                        dve_scan(dve, grp)
                        ph.end(dve)
                    dve_gdn_out(dve, chain)
                    ph.end(dve)
                    dve_residual_tiles(dve, "gdn_out", MOD[:, 2 * DC:3 * DC, :], SEG1, 4)
                else:
                    dve_in(dve, layer, chain)
                    ph.end(dve)
                    dve_conv_norm(dve, layer, chain)
                    ph.end(dve)
                    dve_bias(dve, layer - 2)
                    ph.end(dve)
                    singles, doubles = mixer_jobs(layer)
                    dve_attention(dve, singles, chain)
                    ph.end(dve)
                    dve_attention(dve, doubles, chain)
                    ph.end(dve)
                    dve_sub_norm(dve, layer, chain)
                    ph.end(dve)
                    dve_residual_tiles(dve, f"out{layer}", MOD[:, 2 * DC:3 * DC, :], segs, 4)
                ph.end(dve)
                dve_norm(dve, segs, GAIN[:, 1, :, :])
                ph.end(dve)
                dve_up(dve, f"up{layer}", segs, chain)
                ph.end(dve)
                dve_down(dve, f"down{layer}", MOD[:, 5 * DC:6 * DC, :], segs)
                ph.end(dve)
                if layer in (1, 3):
                    dve_norm(dve, SEG1, FIN_G[layer // 2])
                    if layer == 1:
                        chain(dve.tensor_copy(SM[:, 44:45], SM[:, 0:1]))
                        for k in range(DC):
                            ins = dve.tensor_copy(X[:, k, 0:T], H[:, k, 0:T])
                    else:
                        dve.drain().then_inc(sig("out_normed"), 1)
                    ph.end(dve)

        @block.gpsimd
        def _(pool):
            ph = Phase()
            ph.end(pool)
            for layer in range(4):
                for _ in range(3):
                    ph.end(pool)
                if layer == 0:
                    ph.end(pool)
                    ph.end(pool)
                    pool_stick(pool)
                    ph.end(pool)
                elif layer == 1:
                    pool_gdn_prep(pool)
                    ph.end(pool)
                    for grp in range(2):
                        pool_gdn_inverse(pool, grp)
                        ph.end(pool)
                        ph.end(pool)
                    ph.end(pool)
                else:
                    for _ in range(5):
                        ph.end(pool)
                for _ in range(4):
                    ph.end(pool)
                if layer in (1, 3):
                    ph.end(pool)


def constants():
    c = np.zeros((P, CONST_W), np.float32)

    def put(name, v):
        a, w = CONST[name]
        c[:v.shape[0], a:a + w] = v
    i, j = np.arange(P)[:, None], np.arange(P)[None, :]
    put("ident", np.eye(P))
    put("ones", np.ones((P, P)))
    put("tri", i <= j)
    put("negtri", -1.0 * (i >= j))
    put("negones", -np.ones((P, P)))

    def swap(width, half):
        m = np.zeros((P, P))
        for x in range(P):
            y = x % width
            if y < 2 * half:
                m[x + half if y < half else x - half, x] = 1
        return m
    put("perm_a1", swap(64, 8))
    put("perm_64", swap(64, 32))
    put("perm_32", swap(32, 16))
    put("causal", np.where(j <= i, 0, NEG))
    put("band_lo", np.where(j >= i, 0, NEG))
    put("band_hi", np.where(j <= i, 0, NEG))
    levels = []
    for lv in range(7):
        s = 1 << lv
        levels.append((i // (2 * s) == j // (2 * s)) & (i % (2 * s) >= s) & (j % (2 * s) < s))
    put("level", np.concatenate(levels, 1))
    put("onehot", (np.arange(31)[:, None] == 78 - j).astype(np.float32))
    q, k = np.arange(64)[:, None], np.arange(64)[None, :]
    start = np.clip(q - 8, 0, 48)
    put("colmask", np.tile(np.where((k >= start) & (k < start + 16), 0, NEG), (2, 1)))
    put("half64", i // 64 == j // 64)
    freq = np.float32(500000.0) ** (-np.arange(8, dtype=np.float32) * np.float32(2.0) / np.float32(16))
    f, s = np.zeros((P, 1)), np.zeros((P, 1))
    for x in range(P):
        if x % 64 < 16:
            f[x] = freq[x % 8]
            s[x] = -1 if x % 64 < 8 else 1
    put("freq", f)
    put("sign", s)
    return c


def axial_tables():
    out = np.zeros((P, 4, T), np.float32)
    t = np.arange(T)
    row, col = (t // 64).astype(np.float32), (t % 64).astype(np.float32)
    for n, dim in enumerate((64, 32)):
        nf = dim // 4
        inv = np.float32(10000.0) ** (-np.arange(nf, dtype=np.float32) / np.float32(nf))
        ang = np.concatenate([row[:, None] * inv, col[:, None] * inv], -1)
        for x in range(P):
            y = x % dim
            a = ang[:, y % (dim // 2)]
            out[x, 2 * n] = np.cos(a)
            out[x, 2 * n + 1] = np.sin(a) * (-1 if y < dim // 2 else 1)
    return out


def column_tiles(w):
    n = w.shape[1] // 256
    return w.reshape(DC, P, n, 256).transpose(2, 1, 0, 3).reshape(n, P, TILE)


def padded(w, width=256):
    return np.pad(w, ((0, 0), (0, width - w.shape[1])))


def up_tiles(gate, up):
    g, u = gate.reshape(D, FC, P), up.reshape(D, FC, P)
    return column_tiles(np.stack([g, u], 2).reshape(D, 2 * F))


def down_tiles(w):
    return w.reshape(2, FC // 2, P, DC, P).transpose(3, 0, 2, 1, 4).reshape(2 * DC, P, DOWN)


def weight_tiles(i):
    w, d = [], []
    for layer in range(4):
        if layer < 2:
            w.append(column_tiles(i["ada_w"][layer]))
            if layer == 0:
                a = i["attn_w_in"][0]
                w.append(column_tiles(np.concatenate([a[:, 0:1024], a[:, 1536:2560], a[:, 1024:1536], a[:, 2560:3072]], 1)))
                w.append(column_tiles(i["attn_w_out"][0]))
            else:
                a = i["gdn_w_in"][0]
                w.append(column_tiles(np.concatenate([a[:, 0:4096], padded(a[:, 4096:])], 1)))
                w.append(column_tiles(i["gdn_w_out"][0]))
            a = i["ffn_w_in"][layer]
            w.append(up_tiles(a[:, 0:F], a[:, F:]))
            d.append(down_tiles(i["ffn_w_out"][layer]))
        else:
            l = layer - 2
            w.append(column_tiles(i["w_ada_2"][l]))
            a = i["w_in_2"][l]
            qa, ka, va, ub, qc, kc, vc, qd, kd, vd = np.split(a, np.cumsum([256, 128, 128, 512, 256, 256, 256, 256, 256]), 1)
            qa = qa[:, np.r_[0:64, 128:192, 64:128, 192:256]]
            w.append(column_tiles(np.concatenate([ub, qa, qc, kc, qd, kd, padded(ka), vc, vd, padded(va)], 1)))
            w.append(column_tiles(i["w_out_2"][l]))
            w.append(up_tiles(i["w_gate_2"][l], i["w_up_2"][l]))
            d.append(down_tiles(i["w_down_2"][l]))
    return np.concatenate(w), np.concatenate(d)


def parameters(i):
    p = np.zeros((P, PARAM_W), np.float32)

    def put(name, v):
        a, w = PARAM[name]
        p[:v.shape[0], a:a + w] = v.reshape(v.shape[0], w)

    def cols(v):
        v = np.asarray(v)
        return v.reshape(-1, P).T
    put("c1", cols(i["c"]))
    put("c2", np.stack([cols(i["c_2"]), cols(i["c_ctx_2"])], 2))
    put("ada_b", np.concatenate([cols(i["ada_b"]), cols(i["b_ada_2"])], 1))
    put("mix_g", np.concatenate([cols(i["norm_mix_g"]), cols(i["norm1_g_2"])], 1))
    put("ffn_g", np.concatenate([cols(i["norm_ffn_g"]), cols(i["norm2_g_2"])], 1))
    put("fin_g", np.concatenate([cols(i["final_norm_g"]), cols(i["final_g_2"])], 1))
    put("gconv", cols(i["gdn_conv_w"][0]))
    put("gnorm", cols(i["gdn_norm_g"]))
    put("alog", np.broadcast_to(i["gdn_a_log"], (P, GH)))
    put("dtb", np.broadcast_to(i["gdn_dt_bias"], (P, GH)))
    put("sink", np.broadcast_to(i["attn_sink_2"].reshape(1, 8), (P, 8)))
    put("cw", i["conv_w_2"].reshape(2, 31, 2, P).transpose(3, 0, 2, 1))
    put("cb", cols(i["conv_b_2"]))
    put("lng", cols(i["conv_ln_g_2"]))
    put("lnb", cols(i["conv_ln_b_2"]))
    lq = np.stack([i["diff_lq1_2"], i["diff_lk1_2"], i["diff_lq2_2"], i["diff_lk2_2"]], 1)
    put("lq", np.broadcast_to(lq.reshape(1, 256), (P, 256)))
    put("subg", np.concatenate([i["diff_subln_g_2"].T, i["diff_subln_g_2"].T], 0))
    put("rpb", i["na_rpb_2"].transpose(3, 0, 1, 2))
    return p


def kernel(**inputs):
    import concourse.bacc as bacc
    from concourse.bass_utils import run_bass_kernel_spmd

    i = {name: np.asarray(v) for name, v in inputs.items()}
    w, d = weight_tiles(i)
    arrays = {
        "w_tiles": w, "d_tiles": d,
        "xT": np.ascontiguousarray(i["x"][0].T.reshape(DC, P, T).transpose(1, 0, 2)),
        "ctxT": np.ascontiguousarray(i["ctx_2"][0].T.reshape(DC, P, TC).transpose(1, 0, 2)),
        "positions": i["positions"], "consts": constants(), "params": parameters(i), "rope_tables": axial_tables(),
    }
    nc = bacc.Bacc("TRN2", target_bir_lowering=False, num_devices=1)
    args = [nc.dram_tensor(name, a.shape, mybir.dt.from_np(a.dtype), kind="ExternalInput").ap() for name, a in arrays.items()]
    args.append(nc.dram_tensor("outT", (P, DC, T), F32, kind="ExternalOutput").ap())
    build_program(nc, *args)
    r = run_bass_kernel_spmd(nc, [arrays], core_ids=[0])
    out = r.results[0]["outT"]
    return np.ascontiguousarray(out.transpose(1, 0, 2).reshape(1, D, T).transpose(0, 2, 1))
```

```python
from contextlib import ExitStack

import numpy as np
import concourse.bass as bass
from concourse import mybir

F32 = mybir.dt.float32
I32 = mybir.dt.int32
ALU = mybir.AluOpType
ACT = mybir.ActivationFunctionType
AX_X = mybir.AxisListType.X

P = 128
D = 1024
DC = D // P
T = 512
TC = 256
TA = T + TC
NT = T // P
F = 2816
FC = F // P
EPS = 1e-6
NEG = -1e30
ADA = 24
SLOTS = 4
TILE = DC * 256
DOWN = FC // 2 * P
GH = 8
GC = 24
TWO_PI = 2 * np.pi
PI_A, PI_B = 6.28125, 0.0019350051879882812
PI_C = TWO_PI - PI_A - PI_B
ROUND = 12582912.0

CONST = {}
_at = 0
for _name, _w in [("ident", P), ("ones", P), ("tri", P), ("negtri", P), ("negones", P), ("perm_a1", P),
                  ("perm_64", P), ("perm_32", P), ("causal", P), ("band_lo", P), ("band_hi", P),
                  ("level", 7 * P), ("onehot", P), ("colmask", 64), ("half64", P), ("freq", 1), ("sign", 1)]:
    CONST[_name] = (_at, _w)
    _at += _w
CONST_W = _at

PARAM = {}
_at = 0
for _name, _w in [("c1", DC), ("c2", 2 * DC), ("ada_b", 4 * 48), ("mix_g", 4 * DC), ("ffn_g", 4 * DC),
                  ("fin_g", 2 * DC), ("gconv", 4 * GC), ("gnorm", 1), ("alog", GH), ("dtb", GH),
                  ("sink", 2 * 4), ("cw", 2 * 2 * 31), ("cb", 2 * 2), ("lng", 2 * 2), ("lnb", 2 * 2),
                  ("lq", 2 * 4 * 32), ("subg", 2), ("rpb", 2 * 4 * 15)]:
    PARAM[_name] = (_at, _w)
    _at += _w
PARAM_W = _at


def linear_plan():
    plan = []
    for layer in range(4):
        if layer == 0:
            plan += [("ada0", "w", ADA // 2), ("attn_in", "w", ADA), ("attn_out", "w", 4)]
        elif layer == 1:
            plan += [("gdn_in", "w", 17), ("gdn_out", "w", 4)]
        else:
            plan += [(f"in{layer}", "w", 11), (f"out{layer}", "w", 4)]
        plan += [(f"up{layer}", "w", FC + (ADA if layer < 3 else 0)), (f"down{layer}", "d", 2 * DC)]
    return plan


def results(name, kind, n):
    if name == "ada0":
        return 0
    return n // 2 if kind == "d" or name == "attn_in" else FC if name.startswith("up") else n


def build_program(nc, w_tiles, d_tiles, xT, ctxT, positions, consts, params, rope_tables, outT):
    COUNT = {name: n for name, _, n in linear_plan()}
    G0, E0, at, read = {}, {}, 0, 8
    FROM = {}
    seen = {"w": 0, "d": 0}
    for name, kind, n in linear_plan():
        G0[name], FROM[name] = at, seen[kind]
        E0[name] = read
        at += n
        read += results(name, kind, n)
        seen[kind] += n

    ctx = ExitStack()
    with ctx:
        def sb(name, shape, dt=F32):
            return ctx.enter_context(nc.sbuf_tensor(name, shape, dt))

        def sem(name):
            return ctx.enter_context(nc.semaphore(name))

        ring = sb("ring", [P, SLOTS, TILE])
        X = sb("X", [P, DC, TA])
        H = sb("H", [P, DC, TA])
        BIG = sb("BIG", [P, FC * TA])
        WORK = sb("WORK", [P, 9216])
        CN = sb("CN", [P, CONST_W])
        PR = sb("PR", [P, PARAM_W])
        MOD = sb("MOD", [P, 2, 48, 2])
        GAIN = sb("GAIN", [P, 2, DC, 2])
        SC = sb("SC", [P, 3 * DC])
        SM = sb("SM", [P, 64])
        PS = ctx.enter_context(nc.psum_tensor("PS", [P, 4096], F32))

        def const(name):
            a, w = CONST[name]
            return CN[:, a:a + w]

        def par(name):
            a, w = PARAM[name]
            return PR[:, a:a + w]

        ident, ones = const("ident"), const("ones")

        loaded = sem("loaded")
        tile_loaded = [sem(f"tile_loaded{s}") for s in range(SLOTS)]
        tile_done = sem("tile_done")
        evac_done = sem("evac_done")
        phase_done = sem("phase_done")
        dve_chain = sem("dve_chain")
        act_chain = sem("act_chain")
        pool_chain = sem("pool_chain")
        stored = sem("stored")
        tables_loaded = sem("tables_loaded")
        scratch = {}

        def sig(name):
            if name not in scratch:
                scratch[name] = sem(name)
            return scratch[name]

        class Chain:

            def __init__(self, eng, s):
                self.eng, self.s, self.n = eng, s, 0

            def __call__(self, ins):
                ins.then_inc(self.s, 1)
                self.n = self.n + 1
                self.eng.wait_ge(self.s, self.n)

        def over_tiles(eng, n, body, chain=None, g0=0):
            rounds = n // SLOTS
            if rounds > 1:
                base = chain.n if chain else 0
                per = 0
                with eng.Fori(0, rounds) as i:
                    if chain:
                        per = body.steps * SLOTS
                        chain.n = i * per + base
                    for u in range(SLOTS):
                        body(i * SLOTS + u, u, i)
                if chain:
                    chain.n = base + per * rounds
            else:
                for i in range(rounds):
                    for u in range(SLOTS):
                        body(i * SLOTS + u, u, i)
            for u in range(n - rounds * SLOTS):
                body(rounds * SLOTS + u, u, rounds)

        def over_pairs(eng, n, first, second, chain=None, steps=0):
            base = chain.n if chain else 0
            with eng.Fori(0, n // 2) as i:
                if chain:
                    chain.n = i * (2 * steps) + base
                for v in range(2):
                    first(i * 2 + v, v, i)
                    second(i * 2 + v, v, i)
            if chain:
                chain.n = base + steps * n

        class Phase:
            def __init__(self):
                self.n = 0

            def end(self, eng):
                self.n += 1
                eng.drain().then_inc(phase_done, 1)
                eng.wait_ge(phase_done, 4 * self.n)

        BASE = {}

        def base(who, name, count):
            key = (who, name)
            at = BASE.get(key, 0)
            BASE[key] = at + count
            return at

        SEG1 = [(0, T)]
        SEG2 = [(0, T), (T, TC)]

        def wait_tile(pe, name, u, i):
            g = G0[name] + u
            pe.wait_ge(tile_loaded[g % SLOTS], (i + g // SLOTS + 1) * 16)
            return g % SLOTS

        def pe_feature_tiles(pe, name, src, segs, n, first=0, chunks=2, nb=None):
            e0 = E0[name] + first
            nb = nb or 4 // len(segs)
            W = 4096 // nb

            def body(t, u, i):
                slot = wait_tile(pe, name, u + first, i)
                pe.wait_ge(evac_done, t + (e0 - nb + 1))
                buf = (u + first) % nb
                for j in range(chunks):
                    for s, (c0, w) in enumerate(segs):
                        o = buf * W + j * W // 2 + s * 512
                        for k in range(DC):
                            mm = pe.matmul(PS[:, o:o + w], ring[:, slot, k * 256 + j * P:k * 256 + (j + 1) * P],
                                           src[:, k, c0:c0 + w], start=k == 0, stop=k == DC - 1)
                mm.then_inc(tile_done, 1)
            over_tiles(pe, n, body)

        def act_copy_tiles(act, name, dst, segs, n, first=0, chunks=2, nb=None):
            g0 = G0[name] + first
            nb = nb or 4 // len(segs)
            W = 4096 // nb
            width = sum(w for _, w in segs)

            def body(t, u, i):
                act.wait_ge(tile_done, t + (g0 + 1))
                buf = (u + first) % nb
                act.activation(dst[:, bass.ds((t + first) * 2, chunks), 0:width],
                               PS[:, buf * W:buf * W + W].rearrange("p (j c) -> p j c", j=2)[:, 0:chunks, 0:width],
                               ACT.Copy).then_inc(evac_done, 1)
            over_tiles(act, n, body)

        def pe_token_tiles(pe, name, tokens, n, first, cols=256, nb=4):
            e0 = E0[name] + first
            W = 4096 // nb
            for t in range(n):
                slot = wait_tile(pe, name, first + t, 0)
                pe.wait_ge(evac_done, e0 + t - nb + 1)
                o = (first + t) % nb * W
                for a in range(tokens // P):
                    for k in range(DC):
                        mm = pe.matmul(PS[:, o + a * 256:o + a * 256 + cols], H[:, k, a * P:(a + 1) * P],
                                       ring[:, slot, k * 256:k * 256 + cols], start=k == 0, stop=k == DC - 1)
                mm.then_inc(tile_done, 1)

        def act_token_tiles(act, name, dst, tokens, n, first, cols=256, nb=4, col0=0):
            g0 = G0[name] + first
            W = 4096 // nb
            A = tokens // P
            for t in range(n):
                act.wait_ge(tile_done, g0 + t + 1)
                o = (first + t) % nb * W
                act.activation(dst[:, :, col0 + t * 256:col0 + t * 256 + cols],
                               PS[:, o:o + A * 256].rearrange("p (a c) -> p a c", a=A)[:, :, 0:cols],
                               ACT.Copy).then_inc(evac_done, 1)

        def dve_residual_tiles(dve, name, gate, segs, n):
            g0 = G0[name]
            nb = 4 // len(segs)
            W = 4096 // nb

            def body(t, u, i):
                dve.wait_ge(tile_done, t + (g0 + 1))
                buf = u % nb
                for j in range(2):
                    for s, (c0, w) in enumerate(segs):
                        o = buf * W + j * W // 2 + s * 512
                        m = t * 2 + j
                        ins = dve.scalar_tensor_tensor(
                            out=X[:, bass.ds(m, 1), c0:c0 + w], in0=PS[:, o:o + w].rearrange("p (a c) -> p a c", a=1),
                            scalar=gate[:, bass.ds(m, 1), s], in1=X[:, bass.ds(m, 1), c0:c0 + w],
                            op0=ALU.mult, op1=ALU.add)
                ins.then_inc(evac_done, 1)
            over_tiles(dve, n, body)

        HID = BIG[:, :].rearrange("p (k t) -> p k t", k=FC)

        def pe_down(pe, name, segs):
            e0 = E0[name]

            def body(t, u, i):
                slot = wait_tile(pe, name, u, i)
                if u % 2 == 0:
                    pe.wait_ge(evac_done, i * 2 + (e0 + u // 2 - 1))
                buf = (u // 2) % 2
                for s, (c0, w) in enumerate(segs):
                    o = buf * 1024 + s * 512
                    for k in range(FC // 2):
                        kk = (u % 2) * (FC // 2) + k
                        mm = pe.matmul(PS[:, o:o + w], ring[:, slot, k * P:(k + 1) * P], HID[:, kk, c0:c0 + w],
                                       start=kk == 0, stop=kk == FC - 1, skip_group_check=True)
                mm.then_inc(tile_done, 1)
            over_tiles(pe, 2 * DC, body)

        def dve_down(dve, name, gate, segs):
            e0 = E0[name]
            g0 = G0[name]

            def body(t, u, i):
                if u % 2 == 0:
                    return
                dve.wait_ge(tile_done, t + (g0 + 1))
                buf = (u // 2) % 2
                m = i * 2 + u // 2
                for s, (c0, w) in enumerate(segs):
                    o = buf * 1024 + s * 512
                    ins = dve.scalar_tensor_tensor(
                        out=X[:, bass.ds(m, 1), c0:c0 + w], in0=PS[:, o:o + w].rearrange("p (a c) -> p a c", a=1),
                        scalar=gate[:, bass.ds(m, 1), s], in1=X[:, bass.ds(m, 1), c0:c0 + w],
                        op0=ALU.mult, op1=ALU.add)
                ins.then_inc(evac_done, 1)
            over_tiles(dve, 2 * DC, body)

        def up_columns(v, segs):
            if len(segs) == 1:
                return [v * 1024], [v * 1024 + 512]
            return [v * 1536, v * 1536 + 1024], [v * 1536 + 512, v * 1536 + 1280]

        def pe_up(pe, layer, segs):
            name = f"up{layer}"
            e0 = E0[name]

            def product(slot, m, v):
                pe.wait_ge(evac_done, m + (e0 - 1))
                for j, cols in enumerate(up_columns(v, segs)):
                    for o, (c0, w) in zip(cols, segs):
                        for k in range(DC):
                            mm = pe.matmul(PS[:, o:o + w], ring[:, slot, k * 256 + j * P:k * 256 + (j + 1) * P],
                                           H[:, k, c0:c0 + w], start=k == 0, stop=k == DC - 1)
                mm.then_inc(tile_done, 1)
            if layer == 3:
                over_tiles(pe, FC, lambda t, u, i: product(wait_tile(pe, name, u, i), t, u % 2))
                return
            over_pairs(pe, FC, lambda m, v, i: product(wait_tile(pe, name, 2 * v, i), m, v),
                       lambda m, v, i: pe_ada_tile(pe, layer + 1, m, v))
            for n in range(FC, ADA):
                pe_ada_tile(pe, layer + 1, n, n % 2)

        def act_up(act, layer, segs):
            g0, e0 = G0[f"up{layer}"], E0[f"up{layer}"]

            def silu(m, v, done):
                act.wait_ge(tile_done, done)
                act.wait_ge(evac_done, m + (e0 - 1))
                for o, (c0, w) in zip(up_columns(v, segs)[0], segs):
                    ins = act.activation(WORK[:, v * TA + c0:v * TA + c0 + w], PS[:, o:o + w], ACT.Silu)
                ins.then_inc(sig("gate_silu"), 1)
            if layer == 3:
                over_tiles(act, FC, lambda t, u, i: silu(t, u % 2, t + (g0 + 1)))
            else:
                over_pairs(act, FC, lambda m, v, i: silu(m, v, i * 4 + (g0 + 2 * v + 1)), lambda m, v, i: None)

        def dve_up(dve, layer, segs, chain):
            name = f"up{layer}"
            b = base("dve", "gate_silu", FC)

            def hidden(m, v):
                dve.wait_ge(sig("gate_silu"), m + (b + 1))
                for o, (c0, w) in zip(up_columns(v, segs)[1], segs):
                    ins = dve.tensor_tensor(HID[:, bass.ds(m, 1), c0:c0 + w],
                                            WORK[:, v * TA + c0:v * TA + c0 + w].rearrange("p (a c) -> p a c", a=1),
                                            PS[:, o:o + w].rearrange("p (a c) -> p a c", a=1), ALU.mult)
                ins.then_inc(evac_done, 1)
            if layer == 3:
                over_tiles(dve, FC, lambda t, u, i: hidden(t, u % 2))
                return
            over_pairs(dve, FC, lambda m, v, i: dve_ada_tile(dve, layer + 1, name, 2 * v + 1, i, v, chain),
                       lambda m, v, i: hidden(m, v), chain, ada_steps(layer + 1))
            for n in range(FC, ADA):
                dve_ada_tile(dve, layer + 1, name, FC + n, 0, n % 2, chain, apart=2)
            dve_ada_end(dve, layer + 1, name, chain)

        ACC = WORK[:, 3072:4096].rearrange("p (b v c) -> p b v c", b=2, v=2)
        ADA_PS = PS[:, 3072:3072 + 96].rearrange("p (n v) -> p n v", v=2)

        def vectors(layer):
            return [SC[:, 0:DC]] if layer < 2 else [SC[:, DC + v:3 * DC:2] for v in range(2)]

        def ada_steps(layer):
            return len(vectors(layer)) * DC - 1

        def dve_ada_tile(dve, layer, name, u, i, buf, chain, apart=4):
            g = G0[name] + u
            dve.wait_ge(tile_loaded[g % SLOTS], (i + g // SLOTS + 1) * 16)
            if g >= apart or not isinstance(i, int):
                dve.wait_ge(tile_done, i * SLOTS + (g - apart + 1))
            vs = vectors(layer)
            for v, c in enumerate(vs):
                for k in range(DC):
                    w, acc = ring[:, g % SLOTS, k * 256:(k + 1) * 256], ACC[:, buf, v, :]
                    if k == 0:
                        ins = dve.tensor_scalar(acc, w, c[:, 0:1], None, ALU.mult)
                    else:
                        ins = dve.scalar_tensor_tensor(out=acc, in0=w, scalar=c[:, k:k + 1], in1=acc,
                                                       op0=ALU.mult, op1=ALU.add)
                    if k < DC - 1 or v < len(vs) - 1:
                        chain(ins)
            ins.then_inc(sig("ada_weighted"), 1)

        def ada_base(layer):
            return layer * ADA

        def pe_ada_tile(pe, layer, n, buf):
            pe.wait_ge(sig("ada_weighted"), n + (ada_base(layer) + 1))
            for j in range(2):
                for v in range(len(vectors(layer))):
                    mm = pe.matmul(ADA_PS[:, bass.ds(n * 2 + j, 1), v], ACC[:, buf, v, j * P:(j + 1) * P], ones[:, 0:1],
                                   start=True, stop=True)
            mm.then_inc(tile_done, 1)

        def pe_ada0(pe):
            over_tiles(pe, ADA // 2, lambda t, u, i: pe_ada_tile(pe, 0, t, u % 2))

        def dve_ada0(dve, chain):
            def tile(u, i):
                dve_ada_tile(dve, 0, "ada0", u, i, u % 2, chain, apart=2)
            for u in range(SLOTS):
                tile(u, 0)
            base, per = chain.n, SLOTS * ada_steps(0)
            with dve.Fori(1, ADA // 2 // SLOTS) as i:
                chain.n = (i - 1) * per + base
                for u in range(SLOTS):
                    tile(u, i)
            chain.n = base + per * (ADA // 2 // SLOTS - 1)
            dve_ada_end(dve, 0, "ada0", chain, ADA // 2)

        def pe_attn_in(pe):
            e0 = E0["attn_in"]

            def features(m, v, i):
                slot = wait_tile(pe, "attn_in", 2 * v, i)
                pe.wait_ge(evac_done, m + (e0 - 1))
                for j in range(2):
                    o = v * 1024 + j * 512
                    for k in range(DC):
                        mm = pe.matmul(PS[:, o:o + T], ring[:, slot, k * 256 + j * P:k * 256 + (j + 1) * P],
                                       H[:, k, 0:T], start=k == 0, stop=k == DC - 1)
                mm.then_inc(tile_done, 1)
            over_pairs(pe, 8, features, lambda m, v, i: pe_ada_tile(pe, 0, m + ADA // 2, v))
            for m in range(8, 12):
                slot = wait_tile(pe, "attn_in", 2 * m, 0)
                pe.wait_ge(evac_done, e0 + m - 1)
                for a in range(NT):
                    o = (m % 2) * 1024 + a * 256
                    for k in range(DC):
                        mm = pe.matmul(PS[:, o:o + 256], H[:, k, a * P:(a + 1) * P], ring[:, slot, k * 256:(k + 1) * 256],
                                       start=k == 0, stop=k == DC - 1)
                mm.then_inc(tile_done, 1)
                pe_ada_tile(pe, 0, m + ADA // 2, m % 2)

        def act_attn_in(act):
            g0 = G0["attn_in"]

            def features(m, v, i):
                act.wait_ge(tile_done, i * 4 + (g0 + 2 * v + 1))
                act.activation(QK1[:, bass.ds(m * 2, 2), :],
                               PS[:, v * 1024:(v + 1) * 1024].rearrange("p (j c) -> p j c", j=2),
                               ACT.Copy).then_inc(evac_done, 1)
            over_pairs(act, 8, features, lambda m, v, i: None)
            for m in range(8, 12):
                act.wait_ge(tile_done, g0 + 2 * m + 1)
                act.activation(V1[:, :, (m - 8) * 256:(m - 7) * 256],
                               PS[:, (m % 2) * 1024:(m % 2 + 1) * 1024].rearrange("p (a c) -> p a c", a=NT),
                               ACT.Copy).then_inc(evac_done, 1)

        def dve_attn_in(dve, chain):
            over_pairs(dve, 12, lambda m, v, i: dve_ada_tile(dve, 0, "attn_in", 2 * v + 1, i, v, chain),
                       lambda m, v, i: None, chain, ada_steps(0))
            dve_ada_end(dve, 0, "attn_in", chain)

        def dve_ada_end(dve, layer, name, chain, tiles=ADA):
            mod = MOD[:, layer % 2, :, :]
            n = 2 * tiles
            dve.wait_ge(tile_done, G0[name] + COUNT[name])
            bias = par("ada_b").rearrange("p (l n) -> p l n", l=4)[:, layer, :]
            for v in range(len(vectors(layer))):
                chain(dve.tensor_tensor(mod[:, 0:n, v], ADA_PS[:, 0:n, v], bias[:, 0:n], ALU.add))
                for which, row in ((0, DC), (1, 4 * DC)):
                    if row < n:
                        g = par("mix_g" if which == 0 else "ffn_g").rearrange("p (l k) -> p l k", l=4)[:, layer, :]
                        dve.scalar_tensor_tensor(out=GAIN[:, which, :, v], in0=mod[:, row:row + DC, v], scalar=1.0,
                                                 in1=g, op0=ALU.add, op1=ALU.mult)

        SQ = [WORK[:, 0:TA], WORK[:, TA:2 * TA]]
        RSTD = WORK[:, 2 * TA:3 * TA]

        def act_norm(act, segs, chain, shift=None):
            width = sum(w for _, w in segs)
            b_mm = base("act", "norm_summed", DC)
            b_h = base("act", "norm_scaled", DC)
            for k in range(DC):
                if k >= 2:
                    act.wait_ge(sig("norm_summed"), b_mm + k - 1)
                act.activation(SQ[k % 2][:, 0:width], X[:, k, 0:width], ACT.Square).then_inc(sig("norm_squared"), 1)
            act.wait_ge(sig("norm_summed"), b_mm + DC)
            chain(act.activation(RSTD[:, 0:width], PS[:, 0:width], ACT.Ln, scale=1.0 / D, bias=SM[:, 0:1]))
            act.activation(RSTD[:, 0:width], RSTD[:, 0:width], ACT.Exp, scale=-0.5).then_inc(sig("norm_rstd"), 1)
            for k in range(DC):
                act.wait_ge(sig("norm_scaled"), b_h + k + 1)
                if shift is not None:
                    for s, (c0, w) in enumerate(segs):
                        act.activation(H[:, k, c0:c0 + w], H[:, k, c0:c0 + w], ACT.Identity, bias=shift[:, k, s:s + 1])

        def pe_norm(pe, segs):
            b = base("pe", "norm_squared", DC)
            for k in range(DC):
                pe.wait_ge(sig("norm_squared"), b + k + 1)
                for c0, w in segs:
                    mm = pe.matmul(PS[:, c0:c0 + w], ones, SQ[k % 2][:, c0:c0 + w], start=k == 0, stop=k == DC - 1)
                mm.then_inc(sig("norm_summed"), 1)

        def dve_norm(dve, segs, gain):
            b = base("dve", "norm_rstd", 1)
            dve.wait_ge(sig("norm_rstd"), b + 1)
            for k in range(DC):
                for s, (c0, w) in enumerate(segs):
                    ins = dve.scalar_tensor_tensor(out=H[:, k, c0:c0 + w], in0=X[:, k, c0:c0 + w],
                                                   scalar=gain[:, k, s:s + 1], in1=RSTD[:, c0:c0 + w],
                                                   op0=ALU.mult, op1=ALU.mult)
                ins.then_inc(sig("norm_scaled"), 1)

        S_SB = [WORK[:, n * TA:(n + 1) * TA] for n in (0, 1, 2, 3, 6, 7, 8, 9)]
        PT = [WORK[:, (4 + n) * TA:(5 + n) * TA] for n in range(2)]

        def map_list(jobs):
            return [(n, m) for n, job in enumerate(jobs) for m in range(len(job["q"]))]

        def small(n, s):
            return SM[:, 8 + n * 8 + s % 8:9 + n * 8 + s % 8]

        def attention_depth(jobs):
            return (8, 3) if len(jobs[0]["q"]) == 2 else (4, 2)

        def pe_attention(pe, jobs):
            bufs, ahead = attention_depth(jobs)
            maps = map_list(jobs)
            b_read = base("pe", "scores_read", len(maps))
            b_p = base("pe", "weights_ready", len(jobs))
            b_pt = base("pe", "turned_copied", len(jobs))
            b_o = base("pe", "heads_copied", len(jobs))

            def scores(s):
                n, m = maps[s]
                job = jobs[n]
                if s >= 2:
                    pe.wait_ge(sig("scores_read"), b_read + s - 1)
                for o, k in job["k"][m]:
                    a = (s % 2) * 1024 + o
                    mm = pe.matmul(PS[:, a:a + k.shape[-1]], job["q"][m], k, start=True, stop=True)
                mm.then_inc(sig("scores_ready"), 1)

            def turn(n):
                s = max(x for x, (j, _) in enumerate(maps) if j == n)
                pe.wait_ge(sig("weights_ready"), b_p + n + 1)
                if n >= 1:
                    pe.wait_ge(sig("turned_copied"), b_pt + n)
                for x in range(len(jobs[n]["v"])):
                    mm = pe.transpose(PS[:, 2048 + x * P:2048 + (x + 1) * P], S_SB[s % bufs][:, x * P:(x + 1) * P], ident)
                mm.then_inc(sig("turned"), 1)

            def outputs(n):
                job = jobs[n]
                pe.wait_ge(sig("turned_copied"), b_pt + n + 1)
                if n >= 2:
                    pe.wait_ge(sig("heads_copied"), b_o + n - 1)
                off = job["off"]
                o = 3072 + (n % 2) * 512
                for x, v in enumerate(job["v"]):
                    mm = pe.matmul(PS[off:off + 64, o:o + P], v, PT[n % 2][:, x * P:(x + 1) * P],
                                   start=x == 0, stop=x == len(job["v"]) - 1)
                mm.then_inc(sig("heads_ready"), 1)

            per = len(jobs[0]["q"])
            made = 0
            for n in range(len(jobs)):
                for s in range(made, min((n + 1) * per + ahead + 1, len(maps))):
                    scores(s)
                    made = s + 1
                if n >= 1:
                    outputs(n - 1)
                turn(n)
            outputs(len(jobs) - 1)

        def dve_attention(dve, jobs, chain):
            maps = map_list(jobs)
            b_s = base("dve", "scores_ready", len(maps))
            b_t = base("dve", "turned", len(jobs))
            b_e = base("dve", "exps_ready", len(maps))
            bufs, ahead = attention_depth(jobs)

            def score_part(s):
                n, m = maps[s]
                job = jobs[n]
                per = len(job["q"])
                nk = len(job["v"]) * P
                S = S_SB[s % bufs]
                dve.wait_ge(sig("scores_ready"), b_s + s + 1)
                if s >= bufs:
                    dve.wait_ge(sig("turned"), b_t + (s - bufs) // per + 1)
                pieces = job["pieces"]
                for x, (o, p0, w, mask) in enumerate(pieces):
                    src = PS[:, (s % 2) * 1024 + p0:(s % 2) * 1024 + p0 + w]
                    if mask is None:
                        ins = dve.tensor_scalar(S[:, o:o + w], src, job["scale"], None, ALU.mult)
                    else:
                        ins = dve.scalar_tensor_tensor(out=S[:, o:o + w], in0=src, scalar=job["scale"], in1=mask,
                                                       op0=ALU.mult, op1=ALU.add)
                    if x < len(pieces) - 1:
                        chain(ins)
                ins.then_inc(sig("scores_read"), 1)
                dve.wait_ge(sig("scores_read"), b_read + s + 1)
                if job["sink"] is None:
                    dve.tensor_reduce(small(0, s), S[:, 0:nk], AX_X, ALU.max,
                                      negate=True).then_inc(sig("max_ready"), 1)
                else:
                    chain(dve.tensor_reduce(small(0, s), S[:, 0:nk], AX_X, ALU.max, negate=True))
                    dve.scalar_tensor_tensor(out=small(0, s), in0=job["sink"], scalar=-1.0,
                                             in1=small(0, s), op0=ALU.mult,
                                             op1=ALU.min).then_inc(sig("max_ready"), 1)

            def weight_part(s):
                n, m = maps[s]
                job = jobs[n]
                nk = len(job["v"]) * P
                S = S_SB[s % bufs]
                dve.wait_ge(sig("exps_ready"), b_e + s + 1)
                total, inv = small(1, s), small(2, s)
                if job["sink"] is not None:
                    chain(dve.tensor_tensor(total, total, small(3, s), ALU.add))
                chain(dve.reciprocal(inv, total))
                if m == 1:
                    chain(dve.tensor_scalar(inv, inv, job["neg_lam"], None, ALU.mult))
                    dve.scalar_tensor_tensor(out=S[:, 0:nk], in0=S[:, 0:nk], scalar=inv,
                                             in1=S_SB[(s - 1) % bufs][:, 0:nk], op0=ALU.mult,
                                             op1=ALU.add).then_inc(sig("weights_ready"), 1)
                elif len(job["q"]) == 2:
                    chain(dve.tensor_scalar(S[:, 0:nk], S[:, 0:nk], inv, None, ALU.mult))
                else:
                    dve.tensor_scalar(S[:, 0:nk], S[:, 0:nk], inv, None, ALU.mult).then_inc(sig("weights_ready"), 1)

            b_read = base("dve", "scores_read", len(maps))
            for s in range(ahead):
                score_part(s)
            for s in range(len(maps)):
                if s + ahead < len(maps):
                    score_part(s + ahead)
                weight_part(s)

        def act_attention(act, jobs, chain):
            maps = map_list(jobs)
            b_m = base("act", "max_ready", len(maps))
            b_t = base("act", "turned", len(jobs))
            b_h = base("act", "heads_ready", len(jobs))
            bufs, _ = attention_depth(jobs)

            def exps(s):
                n, m = maps[s]
                job = jobs[n]
                nk = len(job["v"]) * P
                S = S_SB[s % bufs]
                act.wait_ge(sig("max_ready"), b_m + s + 1)
                if job["sink"] is not None:
                    chain(act.activation(small(3, s), job["sink"], ACT.Exp, bias=small(0, s)))
                act.activation(S[:, 0:nk], S[:, 0:nk], ACT.Exp, bias=small(0, s),
                               accum_out=small(1, s)).then_inc(sig("exps_ready"), 1)

            def copy_turned(n):
                act.wait_ge(sig("turned"), b_t + n + 1)
                if n >= 2:
                    act.wait_ge(sig("heads_ready"), b_h + n - 1)
                nk = len(jobs[n]["v"]) * P
                act.activation(PT[n % 2][:, 0:nk], PS[:, 2048:2048 + nk], ACT.Copy).then_inc(sig("turned_copied"), 1)

            def copy_heads(n):
                act.wait_ge(sig("heads_ready"), b_h + n + 1)
                job = jobs[n]
                off = job["off"]
                o = 3072 + (n % 2) * 512
                act.activation(job["out"], PS[off:off + 64, o:o + P], ACT.Copy).then_inc(sig("heads_copied"), 1)

            per = len(jobs[0]["q"])
            for s in range(per):
                exps(s)
            for n in range(len(jobs)):
                if n + 1 < len(jobs):
                    for s in range((n + 1) * per, (n + 2) * per):
                        exps(s)
                copy_turned(n)
                if n >= 1:
                    copy_heads(n - 1)
            copy_heads(len(jobs) - 1)

        def pe_rope(pe, chunks):
            b = base("pe", "rotated", len(chunks))
            for n, (c, perm, _, _) in enumerate(chunks):
                if n >= 4:
                    pe.wait_ge(sig("rotated"), b + n - 3)
                pe.matmul(PS[:, (n % 4) * 512:(n % 4) * 512 + T], perm, c, start=True, stop=True).then_inc(sig("swapped"), 1)

        def dve_rope(dve, chunks, chain):
            b = base("dve", "swapped", len(chunks))
            for n, (c, _, cos, sin) in enumerate(chunks):
                dve.wait_ge(sig("swapped"), b + n + 1)
                tmp = ROPE_TMP[:, (n % 2) * T:(n % 2) * T + T]
                dve.tensor_tensor(tmp, PS[:, (n % 4) * 512:(n % 4) * 512 + T], sin, ALU.mult)
                chain(dve.tensor_tensor(c, c, cos, ALU.mult))
                dve.tensor_tensor(c, c, tmp, ALU.add).then_inc(sig("rotated"), 1)

        ROPE_TMP = WORK[:, 8192:9216]

        QK1 = BIG[:, 0:16 * T].rearrange("p (k t) -> p k t", k=16)
        V1 = BIG[:, 16 * T:24 * T].rearrange("p (a c) -> p a c", a=NT)
        COS1, SIN1 = WORK[:, 0:T], WORK[:, T:2 * T]
        POS = WORK[:, 5 * T:6 * T]
        TMP1, TMP2 = WORK[:, 3 * T:4 * T], WORK[:, 4 * T:5 * T]

        def dve_angles(dve, chain):
            dve.wait_ge(tables_loaded, 16)
            chain(dve.tensor_copy(POS, POS.bitcast(I32)))
            chain(dve.tensor_scalar(POS, POS, const("freq"), None, ALU.mult))
            for dst, ahead in ((COS1, 0.25), (SIN1, 0.0)):
                chain(dve.tensor_scalar(TMP1, POS, 1 / TWO_PI, ahead, ALU.mult, ALU.add))
                chain(dve.tensor_scalar(TMP1, TMP1, ROUND, ROUND, ALU.add, ALU.subtract))
                chain(dve.scalar_tensor_tensor(out=dst, in0=TMP1, scalar=-PI_A, in1=POS, op0=ALU.mult, op1=ALU.add))
                chain(dve.scalar_tensor_tensor(out=dst, in0=TMP1, scalar=-PI_B, in1=dst, op0=ALU.mult, op1=ALU.add))
                chain(dve.scalar_tensor_tensor(out=dst, in0=TMP1, scalar=-PI_C, in1=dst, op0=ALU.mult, op1=ALU.add))
                if ahead:
                    chain(dve.tensor_scalar(dst, dst, np.pi / 2, None, ALU.add))
                ins = dve.tensor_scalar(dst, dst, 3.1415925, -3.1415925, ALU.min, ALU.max)
                if ahead:
                    chain(ins)
            ins.then_inc(sig("angles_ready"), 1)

        def causal_jobs():
            jobs = []
            for h in range(8):
                r = slice((h % 2) * 64, (h % 2) * 64 + 64)
                for i in range(NT):
                    pieces = [(0, 0, i * P, None)] if i else []
                    pieces.append((i * P, i * P, P, const("causal")))
                    jobs.append(dict(q=[QK1[r, h // 2, i * P:(i + 1) * P]],
                                     k=[[(0, QK1[r, 4 + h // 2, 0:(i + 1) * P])]],
                                     v=[V1[:, a, h * 64:(h + 1) * 64] for a in range(i + 1)],
                                     pieces=pieces, scale=0.125, sink=None, off=(h % 2) * 64,
                                     out=H[r, h // 2, i * P:(i + 1) * P]))
            return jobs

        OFFS = [0, 512, 1024, 896]
        SBW = 1280
        SP_ = [WORK[:, n * SBW:(n + 1) * SBW] for n in range(2)]
        SW = [WORK[:, (2 + n) * SBW:(3 + n) * SBW] for n in range(2)]

        def sb_bank(h, i):
            return (h % 2) * 1536 + OFFS[i]

        def pe_stick(pe):
            def z(h):
                if h >= 2:
                    pe.wait_ge(sig("sticks_read"), h - 1)
                r = slice((h % 2) * 64, (h % 2) * 64 + 64)
                for i in (0, 1, 3, 2):
                    a, w = sb_bank(h, i), T - i * P
                    mm = pe.matmul(PS[:, a:a + w], QK1[r, 12 + h // 2, i * P:(i + 1) * P],
                                   QK1[r, 8 + h // 2, i * P:T], start=i != 3, stop=True, skip_group_check=True)
                mm.then_inc(sig("z_ready"), 1)

            def sums(h):
                pe.wait_ge(sig("softplus_masked"), h + 1)
                for i in (0, 1, 3, 2):
                    for j in range(i, NT):
                        a = sb_bank(h, i) + (j - i) * P
                        w = T - j * P
                        mm = pe.matmul(PS[:, a:a + w], const("negtri") if j == i else const("negones"),
                                       SP_[h % 2][:, OFFS[j]:OFFS[j] + w], start=False, stop=True, skip_group_check=True)
                mm.then_inc(sig("sticks_ready"), 1)

            def outputs(h):
                pe.wait_ge(sig("sticks_masked"), h + 1)
                if h >= 2:
                    pe.wait_ge(sig("stick_heads_copied"), h - 1)
                off = (h % 2) * 64
                for i in range(NT):
                    o = 3072 + (h % 2) * 512
                    mm = pe.matmul(PS[off:off + 64, o + i * P:o + T], V1[:, i, 512 + h * 64:512 + (h + 1) * 64],
                                   SW[h % 2][:, OFFS[i]:OFFS[i] + T - i * P], start=i == 0, stop=i == NT - 1,
                                   skip_group_check=True)
                mm.then_inc(sig("stick_heads_ready"), 1)

            z(0)
            for h in range(8):
                if h + 1 < 8:
                    z(h + 1)
                sums(h)
                if h >= 1:
                    outputs(h - 1)
            outputs(7)

        def act_stick(act, chain):
            def softplus(h):
                act.wait_ge(sig("z_ready"), h + 1)
                if h >= 2:
                    act.wait_ge(sig("sticks_ready"), h - 1)
                L, a = SP_[h % 2], (h % 2) * 1536
                chain(act.activation(L, PS[:, a:a + SBW], ACT.Abs))
                chain(act.activation(L, L, ACT.Exp, scale=-1.0))
                act.activation(L, L, ACT.Ln, bias=SM[:, 1:2]).then_inc(sig("log_ready"), 1)

            def weights(h):
                act.wait_ge(sig("sticks_ready"), h + 1)
                if h >= 2:
                    act.wait_ge(sig("stick_heads_ready"), h - 1)
                a = (h % 2) * 1536
                act.activation(SW[h % 2], PS[:, a:a + SBW], ACT.Exp).then_inc(sig("sticks_read"), 1)

            def copy(h):
                off = (h % 2) * 64
                act.wait_ge(sig("stick_heads_ready"), h + 1)
                act.activation(H[off:off + 64, 4 + h // 2, 0:T], PS[off:off + 64, 3072 + (h % 2) * 512:3072 + (h % 2) * 512 + T],
                               ACT.Copy).then_inc(sig("stick_heads_copied"), 1)

            softplus(0)
            for h in range(8):
                if h + 1 < 8:
                    softplus(h + 1)
                weights(h)
                if h >= 1:
                    copy(h - 1)
            copy(7)

        def dve_stick(dve):
            for h in range(8):
                dve.wait_ge(sig("log_ready"), h + 1)
                a = (h % 2) * 1536
                dve.scalar_tensor_tensor(out=SP_[h % 2], in0=PS[:, a:a + SBW], scalar=0.0, in1=SP_[h % 2],
                                         op0=ALU.max, op1=ALU.add).then_inc(sig("softplus_ready"), 1)

        def pool_stick(pool):
            def keep_past(buf):
                for i in range(NT):
                    v = buf[:, OFFS[i]:OFFS[i] + P]
                    ins = pool.affine_select(out=v, in_=v, compare_op=ALU.is_gt, fill=0.0, base=0,
                                             pattern=[[1, P]], channel_multiplier=-1)
                return ins
            def soft(h):
                pool.wait_ge(sig("softplus_ready"), h + 1)
                keep_past(SP_[h % 2]).then_inc(sig("softplus_masked"), 1)
            soft(0)
            for h in range(8):
                if h + 1 < 8:
                    soft(h + 1)
                pool.wait_ge(sig("sticks_read"), h + 1)
                keep_past(SW[h % 2]).then_inc(sig("sticks_masked"), 1)
        def rope1_chunks():
            return [(QK1[:, x, :], const("perm_a1"), COS1, SIN1) for x in range(8)]

        FIN_G = [par("fin_g").rearrange("p (l k v) -> p l k v", l=2, v=1)[:, n, :, :] for n in range(2)]
        GQ = BIG[:, 0:32 * T].rearrange("p (k t) -> p k t", k=32)
        CONV_IN = [WORK[:, n * 1030:n * 1030 + 1030].rearrange("p (j t) -> p j t", j=2) for n in range(2)]
        CONV_OUT = [WORK[:, 2080 + n * 1024:3104 + n * 1024] for n in range(2)]
        HF = H[:, :, :].rearrange("p k t -> p (k t)")
        KTOK = HF[:, 0:8 * T].rearrange("p (h c d) -> p h c d", h=GH, c=NT)
        VTOK = BIG[:, 16 * T:24 * T].rearrange("p (h c d) -> p h c d", h=GH, c=NT)
        GS0 = 4096 + 4 * P + 1024
        AB = HF[:, GS0:GS0 + 64].rearrange("p (c n) -> p c n", c=NT)

        def gate_vec(n):
            return HF[:, GS0 + 64 + 32 * n:GS0 + 96 + 32 * n]
        GRAW, BETA, GCUM, NCOEF, EG, EKD, EGL, GTMP = [gate_vec(n) for n in range(8)]
        STATE = HF[:, 4096:4096 + 4 * P].rearrange("p (h e) -> p h e", h=4)
        VNEW = HF[:, 4096 + 4 * P:4096 + 8 * P]
        QEXP = HF[:, 4096 + 8 * P:4096 + 12 * P]
        SEL = lambda v, c, h: v[:, c * GH + h:c * GH + h + 1]

        def act_gdn_in(act, chain):
            g0, e0 = G0["gdn_in"], E0["gdn_in"]
            b = base("act", "convolved", 12)

            def body(t, u, i):
                act.wait_ge(tile_done, t + (g0 + 1))
                act.wait_ge(sig("convolved"), t + (b + 7))
                act.activation(CONV_IN[u % 2][:, :, 3:3 + T], PS[:, (u % 4) * 1024:(u % 4 + 1) * 1024]
                               .rearrange("p (j c) -> p j c", j=2), ACT.Copy).then_inc(evac_done, 1)
                act.wait_ge(sig("convolved"), t + (b + 9))
                act.activation(GQ[:, bass.ds(t * 2, 2), :], CONV_OUT[u % 2].rearrange("p (j c) -> p j c", j=2),
                               ACT.Silu).then_inc(sig("conv_silu"), 1)
            act.drain().then_inc(sig("conv_silu"), 2)
            over_tiles(act, 12, body)
            for t in range(4):
                act.wait_ge(tile_done, g0 + 12 + t + 1)
                act.activation(GQ[:, 24 + 2 * t:26 + 2 * t, :], PS[:, t * 1024:(t + 1) * 1024]
                               .rearrange("p (j c) -> p j c", j=2), ACT.Silu).then_inc(evac_done, 1)
            act.wait_ge(tile_done, g0 + 17)
            act.activation(AB, PS[:, 0:64].rearrange("p (c n) -> p c n", c=NT), ACT.Copy).then_inc(evac_done, 1)

        def dve_gdn_in(dve, chain):
            e0 = E0["gdn_in"]
            b = 2
            dve.memset(CONV_IN[0][:, :, 0:3], 0.0)
            dve.memset(CONV_IN[1][:, :, 0:3], 0.0).then_inc(sig("convolved"), 8)
            dve.wait_ge(sig("convolved"), 8)
            w = par("gconv").rearrange("p (k n) -> p k n", k=4)

            def body(t, u, i):
                dve.wait_ge(evac_done, t + (e0 + 1))
                src = CONV_IN[u % 2]
                y2 = CONV_OUT[u % 2].rearrange("p (j c) -> p j c", j=2)
                dve.wait_ge(sig("conv_silu"), t + (b - 1))
                for tap in range(4):
                    for j in range(2):
                        y = y2[:, j:j + 1, :]
                        x = src[:, j:j + 1, tap:tap + T]
                        s = w[:, tap, bass.ds(t * 2 + j, 1)]
                        if tap == 0:
                            ins = dve.tensor_scalar(y, x, s, None, ALU.mult)
                        else:
                            ins = dve.scalar_tensor_tensor(out=y, in0=x, scalar=s, in1=y, op0=ALU.mult, op1=ALU.add)
                    if tap < 3:
                        chain(ins)
                    else:
                        ins.then_inc(sig("convolved"), 1)
            body.steps = 3
            over_tiles(dve, 12, body, chain)

        def pe_gdn_in(pe):
            pe_feature_tiles(pe, "gdn_in", H, SEG1, 12)
            pe_feature_tiles(pe, "gdn_in", H, SEG1, 4, first=12)
            slot = wait_tile(pe, "gdn_in", 16, 0)
            pe.wait_ge(evac_done, E0["gdn_in"] + 13)
            for a in range(NT):
                for k in range(DC):
                    mm = pe.matmul(PS[:, a * 16:a * 16 + 16], H[:, k, a * P:(a + 1) * P], ring[:, slot, k * 256:k * 256 + 16],
                                   start=k == 0, stop=k == DC - 1)
            mm.then_inc(tile_done, 1)

        def act_gdn_prep(act, chain):
            for n in range(16):
                act.wait_ge(sig("l2_summed"), n + 1)
                if n >= 2:
                    act.wait_ge(sig("l2_scaled"), n - 1)
                R = WORK[:, (2 + n % 2) * T:(3 + n % 2) * T]
                s = float(P) if n < 8 else 1.0
                chain(act.activation(R, PS[:, (n % 2) * 512:(n % 2) * 512 + T], ACT.Ln, scale=s,
                                     bias=SM[:, 2:3] if n < 8 else SM[:, 0:1]))
                act.activation(R, R, ACT.Exp, scale=-0.5).then_inc(sig("l2_rstd"), 1)
            act.wait_ge(sig("dt_added"), 1)
            a = AB[:, :, 0:GH]
            t3 = GTMP.rearrange("p (c n) -> p c n", c=NT)
            chain(act.activation(t3, a, ACT.Abs))
            chain(act.activation(GTMP, GTMP, ACT.Exp, scale=-1.0))
            chain(act.activation(GTMP, GTMP, ACT.Ln, bias=SM[:, 1:2]))
            act.activation(BETA.rearrange("p (c n) -> p c n", c=NT), AB[:, :, GH:2 * GH], ACT.Exp, scale=-1.0)
            act.activation(SM[:, 24:32], par("alog"), ACT.Exp).then_inc(sig("gate_parts"), 1)
            act.wait_ge(sig("gcum_ready"), 1)
            act.activation(EG, GCUM, ACT.Exp)
            act.activation(EKD, GTMP, ACT.Exp)
            act.activation(EGL, PS[:, 2048 + 32:2048 + 64], ACT.Exp).then_inc(sig("gate_exps"), 1)

        def pool_gdn_prep(pool):
            for n in range(16):
                if n >= 2:
                    pool.wait_ge(sig("l2_summed"), n - 1)
                pool.tensor_tensor(WORK[:, (n % 2) * T:(n % 2 + 1) * T], GQ[:, n, :], GQ[:, n, :],
                                   ALU.mult).then_inc(sig("l2_squared"), 1)

        def pe_gdn_prep(pe):
            for n in range(16):
                pe.wait_ge(sig("l2_squared"), n + 1)
                if n >= 2:
                    pe.wait_ge(sig("l2_rstd"), n - 1)
                pe.matmul(PS[:, (n % 2) * 512:(n % 2) * 512 + T], ones, WORK[:, (n % 2) * T:(n % 2 + 1) * T],
                          start=True, stop=True).then_inc(sig("l2_summed"), 1)
            pe.wait_ge(sig("graw_ready"), 1)
            pe.matmul(PS[:, 2048:2048 + 32], const("tri"), GRAW, start=True, stop=True)
            pe.matmul(PS[:, 2048 + 32:2048 + 64], ones, GRAW, start=True, stop=True).then_inc(sig("gsums_ready"), 1)
            for n in range(16):
                h = n % 8
                if n < 8:
                    pe.wait_ge(sig("l2_scaled"), 9 + h)
                if n >= 2:
                    pe.wait_ge(sig("tokens_copied"), n - 1)
                for c in range(NT):
                    mm = pe.transpose(PS[:, 1024 + (n % 2) * 512 + c * P:1024 + (n % 2) * 512 + (c + 1) * P],
                                      GQ[:, 8 + n, c * P:(c + 1) * P], ident)
                mm.then_inc(sig("tokens_turned"), 1)

        def dve_gdn_prep(dve, chain):
            a = AB[:, :, 0:GH]
            for c in range(NT):
                ins = dve.tensor_tensor(AB[:, c, 0:GH], AB[:, c, 0:GH], par("dtb"), ALU.add)
            ins.then_inc(sig("dt_added"), 1)
            for n in range(16):
                dve.wait_ge(sig("l2_rstd"), n + 1)
                dve.tensor_tensor(GQ[:, n, :], GQ[:, n, :], WORK[:, (2 + n % 2) * T:(3 + n % 2) * T],
                                  ALU.mult).then_inc(sig("l2_scaled"), 1)
            dve.wait_ge(sig("gate_parts"), 1)
            t3 = GTMP.rearrange("p (c n) -> p c n", c=NT)
            chain(dve.scalar_tensor_tensor(out=t3, in0=a, scalar=0.0, in1=t3, op0=ALU.max, op1=ALU.add))
            for c in range(NT):
                ins = dve.scalar_tensor_tensor(out=GRAW[:, c * GH:(c + 1) * GH], in0=GTMP[:, c * GH:(c + 1) * GH],
                                               scalar=-1.0, in1=SM[:, 24:32], op0=ALU.mult, op1=ALU.mult)
            ins.then_inc(sig("graw_ready"), 1)
            chain(dve.tensor_scalar(BETA, BETA, 1.0, None, ALU.add))
            chain(dve.reciprocal(BETA, BETA))
            dve.wait_ge(sig("gsums_ready"), 1)
            chain(dve.tensor_copy(GCUM, PS[:, 2048:2048 + 32]))
            dve.scalar_tensor_tensor(out=GTMP, in0=GCUM, scalar=-1.0, in1=PS[:, 2048 + 32:2048 + 64], op0=ALU.mult,
                                     op1=ALU.add).then_inc(sig("gcum_ready"), 1)
            dve.wait_ge(sig("gate_exps"), 1)
            dve.scalar_tensor_tensor(out=NCOEF, in0=EG, scalar=-1.0, in1=BETA, op0=ALU.mult, op1=ALU.mult)
            for n in range(16):
                h = n % 8
                dve.wait_ge(sig("tokens_turned"), n + 1)
                src = PS[:, 1024 + (n % 2) * 512:1024 + (n % 2) * 512 + T].rearrange("p (c d) -> p c d", c=NT)
                dst, by = (KTOK, EKD) if n < 8 else (VTOK, BETA)
                for c in range(NT):
                    ins = dve.tensor_scalar(dst[:, h, c, :], src[:, c, :], SEL(by, c, h), None, ALU.mult)
                ins.then_inc(sig("tokens_copied"), 1)

        def gbuf(par_, n):
            o = 4096 + par_ * 2560 + n * T
            return WORK[:, o:o + T]
        XT = [WORK[:, n * T:(n + 1) * T] for n in range(4)]
        AT = [WORK[:, (4 + n) * T:(5 + n) * T] for n in range(4)]
        LEVELS = 7

        def gps(q, n, c=None):
            o = (q * 3 + n) * 512
            return PS[:, o:o + T] if c is None else PS[:, o + c * P:o + (c + 1) * P]

        def blk(v, c):
            return v[:, c * P:(c + 1) * P]

        def pe_gdn_inverse(pe, grp):
            kT = lambda h, c: GQ[:, 8 + h, c * P:(c + 1) * P]
            for n in range(0, 4, 2):
                for q in range(2):
                    h = grp * 4 + n + q
                    N = grp * 4 + n + q
                    pe.wait_ge(sig("tri_scaled"), N + 1)
                    if N >= 2:
                        pe.wait_ge(sig("inverse_step" + str(q)), (N // 2) * LEVELS)
                    pe.matmul(gps(q, 0), ones, gbuf(q, 4), start=True, stop=True)
                    for c in range(NT):
                        pe.matmul(gps(q, 1, c), kT(h, c), kT(h, c), start=True, stop=True)
                    for c in range(NT):
                        mm = pe.matmul(gps(q, 2, c), kT(h, c), GQ[:, h, c * P:(c + 1) * P], start=True, stop=True)
                    mm.then_inc(sig("products_ready"), 1)
                for q in range(2):
                    N = grp * 4 + n + q
                    pe.wait_ge(sig("level_masked" + str(q)), (N // 2) * LEVELS + 1)
                    for c in range(NT):
                        mm = pe.transpose(gps(q, 0, c), blk(gbuf(q, 1), c), ident)
                    mm.then_inc(sig("m0_turned"), 1)
                for lv in range(1, LEVELS):
                    for q in range(2):
                        N = grp * 4 + n + q
                        X_, T_, V_, M_ = XT[n + q], gbuf(q, 3), gbuf(q, 4), gbuf(q, 1 + lv % 2)
                        pe.wait_ge(sig("inverse_step" + str(q)), (N // 2) * LEVELS + lv)
                        pe.wait_ge(sig("level_masked" + str(q)), (N // 2) * LEVELS + lv + 1)
                        for c in range(NT):
                            mm = pe.matmul(gps(q, 0, c), blk(M_, c), blk(X_, c), start=True, stop=True)
                        mm.then_inc(sig("mx_ready" + str(q)), 1)
                    for q in range(2):
                        N = grp * 4 + n + q
                        X_, T_, V_ = XT[n + q], gbuf(q, 3), gbuf(q, 4)
                        pe.wait_ge(sig("mx_copied" + str(q)), (N // 2) * (LEVELS - 1) + lv)
                        for c in range(NT):
                            mm = pe.matmul(gps(q, 1, c), blk(T_, c), blk(V_, c), start=True, stop=True)
                        if lv < LEVELS - 1:
                            for c in range(NT):
                                mm = pe.matmul(gps(q, 2, c), blk(V_, c), blk(T_, c), start=True, stop=True)
                        mm.then_inc(sig("update_ready" + str(q)), 1)

        def dve_gdn_inverse(dve, grp, chain):
            for n in range(0, 4, 2):
                for q in range(2):
                    h = N = grp * 4 + n + q
                    if N >= 2:
                        dve.wait_ge(sig("update_ready" + str(q)), (N // 2) * (LEVELS - 1))
                    for c in range(NT):
                        ins = dve.tensor_scalar(blk(gbuf(q, 4), c), const("tri"), SEL(GRAW, c, h), None, ALU.mult)
                    ins.then_inc(sig("tri_scaled"), 1)
                for q in range(2):
                    h = N = grp * 4 + n + q
                    dve.wait_ge(sig("products_ready"), N + 1)
                    if N >= 2:
                        dve.wait_ge(sig("level_masked" + str(q)), (N // 2) * LEVELS)
                    for c in range(NT):
                        dve.tensor_scalar(blk(AT[n + q], c), gps(q, 0, c), SEL(GCUM, c, h), 0.0, ALU.subtract, ALU.min)
                        ins = dve.tensor_scalar(blk(gbuf(q, 0), c), gps(q, 0, c), SEL(GCUM, c, h), 0.0, ALU.subtract, ALU.max)
                    ins.then_inc(sig("gaps_ready"), 1)
                for q in range(2):
                    h = N = grp * 4 + n + q
                    dve.wait_ge(sig("decay_masked"), N + 1)
                    dve.tensor_tensor(AT[n + q], AT[n + q], gps(q, 2), ALU.mult)
                    for c in range(NT):
                        ins = dve.scalar_tensor_tensor(out=blk(gbuf(q, 0), c), in0=gps(q, 1, c), scalar=SEL(BETA, c, h),
                                                       in1=blk(gbuf(q, 0), c), op0=ALU.mult, op1=ALU.mult)
                    ins.then_inc(sig("lower_ready"), 1)
                for q in range(2):
                    N = grp * 4 + n + q
                    dve.wait_ge(sig("level_masked" + str(q)), (N // 2) * LEVELS + 1)
                    dve.wait_ge(sig("m0_turned"), N + 1)
                    for c in range(NT):
                        dve.tensor_tensor(blk(gbuf(q, 3), c), ident, blk(gbuf(q, 1), c), ALU.subtract)
                        ins = dve.tensor_tensor(blk(XT[n + q], c), ident, gps(q, 0, c), ALU.subtract)
                    ins.then_inc(sig("inverse_step" + str(q)), 1)
                for lv in range(1, LEVELS):
                    for q in range(2):
                        N = grp * 4 + n + q
                        dve.wait_ge(sig("update_ready" + str(q)), (N // 2) * (LEVELS - 1) + lv)
                        dve.wait_ge(sig("inverse_step" + str(q)), (N // 2) * LEVELS + lv)
                        if lv < LEVELS - 1:
                            dve.tensor_tensor(gbuf(q, 3), gbuf(q, 3), gps(q, 2), ALU.subtract)
                        dve.tensor_tensor(XT[n + q], XT[n + q], gps(q, 1), ALU.subtract).then_inc(sig("inverse_step" + str(q)), 1)

        def act_gdn_inverse(act, grp, chain):
            for n in range(0, 4, 2):
                for q in range(2):
                    N = grp * 4 + n + q
                    act.wait_ge(sig("gaps_ready"), N + 1)
                    act.activation(AT[n + q], AT[n + q], ACT.Exp)
                    act.activation(gbuf(q, 0), gbuf(q, 0), ACT.Exp, scale=-1.0).then_inc(sig("decay_ready"), 1)
                for lv in range(1, LEVELS):
                    for q in range(2):
                        N = grp * 4 + n + q
                        act.wait_ge(sig("mx_ready" + str(q)), (N // 2) * (LEVELS - 1) + lv)
                        act.activation(gbuf(q, 4), gps(q, 0), ACT.Copy).then_inc(sig("mx_copied" + str(q)), 1)

        def pool_gdn_inverse(pool, grp):
            for n in range(0, 4, 2):
                for q in range(2):
                    N = grp * 4 + n + q
                    pool.wait_ge(sig("decay_ready"), N + 1)
                    a3 = AT[n + q].rearrange("p (c s) -> p c s", c=NT)
                    l3 = gbuf(q, 0).rearrange("p (c s) -> p c s", c=NT)
                    pool.affine_select(out=a3, in_=a3, compare_op=ALU.is_ge, fill=0.0, base=0,
                                       pattern=[[0, NT], [1, P]], channel_multiplier=-1)
                    pool.affine_select(out=l3, in_=l3, compare_op=ALU.is_gt, fill=0.0, base=0,
                                       pattern=[[0, NT], [-1, P]], channel_multiplier=1).then_inc(sig("decay_masked"), 1)
                for lv in range(LEVELS):
                    mask = const("level")[:, lv * P:(lv + 1) * P]
                    for q in range(2):
                        N = grp * 4 + n + q
                        if lv == 0:
                            pool.wait_ge(sig("lower_ready"), N + 1)
                        if lv == 2:
                            pool.wait_ge(sig("inverse_step" + str(q)), (N // 2) * LEVELS + 1)
                        if lv > 2:
                            pool.wait_ge(sig("mx_ready" + str(q)), (N // 2) * (LEVELS - 1) + lv - 2)
                        for c in range(NT):
                            ins = pool.tensor_tensor(blk(gbuf(q, 1 + lv % 2), c), blk(gbuf(q, 0), c), mask, ALU.mult)
                        ins.then_inc(sig("level_masked" + str(q)), 1)
        def bank4(n, h=None):
            return PS[:, n * 512:n * 512 + 512] if h is None else PS[:, n * 512 + h * P:n * 512 + (h + 1) * P]

        def hs(v, h):
            return v[:, h * P:(h + 1) * P]
        RHS = [WORK[:, 8192:8704], WORK[:, 8704:9216]]

        def pe_scan(pe, grp):
            for c in range(NT):
                n = grp * NT + c
                ns = grp * (NT - 1) + c
                kT = lambda h: GQ[:, 8 + grp * 4 + h, c * P:(c + 1) * P]
                qT = lambda h: GQ[:, grp * 4 + h, c * P:(c + 1) * P]
                if c:
                    pe.wait_ge(sig("state_ready"), ns)
                    for h in range(4):
                        pe.matmul(bank4(0, h), kT(h), STATE[:, h, :], start=True, stop=True)
                    for h in range(4):
                        mm = pe.matmul(bank4(1, h), qT(h), STATE[:, h, :], start=True, stop=True)
                    mm.then_inc(sig("from_state"), 1)
                    pe.wait_ge(sig("rhs_ready"), ns)
                for h in range(4):
                    rhs = hs(RHS[0], h) if c else VTOK[:, grp * 4 + h, c, :]
                    mm = pe.matmul(bank4(2, h), blk(XT[h], c), rhs, start=True, stop=True)
                mm.then_inc(sig("vnew_ready"), 1)
                pe.wait_ge(sig("vnew_copied"), n + 1)
                if c < NT - 1:
                    for h in range(4):
                        mm = pe.matmul(bank4(3, h), KTOK[:, grp * 4 + h, c, :], hs(VNEW, h), start=True, stop=True)
                    mm.then_inc(sig("state_sums"), 1)
                if n:
                    pe.wait_ge(sig("out_stored"), n)
                for h in range(4):
                    mm = pe.matmul(bank4(4, h), blk(AT[h], c), hs(VNEW, h), start=True, stop=True)
                mm.then_inc(sig("out_ready"), 1)

        def dve_scan(dve, grp):
            for c in range(NT):
                n = grp * NT + c
                ns = grp * (NT - 1) + c
                if c:
                    dve.wait_ge(sig("from_state"), ns)
                    for h in range(4):
                        ins = dve.scalar_tensor_tensor(out=hs(RHS[0], h), in0=bank4(0, h), scalar=SEL(NCOEF, c, grp * 4 + h),
                                                       in1=VTOK[:, grp * 4 + h, c, :], op0=ALU.mult, op1=ALU.add)
                    ins.then_inc(sig("rhs_ready"), 1)
                if c < NT - 1:
                    dve.wait_ge(sig("state_sums"), ns + 1)
                    for h in range(4):
                        if c:
                            ins = dve.scalar_tensor_tensor(out=STATE[:, h, :], in0=STATE[:, h, :],
                                                           scalar=SEL(EGL, c, grp * 4 + h), in1=bank4(3, h),
                                                           op0=ALU.mult, op1=ALU.add)
                        else:
                            ins = dve.tensor_copy(STATE[:, h, :], bank4(3, h))
                    ins.then_inc(sig("state_ready"), 1)
                    dve.wait_ge(sig("state_ready"), ns + 1)
                dve.wait_ge(sig("out_ready"), n + 1)
                out = VTOK[:, grp * 4:grp * 4 + 4, c, :]
                o = bank4(4).rearrange("p (h e) -> p h e", h=4)
                if c:
                    dve.wait_ge(sig("q_state_scaled"), ns)
                    ins = dve.tensor_tensor(out, QEXP.rearrange("p (h e) -> p h e", h=4), o, ALU.add)
                else:
                    ins = dve.tensor_copy(out, o)
                ins.then_inc(sig("out_stored"), 1)

        def act_scan(act, grp):
            for c in range(NT):
                n = grp * NT + c
                ns = grp * (NT - 1) + c
                if c:
                    act.wait_ge(sig("from_state"), ns)
                    act.wait_ge(sig("out_stored"), n)
                    for h in range(4):
                        ins = act.activation(hs(QEXP, h), bank4(1, h), ACT.Copy, scale=SEL(EG, c, grp * 4 + h))
                    ins.then_inc(sig("q_state_scaled"), 1)
                act.wait_ge(sig("vnew_ready"), n + 1)
                if n:
                    act.wait_ge(sig("out_ready"), n)
                act.activation(VNEW, bank4(2), ACT.Copy).then_inc(sig("vnew_copied"), 1)

        OSQ = [WORK[:, (2 + n) * T:(3 + n) * T] for n in range(2)]

        def act_gdn_out(act, chain):
            for h in range(GH):
                if h >= 2:
                    act.wait_ge(sig("o_normed"), h - 1)
                act.activation(OSQ[h % 2].rearrange("p (c e) -> p c e", c=NT), VTOK[:, h, :, :],
                               ACT.Square).then_inc(sig("o_squared"), 1)
                act.wait_ge(sig("o_summed"), h + 1)
                r = SM[:, 32 + (h % 2) * 4:36 + (h % 2) * 4]
                chain(act.activation(r, r, ACT.Ln, scale=1.0 / P, bias=SM[:, 0:1]))
                act.activation(r, r, ACT.Exp, scale=-0.5).then_inc(sig("o_rstd"), 1)

        def dve_gdn_out(dve, chain):
            for h in range(GH):
                dve.wait_ge(sig("o_squared"), h + 1)
                r = SM[:, 32 + (h % 2) * 4:36 + (h % 2) * 4]
                dve.tensor_reduce(r, OSQ[h % 2].rearrange("p (c e) -> p c e", c=NT), AX_X, ALU.add).then_inc(sig("o_summed"), 1)
                dve.wait_ge(sig("o_rstd"), h + 1)
                for c in range(NT):
                    ins = dve.tensor_scalar(VTOK[:, h, c, :], VTOK[:, h, c, :], r[:, c:c + 1], None, ALU.mult)
                ins.then_inc(sig("o_normed"), 1)
                dve.wait_ge(sig("o_turned"), h + 1)
                dve.scalar_tensor_tensor(out=H[:, h, 0:T], in0=PS[:, (h % 2) * 512:(h % 2) * 512 + T], scalar=par("gnorm"),
                                         in1=GQ[:, 24 + h, :], op0=ALU.mult, op1=ALU.mult).then_inc(sig("gated"), 1)

        def pe_gdn_out(pe):
            for h in range(GH):
                pe.wait_ge(sig("o_normed"), h + 1)
                for c in range(NT):
                    mm = pe.transpose(PS[:, (h % 2) * 512 + c * P:(h % 2) * 512 + (c + 1) * P], VTOK[:, h, c, :], ident)
                mm.then_inc(sig("o_turned"), 1)

        Q2 = BIG[:, 0:15 * TA].rearrange("p (k t) -> p k t", k=15)
        V2 = BIG[:, 15 * TA:15 * TA + 6 * 640].rearrange("p (a c) -> p a c", a=6)
        UB, UG, QA, QC, KC, QD, KD, KA = 0, 2, 4, 6, 8, 10, 12, 14
        GW = 15 + T + 15 + 15 + TC + 15
        GLU = WORK[:, 0:2 * GW].rearrange("p (j t) -> p j t", j=2)
        YW = GW - 30
        YC = WORK[:, 2 * GW:2 * GW + 2 * YW].rearrange("p (j t) -> p j t", j=2)
        GE = WORK[:, 3300:3300 + 2 * TA].rearrange("p (j t) -> p j t", j=2)
        CTX0 = T + 30
        LAST = 3

        def in_tiles(layer):
            q = SEG1 if layer == LAST else SEG2
            return [(0, 4, 2, q), (4, 1, 2, SEG2), (5, 1, 2, q), (6, 1, 2, SEG2), (7, 1, 1, SEG2)]

        def pe_in(pe, layer):
            for first, n, chunks, segs in in_tiles(layer):
                pe_feature_tiles(pe, f"in{layer}", H, segs, n, first, chunks, nb=2)
            pe_token_tiles(pe, f"in{layer}", TA, 2, 8, nb=2)
            pe_token_tiles(pe, f"in{layer}", TA, 1, 10, cols=P, nb=2)

        def act_in(act, layer):
            for first, n, chunks, segs in in_tiles(layer):
                if first == 0:
                    act_copy_tiles(act, f"in{layer}", Q2, segs, 2, 0, chunks, nb=2)
                    act.wait_ge(evac_done, E0[f"in{layer}"] + 2)
                    w = sum(x for _, x in segs)
                    act.activation(GE[:, :, 0:w], Q2[:, UG:UG + 2, 0:w], ACT.Sigmoid).then_inc(sig("glu_gate"), 1)
                    act_copy_tiles(act, f"in{layer}", Q2, segs, 2, 2, chunks, nb=2)
                else:
                    act_copy_tiles(act, f"in{layer}", Q2, segs, n, first, chunks, nb=2)
            act_token_tiles(act, f"in{layer}", V2, TA, 2, 8, nb=2)
            act_token_tiles(act, f"in{layer}", V2, TA, 1, 10, cols=P, nb=2, col0=512)

        def dve_in(dve, layer, chain):
            l = layer - 2
            segs = SEG1 if layer == LAST else SEG2
            w = sum(x for _, x in segs)
            chain(dve.memset(WORK[:, 0:2 * GW], 0.0))
            b = base("dve", "glu_gate", 1)
            dve.wait_ge(sig("glu_gate"), b + 1)
            for (c0, x), o in zip(segs, (15, T + 45)):
                ins = dve.tensor_tensor(GLU[:, :, o:o + x], Q2[:, UB:UB + 2, c0:c0 + x], GE[:, :, c0:c0 + x], ALU.mult)
            chain(ins)
            cw = par("cw").rearrange("p (l j k) -> p l j k", l=2, j=2)
            cb = par("cb").rearrange("p (l j) -> p l j", l=2)
            yw = T if layer == LAST else YW
            for tap in range(31):
                for j in range(2):
                    y, x = YC[:, j, 0:yw], GLU[:, j, tap:tap + yw]
                    if tap == 0:
                        ins = dve.tensor_scalar(y, x, cw[:, l, j, 0:1], cb[:, l, j:j + 1], ALU.mult, ALU.add)
                    else:
                        ins = dve.scalar_tensor_tensor(out=y, in0=x, scalar=cw[:, l, j, tap:tap + 1], in1=y,
                                                       op0=ALU.mult, op1=ALU.add)
                chain(ins)

        YSQ = WORK[:, 3300:3300 + 2 * TA].rearrange("p (j t) -> p j t", j=2)
        YR = WORK[:, 4900:4900 + TA]
        TAB = WORK[:, 5700:5700 + 4 * T].rearrange("p (n t) -> p n t", n=4)

        def yseg(layer):
            return [(0, 0, T)] if layer == LAST else [(0, 0, T), (CTX0, T, TC)]

        def rope2_chunks():
            return [(Q2[:, x, 0:T], const("perm_64"), TAB[:, 0, :], TAB[:, 1, :]) for x in (QA, QA + 1, KA)] + \
                   [(Q2[:, x, 0:T], const("perm_32"), TAB[:, 2, :], TAB[:, 3, :]) for x in (QC, QC + 1, KC, KC + 1)]

        def pe_conv_norm(pe, layer):
            b = base("pe", "centered", 1)
            b2 = base("pe", "y_squared", 1)
            for y0, o, w in yseg(layer):
                for j in range(2):
                    mm = pe.matmul(PS[:, 2048 + o:2048 + o + w], ones, YC[:, j, y0:y0 + w], start=j == 0, stop=j == 1)
            mm.then_inc(sig("y_summed"), 1)
            pe_rope(pe, rope2_chunks())
            pe.wait_ge(sig("y_squared"), b2 + 1)
            for y0, o, w in yseg(layer):
                for j in range(2):
                    mm = pe.matmul(PS[:, 3072 + o:3072 + o + w], ones, YSQ[:, j, o:o + w], start=j == 0, stop=j == 1)
            mm.then_inc(sig("y_squares_summed"), 1)

        def act_conv_norm(act, layer, chain):
            b = base("act", "centered", 1)
            bs = base("act", "y_squares_summed", 1)
            bn = base("act", "y_normed", 1)
            act.wait_ge(sig("centered"), b + 1)
            for y0, o, w in yseg(layer):
                ins = act.activation(YSQ[:, :, o:o + w], YC[:, :, y0:y0 + w], ACT.Square)
            ins.then_inc(sig("y_squared"), 1)
            act.wait_ge(sig("y_squares_summed"), bs + 1)
            w = T if layer == LAST else TA
            chain(act.activation(YR[:, 0:w], PS[:, 3072:3072 + w], ACT.Ln, scale=1.0 / 256, bias=SM[:, 0:1]))
            act.activation(YR[:, 0:w], YR[:, 0:w], ACT.Exp, scale=-0.5).then_inc(sig("y_rstd"), 1)
            act.wait_ge(sig("y_normed"), bn + 1)
            act.activation(H[:, 2:4, 0:w], H[:, 2:4, 0:w], ACT.Silu)

        def dve_conv_norm(dve, layer, chain):
            l = layer - 2
            b1 = base("dve", "y_summed", 1)
            b2 = base("dve", "y_rstd", 1)
            bt = base("dve", "tables_loaded", 16)
            dve.wait_ge(sig("y_summed"), b1 + 1)
            for y0, o, w in yseg(layer):
                for j in range(2):
                    ins = dve.scalar_tensor_tensor(out=YC[:, j, y0:y0 + w], in0=PS[:, 2048 + o:2048 + o + w],
                                                   scalar=-1.0 / 256, in1=YC[:, j, y0:y0 + w], op0=ALU.mult, op1=ALU.add)
            ins.then_inc(sig("centered"), 1)
            dve.wait_ge(tables_loaded, 16 + bt + 16)
            dve_rope(dve, rope2_chunks(), chain)
            dve.wait_ge(sig("y_rstd"), b2 + 1)
            g = par("lng").rearrange("p (l j) -> p l j", l=2)
            be = par("lnb").rearrange("p (l j) -> p l j", l=2)
            for y0, o, w in yseg(layer):
                for j in range(2):
                    ins = dve.tensor_tensor(H[:, 2 + j, o:o + w], YC[:, j, y0:y0 + w], YR[:, o:o + w], ALU.mult)
            chain(ins)
            w = T if layer == LAST else TA
            for j in range(2):
                ins = dve.tensor_scalar(H[:, 2 + j, 0:w], H[:, 2 + j, 0:w], g[:, l, j:j + 1], be[:, l, j:j + 1],
                                        ALU.mult, ALU.add)
            ins.then_inc(sig("y_normed"), 1)
            lq = par("lq").rearrange("p (l n d) -> p l n d", l=2, n=4)
            for m in range(2):
                dve.tensor_tensor(LTMP[:, m, :], lq[:, l, 2 * m, :], lq[:, l, 2 * m + 1, :], ALU.mult)
            chain(dve.memset(SM[:, 42:43], 0.0))
            dve.tensor_reduce(SM[:, 40:42], LTMP, AX_X, ALU.add).then_inc(sig("lam_sums"), 1)
            bl = base("dve", "lam_exps", 1)
            dve.wait_ge(sig("lam_exps"), bl + 1)
            chain(dve.tensor_tensor(SM[:, 42:43], SM[:, 41:42], SM[:, 40:41], ALU.subtract))
            dve.tensor_scalar(SM[:, 42:43], SM[:, 42:43], -lambda_init(l), None, ALU.add)

        LTMP = WORK[:, 7800:7864].rearrange("p (m d) -> p m d", m=2)

        def lambda_init(l):
            return 0.8 - 0.6 * float(np.exp(-0.3 * l))

        def act_lambda(act):
            b = base("act", "lam_sums", 1)
            act.wait_ge(sig("lam_sums"), b + 1)
            act.activation(SM[:, 40:42], SM[:, 40:42], ACT.Exp).then_inc(sig("lam_exps"), 1)

        SLOTN = 14
        BT = WORK[:, 6 * TA:6 * TA + 4 * SLOTN * 64].rearrange("p (h s c) -> p h s c", h=4, s=SLOTN)

        def pe_bias(pe, l):
            rpb = par("rpb").rearrange("p (l h r) -> p l h r", l=2, h=4)
            hot = const("onehot")
            for rnd in range(8):
                for cc in range(8):
                    c = rnd * 8 + cc
                    for p in range(2):
                        o = rnd * 512 + cc * 56
                        mm = pe.matmul(PS[p * 64:p * 64 + 64, o:o + 4 * SLOTN].rearrange("p (h s) -> p h s", h=4),
                                       hot[0:31, 63 - c:127 - c], rpb[0:31, l, :, 1 - p:15 - p], start=True, stop=True)
                mm.then_inc(sig("bias_ready"), 1)

        def dve_bias(dve, l):
            b = base("dve", "bias_ready", 8)
            for rnd in range(8):
                dve.wait_ge(sig("bias_ready"), b + rnd + 1)
                src = PS[:, rnd * 512:rnd * 512 + 448].rearrange("p (c h s) -> p h s c", c=8, h=4)
                mask = const("colmask")[:, rnd * 8:rnd * 8 + 8]
                for h in range(4):
                    dve.tensor_tensor(BT[:, h, :, rnd * 8:rnd * 8 + 8], src[:, h, :, :],
                                      mask.rearrange("p (a c) -> p a c", a=1).to_broadcast([P, SLOTN, 8]), ALU.add)

        def mixer_jobs(layer):
            l = layer - 2
            singles, doubles = [], []
            sinks = par("sink").rearrange("p (l h) -> p l h", l=2)
            qtiles = range(NT if layer == LAST else TA // P)
            for h in range(4):
                g = h // 2
                r = slice(g * 64, g * 64 + 64)
                out_r = slice((h % 2) * 64, (h % 2) * 64 + 64)
                vs = lambda a: V2[:, a, 512 + g * 64:512 + g * 64 + 64]
                for i in qtiles:
                    q = Q2[r, QA + h % 2, i * P:(i + 1) * P]
                    if i < NT:
                        lo, hi = max(i - 1, 0), min(i + 1, NT - 1)
                        n1 = (hi - lo + 1) * P
                        ks = [(0, Q2[r, KA, lo * P:(hi + 1) * P]), (512, Q2[r, KA, T:TA])]
                        pieces = []
                        for x, blk_ in enumerate(range(lo, hi + 1)):
                            m = const("band_lo") if blk_ < i else const("band_hi") if blk_ > i else None
                            pieces.append((x * P, x * P, P, m))
                        pieces.append((n1, 512, TC, None))
                        v = [vs(a) for a in range(lo, hi + 1)] + [vs(4), vs(5)]
                    else:
                        ks = [(0, Q2[r, KA, T:TA])]
                        pieces = [(0, 0, TC, None)]
                        v = [vs(4), vs(5)]
                    singles.append(dict(q=[q], k=[ks], v=v, pieces=pieces, scale=0.125, sink=sinks[:, l, h:h + 1],
                                        off=(h % 2) * 64, out=H[out_r, h // 2, i * P:(i + 1) * P]))
            for h in range(4):
                r = slice((h % 2) * 64, (h % 2) * 64 + 64)
                vs = lambda a: V2[:, a, 256 + h * 64:256 + h * 64 + 64]
                for i in qtiles:
                    q = Q2[r, QD + h // 2, i * P:(i + 1) * P]
                    kv = lambda a, b: Q2[r, KD + h // 2, a:b]
                    if i < NT:
                        ks = [(0, kv(0, T)), (512, kv(T, TA))]
                        bias = BT[:, h, 6 - 2 * i:14 - 2 * i, :].rearrange("p s c -> p (s c)")
                        pieces = [(0, 0, T, bias), (T, 512, TC, None)]
                        v = [vs(a) for a in range(6)]
                    else:
                        ks, pieces, v = [(0, kv(T, TA))], [(0, 0, TC, None)], [vs(4), vs(5)]
                    singles.append(dict(q=[q], k=[ks], v=v, pieces=pieces, scale=0.125, sink=None,
                                        off=(h % 2) * 64, out=H[r, 6 + h // 2, i * P:(i + 1) * P]))
            for h in range(4):
                vs = lambda a: V2[:, a, h * 64:h * 64 + 64]
                for i in qtiles:
                    qs, ks = [], []
                    for m in range(2):
                        r = slice((h % 2) * 64 + m * 32, (h % 2) * 64 + m * 32 + 32)
                        qs.append(Q2[r, QC + h // 2, i * P:(i + 1) * P])
                        kv = lambda a, b: Q2[r, KC + h // 2, a:b]
                        ks.append([(0, kv(0, T)), (512, kv(T, TA))] if i < NT else [(0, kv(T, TA))])
                    full = i < NT
                    r = slice((h % 2) * 64, (h % 2) * 64 + 64)
                    doubles.append(dict(q=qs, k=ks, v=[vs(a) for a in (range(6) if full else (4, 5))],
                                        pieces=[(0, 0, TA if full else TC, None)], scale=32 ** -0.5, sink=None,
                                        neg_lam=SM[:, 42:43], off=(h % 2) * 64, out=H[r, 4 + h // 2, i * P:(i + 1) * P]))
            return singles, doubles

        def act_sub_norm(act, layer, chain):
            w = T if layer == LAST else TA
            b = base("act", "heads_summed", 2)
            for n in range(2):
                act.activation(WORK[:, n * TA:n * TA + w], H[:, 4 + n, 0:w], ACT.Square).then_inc(sig("heads_squared"), 1)
            for n in range(2):
                act.wait_ge(sig("heads_summed"), b + n + 1)
                R = WORK[:, (2 + n) * TA:(2 + n) * TA + w]
                chain(act.activation(R, PS[:, n * 1024:n * 1024 + w], ACT.Ln, scale=1.0 / 64, bias=SM[:, 0:1]))
                act.activation(R, R, ACT.Exp, scale=-0.5).then_inc(sig("heads_rstd"), 1)

        def pe_sub_norm(pe, layer):
            b = base("pe", "heads_squared", 2)
            for n in range(2):
                pe.wait_ge(sig("heads_squared"), b + n + 1)
                for c0, w in SEG1 if layer == LAST else SEG2:
                    mm = pe.matmul(PS[:, n * 1024 + c0:n * 1024 + c0 + w], const("half64"), WORK[:, n * TA + c0:n * TA + c0 + w],
                                   start=True, stop=True)
                mm.then_inc(sig("heads_summed"), 1)

        def dve_sub_norm(dve, layer, chain):
            l = layer - 2
            w = T if layer == LAST else TA
            b = base("dve", "heads_rstd", 2)
            chain(dve.tensor_scalar(SM[:, 43:44], par("subg")[:, l:l + 1], 1.0 - lambda_init(l), None, ALU.mult))
            for n in range(2):
                dve.wait_ge(sig("heads_rstd"), b + n + 1)
                dve.scalar_tensor_tensor(out=H[:, 4 + n, 0:w], in0=H[:, 4 + n, 0:w], scalar=SM[:, 43:44],
                                         in1=WORK[:, (2 + n) * TA:(2 + n) * TA + w], op0=ALU.mult, op1=ALU.mult)
        block = ctx.enter_context(nc.Block())

        @block.sync
        def _(sp):
            sp.dma_start(PR[:, :], params).then_inc(loaded, 16)
            sp.dma_start(CN[:, :], consts).then_inc(loaded, 16)
            sp.dma_start(X[:, :, 0:T], xT).then_inc(loaded, 16)
            sp.dma_start(X[:, :, T:TA], ctxT).then_inc(loaded, 16)
            sp.dma_start(POS.bitcast(I32), positions.to_broadcast([P, T])).then_inc(tables_loaded, 16)
            for name, kind, n in linear_plan():
                src, width = (w_tiles, TILE) if kind == "w" else (d_tiles, DOWN)

                def load(t, u, i, name=name, src=src, width=width):
                    g = G0[name] + u
                    if G0[name] + u >= SLOTS or not isinstance(i, int) or i > 0:
                        sp.wait_ge(tile_done, t + (G0[name] - SLOTS + 1))
                    at = t + FROM[name]
                    sp.dma_start(ring[:, g % SLOTS:g % SLOTS + 1, 0:width],
                                 src[bass.ds(at, 1), :, :].rearrange("a p c -> p a c")).then_inc(tile_loaded[g % SLOTS], 16)
                if G0[name] == 0:
                    for u in range(SLOTS):
                        load(u, u, 0)
                    rounds = n // SLOTS
                    with sp.Fori(1, rounds) as i:
                        for u in range(SLOTS):
                            load(i * SLOTS + u, u, i)
                else:
                    over_tiles(sp, n, load)
            sp.wait_ge(sig("out_normed"), 1)
            sp.dma_start(outT, H[:, :, 0:T]).then_inc(stored, 16)
            sp.wait_ge(stored, 16)

        @block.tensor
        def _(pe):
            ph = Phase()
            pe.wait_ge(loaded, 64)
            ph.end(pe)
            for layer in range(4):
                segs = SEG1 if layer < 2 or layer == LAST else SEG2
                if layer == 0:
                    pe_ada0(pe)
                    ph.end(pe)
                pe_norm(pe, SEG2 if layer >= 2 else SEG1)
                ph.end(pe)
                if layer == 0:
                    pe_attn_in(pe)
                    ph.end(pe)
                    pe_rope(pe, rope1_chunks())
                    ph.end(pe)
                    pe_attention(pe, causal_jobs())
                    ph.end(pe)
                    pe_stick(pe)
                    ph.end(pe)
                    pe_feature_tiles(pe, "attn_out", H, SEG1, 4)
                elif layer == 1:
                    pe_gdn_in(pe)
                    ph.end(pe)
                    pe_gdn_prep(pe)
                    ph.end(pe)
                    for grp in range(2):
                        pe_gdn_inverse(pe, grp)
                        ph.end(pe)
                        pe_scan(pe, grp)
                        ph.end(pe)
                    pe_gdn_out(pe)
                    ph.end(pe)
                    pe_feature_tiles(pe, "gdn_out", H, SEG1, 4)
                else:
                    pe_in(pe, layer)
                    ph.end(pe)
                    pe_conv_norm(pe, layer)
                    ph.end(pe)
                    pe_bias(pe, layer - 2)
                    ph.end(pe)
                    singles, doubles = mixer_jobs(layer)
                    pe_attention(pe, singles)
                    ph.end(pe)
                    pe_attention(pe, doubles)
                    ph.end(pe)
                    pe_sub_norm(pe, layer)
                    ph.end(pe)
                    pe_feature_tiles(pe, f"out{layer}", H, segs, 4)
                ph.end(pe)
                pe_norm(pe, segs)
                ph.end(pe)
                pe_up(pe, layer, segs)
                ph.end(pe)
                pe_down(pe, f"down{layer}", segs)
                ph.end(pe)
                if layer in (1, 3):
                    pe_norm(pe, SEG1)
                    ph.end(pe)

        @block.scalar
        def _(act):
            ph = Phase()
            chain = Chain(act, act_chain)
            act.wait_ge(loaded, 64)
            act.activation(SC[:, :], PR[:, 0:3 * DC], ACT.Exp, scale=-1.0).then_inc(sig("c_exp"), 1)
            act.drain().then_inc(evac_done, 8)
            ph.end(act)
            for layer in range(4):
                segs = SEG1 if layer < 2 or layer == LAST else SEG2
                if layer == 0:
                    ph.end(act)
                mod = MOD[:, layer % 2, :, :]
                act_norm(act, SEG2 if layer >= 2 else SEG1, chain, mod[:, 0:DC, :])
                ph.end(act)
                if layer == 0:
                    act_attn_in(act)
                    ph.end(act)
                    act.wait_ge(sig("angles_ready"), 1)
                    act.activation(QK1[:, 8:12, :], QK1[:, 8:12, :], ACT.Copy, scale=0.125)
                    chain(act.activation(COS1, COS1, ACT.Sin))
                    chain(act.activation(SIN1, SIN1, ACT.Sin))
                    act.activation(SIN1, SIN1, ACT.Copy, scale=const("sign")).then_inc(sig("angles_done"), 1)
                    ph.end(act)
                    act_attention(act, causal_jobs(), chain)
                    ph.end(act)
                    act_stick(act, chain)
                    ph.end(act)
                elif layer == 1:
                    act_gdn_in(act, chain)
                    ph.end(act)
                    act_gdn_prep(act, chain)
                    ph.end(act)
                    for grp in range(2):
                        act_gdn_inverse(act, grp, chain)
                        ph.end(act)
                        act_scan(act, grp)
                        ph.end(act)
                    act_gdn_out(act, chain)
                    ph.end(act)
                else:
                    act_in(act, layer)
                    ph.end(act)
                    act.dma_start(TAB, rope_tables).then_inc(tables_loaded, 16)
                    act_conv_norm(act, layer, chain)
                    act_lambda(act)
                    ph.end(act)
                    ph.end(act)
                    singles, doubles = mixer_jobs(layer)
                    act_attention(act, singles, chain)
                    ph.end(act)
                    act_attention(act, doubles, chain)
                    ph.end(act)
                    act_sub_norm(act, layer, chain)
                    ph.end(act)
                ph.end(act)
                act_norm(act, segs, chain, mod[:, 3 * DC:4 * DC, :])
                ph.end(act)
                act_up(act, layer, segs)
                ph.end(act)
                ph.end(act)
                if layer in (1, 3):
                    act_norm(act, SEG1, chain)
                    ph.end(act)

        @block.vector
        def _(dve):
            ph = Phase()
            chain = Chain(dve, dve_chain)
            dve.memset(SM[:, 0:1], EPS)
            dve.memset(SM[:, 1:2], 1.0)
            dve.memset(SM[:, 2:3], P * EPS)
            dve.wait_ge(loaded, 64)
            dve.wait_ge(sig("c_exp"), 1)
            chain(dve.tensor_scalar(SC[:, :], SC[:, :], 1.0, None, ALU.add))
            chain(dve.reciprocal(SC[:, :], SC[:, :]))
            dve.tensor_tensor(SC[:, :], SC[:, :], PR[:, 0:3 * DC], ALU.mult)
            ph.end(dve)
            for layer in range(4):
                segs = SEG1 if layer < 2 or layer == LAST else SEG2
                if layer == 0:
                    dve_ada0(dve, chain)
                    ph.end(dve)
                mod = MOD[:, layer % 2, :, :]
                dve_norm(dve, SEG2 if layer >= 2 else SEG1, GAIN[:, 0, :, :])
                ph.end(dve)
                if layer == 0:
                    dve_angles(dve, chain)
                    dve_attn_in(dve, chain)
                    ph.end(dve)
                    dve.wait_ge(sig("angles_done"), 1)
                    dve_rope(dve, rope1_chunks(), chain)
                    ph.end(dve)
                    dve_attention(dve, causal_jobs(), chain)
                    ph.end(dve)
                    dve_stick(dve)
                    ph.end(dve)
                    dve_residual_tiles(dve, "attn_out", mod[:, 2 * DC:3 * DC, :], SEG1, 4)
                elif layer == 1:
                    dve_gdn_in(dve, chain)
                    ph.end(dve)
                    dve_gdn_prep(dve, chain)
                    ph.end(dve)
                    for grp in range(2):
                        dve_gdn_inverse(dve, grp, chain)
                        ph.end(dve)
                        dve_scan(dve, grp)
                        ph.end(dve)
                    dve_gdn_out(dve, chain)
                    ph.end(dve)
                    dve_residual_tiles(dve, "gdn_out", mod[:, 2 * DC:3 * DC, :], SEG1, 4)
                else:
                    dve_in(dve, layer, chain)
                    ph.end(dve)
                    dve_conv_norm(dve, layer, chain)
                    ph.end(dve)
                    dve_bias(dve, layer - 2)
                    ph.end(dve)
                    singles, doubles = mixer_jobs(layer)
                    dve_attention(dve, singles, chain)
                    ph.end(dve)
                    dve_attention(dve, doubles, chain)
                    ph.end(dve)
                    dve_sub_norm(dve, layer, chain)
                    ph.end(dve)
                    dve_residual_tiles(dve, f"out{layer}", mod[:, 2 * DC:3 * DC, :], segs, 4)
                ph.end(dve)
                dve_norm(dve, segs, GAIN[:, 1, :, :])
                ph.end(dve)
                dve_up(dve, layer, segs, chain)
                ph.end(dve)
                dve_down(dve, f"down{layer}", mod[:, 5 * DC:6 * DC, :], segs)
                ph.end(dve)
                if layer in (1, 3):
                    dve_norm(dve, SEG1, FIN_G[layer // 2])
                    if layer == 1:
                        chain(dve.tensor_copy(SM[:, 44:45], SM[:, 0:1]))
                        for k in range(DC):
                            ins = dve.tensor_copy(X[:, k, 0:T], H[:, k, 0:T])
                    else:
                        dve.drain().then_inc(sig("out_normed"), 1)
                    ph.end(dve)

        @block.gpsimd
        def _(pool):
            ph = Phase()
            ph.end(pool)
            for layer in range(4):
                for _ in range(3 if layer == 0 else 2):
                    ph.end(pool)
                if layer == 0:
                    ph.end(pool)
                    ph.end(pool)
                    pool_stick(pool)
                    ph.end(pool)
                elif layer == 1:
                    pool_gdn_prep(pool)
                    ph.end(pool)
                    for grp in range(2):
                        pool_gdn_inverse(pool, grp)
                        ph.end(pool)
                        ph.end(pool)
                    ph.end(pool)
                else:
                    for _ in range(5):
                        ph.end(pool)
                for _ in range(4):
                    ph.end(pool)
                if layer in (1, 3):
                    ph.end(pool)


def constants():
    c = np.zeros((P, CONST_W), np.float32)

    def put(name, v):
        a, w = CONST[name]
        c[:v.shape[0], a:a + w] = v
    i, j = np.arange(P)[:, None], np.arange(P)[None, :]
    put("ident", np.eye(P))
    put("ones", np.ones((P, P)))
    put("tri", i <= j)
    put("negtri", -1.0 * (i >= j))
    put("negones", -np.ones((P, P)))

    def swap(width, half):
        m = np.zeros((P, P))
        for x in range(P):
            y = x % width
            if y < 2 * half:
                m[x + half if y < half else x - half, x] = 1
        return m
    put("perm_a1", swap(64, 8))
    put("perm_64", swap(64, 32))
    put("perm_32", swap(32, 16))
    put("causal", np.where(j <= i, 0, NEG))
    put("band_lo", np.where(j >= i, 0, NEG))
    put("band_hi", np.where(j <= i, 0, NEG))
    levels = []
    for lv in range(7):
        s = 1 << lv
        levels.append((i // (2 * s) == j // (2 * s)) & (i % (2 * s) >= s) & (j % (2 * s) < s))
    put("level", np.concatenate(levels, 1))
    put("onehot", (np.arange(31)[:, None] == 78 - j).astype(np.float32))
    q, k = np.arange(64)[:, None], np.arange(64)[None, :]
    start = np.clip(q - 8, 0, 48)
    put("colmask", np.tile(np.where((k >= start) & (k < start + 16), 0, NEG), (2, 1)))
    put("half64", i // 64 == j // 64)
    freq = np.float32(500000.0) ** (-np.arange(8, dtype=np.float32) * np.float32(2.0) / np.float32(16))
    f, s = np.zeros((P, 1)), np.zeros((P, 1))
    for x in range(P):
        if x % 64 < 16:
            f[x] = freq[x % 8]
            s[x] = -1 if x % 64 < 8 else 1
    put("freq", f)
    put("sign", s)
    return c


def axial_tables():
    out = np.zeros((P, 4, T), np.float32)
    t = np.arange(T)
    row, col = (t // 64).astype(np.float32), (t % 64).astype(np.float32)
    for n, dim in enumerate((64, 32)):
        nf = dim // 4
        inv = np.float32(10000.0) ** (-np.arange(nf, dtype=np.float32) / np.float32(nf))
        ang = np.concatenate([row[:, None] * inv, col[:, None] * inv], -1)
        for x in range(P):
            y = x % dim
            a = ang[:, y % (dim // 2)]
            out[x, 2 * n] = np.cos(a)
            out[x, 2 * n + 1] = np.sin(a) * (-1 if y < dim // 2 else 1)
    return out


def column_tiles(w):
    n = w.shape[1] // 256
    return w.reshape(DC, P, n, 256).transpose(2, 1, 0, 3).reshape(n, P, TILE)


def padded(w, width=256):
    return np.pad(w, ((0, 0), (0, width - w.shape[1])))


def up_tiles(gate, up):
    g, u = gate.reshape(D, FC, P), up.reshape(D, FC, P)
    return column_tiles(np.stack([g, u], 2).reshape(D, 2 * F))


def down_tiles(w):
    return w.reshape(2, FC // 2, P, DC, P).transpose(3, 0, 2, 1, 4).reshape(2 * DC, P, DOWN)


def in_turn(a, b):
    n = len(a)
    return np.concatenate([np.stack([a, b[:n]], 1).reshape(2 * n, P, TILE), b[n:]])


def weight_tiles(i):
    w, d = [], []
    ada = [column_tiles(i["ada_w"][0]), column_tiles(i["ada_w"][1]), column_tiles(i["w_ada_2"][0]), column_tiles(i["w_ada_2"][1])]
    for layer in range(4):
        if layer < 2:
            if layer == 0:
                w.append(ada[0][:ADA // 2])
                a = i["attn_w_in"][0]
                tiles = column_tiles(np.concatenate([a[:, 0:1024], a[:, 1536:2560], a[:, 1024:1536], a[:, 2560:3072]], 1))
                w.append(in_turn(tiles, ada[0][ADA // 2:]))
                w.append(column_tiles(i["attn_w_out"][0]))
            else:
                a = i["gdn_w_in"][0]
                w.append(column_tiles(np.concatenate([a[:, 0:4096], padded(a[:, 4096:])], 1)))
                w.append(column_tiles(i["gdn_w_out"][0]))
            a = i["ffn_w_in"][layer]
            w.append(in_turn(up_tiles(a[:, 0:F], a[:, F:]), ada[layer + 1]))
            d.append(down_tiles(i["ffn_w_out"][layer]))
        else:
            l = layer - 2
            a = i["w_in_2"][l]
            qa, ka, va, ub, qc, kc, vc, qd, kd, vd = np.split(a, np.cumsum([256, 128, 128, 512, 256, 256, 256, 256, 256]), 1)
            qa = qa[:, np.r_[0:64, 128:192, 64:128, 192:256]]
            w.append(column_tiles(np.concatenate([ub, qa, qc, kc, qd, kd, padded(ka), vc, vd, padded(va)], 1)))
            w.append(column_tiles(i["w_out_2"][l]))
            up = up_tiles(i["w_gate_2"][l], i["w_up_2"][l])
            w.append(in_turn(up, ada[3]) if layer == 2 else up)
            d.append(down_tiles(i["w_down_2"][l]))
    return np.concatenate(w), np.concatenate(d)


def parameters(i):
    p = np.zeros((P, PARAM_W), np.float32)

    def put(name, v):
        a, w = PARAM[name]
        p[:v.shape[0], a:a + w] = v.reshape(v.shape[0], w)

    def cols(v):
        v = np.asarray(v)
        return v.reshape(-1, P).T
    put("c1", cols(i["c"]))
    put("c2", np.stack([cols(i["c_2"]), cols(i["c_ctx_2"])], 2))
    put("ada_b", np.concatenate([cols(i["ada_b"]), cols(i["b_ada_2"])], 1))
    put("mix_g", np.concatenate([cols(i["norm_mix_g"]), cols(i["norm1_g_2"])], 1))
    put("ffn_g", np.concatenate([cols(i["norm_ffn_g"]), cols(i["norm2_g_2"])], 1))
    put("fin_g", np.concatenate([cols(i["final_norm_g"]), cols(i["final_g_2"])], 1))
    put("gconv", cols(i["gdn_conv_w"][0]))
    put("gnorm", cols(i["gdn_norm_g"]))
    put("alog", np.broadcast_to(i["gdn_a_log"], (P, GH)))
    put("dtb", np.broadcast_to(i["gdn_dt_bias"], (P, GH)))
    put("sink", np.broadcast_to(i["attn_sink_2"].reshape(1, 8), (P, 8)))
    put("cw", i["conv_w_2"].reshape(2, 31, 2, P).transpose(3, 0, 2, 1))
    put("cb", cols(i["conv_b_2"]))
    put("lng", cols(i["conv_ln_g_2"]))
    put("lnb", cols(i["conv_ln_b_2"]))
    lq = np.stack([i["diff_lq1_2"], i["diff_lk1_2"], i["diff_lq2_2"], i["diff_lk2_2"]], 1)
    put("lq", np.broadcast_to(lq.reshape(1, 256), (P, 256)))
    put("subg", np.concatenate([i["diff_subln_g_2"].T, i["diff_subln_g_2"].T], 0))
    put("rpb", i["na_rpb_2"].transpose(3, 0, 1, 2))
    return p


def kernel(**inputs):
    import concourse.bacc as bacc
    from concourse.bass_utils import run_bass_kernel_spmd

    i = {name: np.asarray(v) for name, v in inputs.items()}
    w, d = weight_tiles(i)
    arrays = {
        "w_tiles": w, "d_tiles": d,
        "xT": np.ascontiguousarray(i["x"][0].T.reshape(DC, P, T).transpose(1, 0, 2)),
        "ctxT": np.ascontiguousarray(i["ctx_2"][0].T.reshape(DC, P, TC).transpose(1, 0, 2)),
        "positions": i["positions"], "consts": constants(), "params": parameters(i), "rope_tables": axial_tables(),
    }
    nc = bacc.Bacc("TRN2", target_bir_lowering=False, num_devices=1)
    args = [nc.dram_tensor(name, a.shape, mybir.dt.from_np(a.dtype), kind="ExternalInput").ap() for name, a in arrays.items()]
    args.append(nc.dram_tensor("outT", (P, DC, T), F32, kind="ExternalOutput").ap())
    build_program(nc, *args)
    r = run_bass_kernel_spmd(nc, [arrays], core_ids=[0])
    out = r.results[0]["outT"]
    return np.ascontiguousarray(out.transpose(1, 0, 2).reshape(1, D, T).transpose(0, 2, 1))
```

```python
from contextlib import ExitStack

import numpy as np
import concourse.bass as bass
from concourse import mybir

F32 = mybir.dt.float32
F32R = mybir.dt.float32r
I32 = mybir.dt.int32
ALU = mybir.AluOpType
ACT = mybir.ActivationFunctionType
AX_X = mybir.AxisListType.X

P = 128
D = 1024
DC = D // P
T = 512
TC = 256
TA = T + TC
NT = T // P
F = 2816
FC = F // P
EPS = 1e-6
NEG = -1e30
ADA = 24
SLOTS = 4
TILE = DC * 256
UP = FC // 2
DOWN = UP * P
GH = 8
GC = 24
TWO_PI = 2 * np.pi
PI_A, PI_B = 6.28125, 0.0019350051879882812
PI_C = TWO_PI - PI_A - PI_B
ROUND = 12582912.0

CONST = {}
_at = 0
for _name, _w in [("ident", P), ("ones", P), ("tri", P), ("negtri", P), ("negones", P), ("perm_a1", P),
                  ("perm_64", P), ("perm_32", P), ("causal", P), ("bands", 3 * P),
                  ("level", 7 * P), ("onehot", P), ("colmask", 64), ("half64", P), ("freq", 1), ("sign", 1)]:
    CONST[_name] = (_at, _w)
    _at += _w
CONST_W = _at

PARAM = {}
_at = 0
for _name, _w in [("c1", DC), ("c2", 2 * DC), ("ada_b", 4 * 48), ("mix_g", 4 * DC), ("ffn_g", 4 * DC),
                  ("fin_g", 2 * DC), ("gconv", 4 * GC), ("gnorm", 1), ("alog", GH), ("dtb", GH),
                  ("sink", 2 * 4), ("cw", 2 * 2 * 31), ("cb", 2 * 2), ("lng", 2 * 2), ("lnb", 2 * 2),
                  ("lq", 2 * 4 * 32), ("subg", 2), ("rpb", 2 * 4 * 15)]:
    PARAM[_name] = (_at, _w)
    _at += _w
PARAM_W = _at


def passes(layer):
    return [(0, 0, T), (1, T, TC)] if layer == 2 else [(0, 0, T)]


def linear_plan():
    plan = []
    for layer in range(4):
        if layer == 0:
            plan += [("ada0", "w", ADA // 2, 0, 1, None), ("attn_in", "w", ADA, 12, 1, None), ("attn_out", "w", 4, 4, 1, None)]
        elif layer == 1:
            plan += [("gdn_in", "w", 17, 17, 1, None), ("gdn_out", "w", 4, 4, 1, None)]
        else:
            plan += [(f"in{layer}", "w", 11, 11, 1, None), (f"out{layer}", "w", 4, 4, 1, None)]
        for s, _, _ in passes(layer):
            for half in range(2):
                up, down = f"up{layer}{s}{half}", f"down{layer}{s}{half}"
                if s == 0:
                    plan.append((up, "w", UP if layer == 3 else 2 * UP, UP, 1, None))
                    plan.append((down, "d", DC, DC, 1, None))
                    if layer < 3:
                        plan.append((f"after_{down}", "w", 1, 0, 1, None))
                else:
                    plan.append((up, "w", UP, UP, 2, f"up{layer}0{half}"))
                    plan.append((down, "d", DC, DC, 1, f"down{layer}0{half}"))
    return plan


def build_program(nc, w_tiles, d_tiles, xT, ctxT, positions, consts, params, rope_tables, outT):
    COUNT = {step[0]: step[2] for step in linear_plan()}
    G0, E0, at, read = {}, {}, 0, 8
    FROM = {}
    seen = {"w": 0, "d": 0}
    for name, kind, n, filled, _, again in linear_plan():
        G0[name], FROM[name] = at, FROM[again] if again else seen[kind]
        E0[name] = read
        at += n
        read += filled
        seen[kind] += 0 if again else n

    ctx = ExitStack()
    with ctx:
        def sb(name, shape, dt=F32):
            return ctx.enter_context(nc.sbuf_tensor(name, shape, dt))

        def sem(name):
            return ctx.enter_context(nc.semaphore(name))

        ring = sb("ring", [P, SLOTS, TILE])
        X = sb("X", [P, DC, TA])
        CN = sb("CN", [P, CONST_W])
        PR = sb("PR", [P, PARAM_W])
        MOD = sb("MOD", [P, 2, 48, 2])
        GAIN = sb("GAIN", [P, 2, 2, DC, 2])
        SC = sb("SC", [P, 3 * DC])
        SM = sb("SM", [P, 64])
        ACC = sb("ACC", [P, 2, 2, 256])
        with ExitStack() as mixer:
            def part(name, shape, dt=F32):
                return mixer.enter_context(nc.sbuf_tensor(name, shape, dt))
            BIG = part("BIG", [P, 32 * T])
            WORK = part("WORK", [P, 9216])
            H = part("H", [P, DC, TA])
            part("END", [P, 1152])
        with ExitStack() as ffn:
            def part(name, shape, dt=F32R):
                return ffn.enter_context(nc.sbuf_tensor(name, shape, dt))
            with ExitStack() as heads:
                O_HI = heads.enter_context(nc.sbuf_tensor("O_HI", [P, DC, TA], F32R))
                O_LO = heads.enter_context(nc.sbuf_tensor("O_LO", [P, DC, TA], F32R))
            with ExitStack() as hidden:
                HID_HI = hidden.enter_context(nc.sbuf_tensor("HID_HI", [P, UP, T], F32R))
                HID_LO = hidden.enter_context(nc.sbuf_tensor("HID_LO", [P, UP, T], F32R))
            NORMED = part("NORMED", [P, DC, T], F32)
            NORM_SQ = part("NORM_SQ", [P, 2, T], F32)
            NORM_RSTD = part("NORM_RSTD", [P, T], F32)
            part("HIDDEN_REST", [P, (2 * UP - 11) * T])
            GATED = part("GATED", [P, 2, T], F32)
            HIDDEN = part("HIDDEN", [P, 2, T], F32)
            part("GAP", [P, 3200])
            with ExitStack() as units:
                units.enter_context(nc.sbuf_tensor("UNIT_GAP", [P, 2 * TILE], F32R))
                U_HI = units.enter_context(nc.sbuf_tensor("U_HI", [P, 2, TILE // 2], F32R))
                U_LO = units.enter_context(nc.sbuf_tensor("U_LO", [P, 2, TILE // 2], F32R))
            W_HI, W_LO = part("W_HI", [P, 2, TILE]), part("W_LO", [P, 2, TILE])
            H_HI, H_LO = part("H_HI", [P, DC, T]), part("H_LO", [P, DC, T])
        PS = ctx.enter_context(nc.psum_tensor("PS", [P, 4096], F32))

        def const(name):
            a, w = CONST[name]
            return CN[:, a:a + w]

        def par(name):
            a, w = PARAM[name]
            return PR[:, a:a + w]

        ident, ones = const("ident"), const("ones")

        params_loaded = sem("params_loaded")
        consts_loaded = sem("consts_loaded")
        x_loaded = sem("x_loaded")
        tile_loaded = [sem(f"tile_loaded{s}") for s in range(SLOTS)]
        tile_done = sem("tile_done")
        evac_done = sem("evac_done")
        phase_done = sem("phase_done")
        dve_chain = sem("dve_chain")
        act_chain = sem("act_chain")
        stored = sem("stored")
        tables_loaded = sem("tables_loaded")
        scratch = {}

        def sig(name):
            if name not in scratch:
                scratch[name] = sem(name)
            return scratch[name]

        class Chain:

            def __init__(self, eng, s):
                self.eng, self.s, self.n = eng, s, 0

            def __call__(self, ins):
                ins.then_inc(self.s, 1)
                self.n = self.n + 1
                self.eng.wait_ge(self.s, self.n)

        def over_tiles(eng, n, body, chain=None):
            rounds = n // SLOTS
            if rounds > 1:
                base, per = (chain.n, body.steps * SLOTS) if chain else (0, 0)
                with eng.Fori(0, rounds) as i:
                    if chain:
                        chain.n = i * per + base
                    for u in range(SLOTS):
                        body(i * SLOTS + u, u, i)
                if chain:
                    chain.n = base + per * rounds
            else:
                for i in range(rounds):
                    for u in range(SLOTS):
                        body(i * SLOTS + u, u, i)
            for u in range(n - rounds * SLOTS):
                body(rounds * SLOTS + u, u, rounds)

        def over_pairs(eng, n, first, second, chain=None, steps=0):
            base = chain.n if chain else 0
            with eng.Fori(0, n // 2) as i:
                if chain:
                    chain.n = i * (2 * steps) + base
                for v in range(2):
                    first(i * 2 + v, v, i)
                    second(i * 2 + v, v, i)
            if chain:
                chain.n = base + steps * n

        class Phase:
            def __init__(self):
                self.n = 0

            def end(self, eng):
                self.n += 1
                eng.drain().then_inc(phase_done, 1)
                eng.wait_ge(phase_done, 4 * self.n)

        BASE = {}

        def base(who, name, count):
            key = (who, name)
            at = BASE.get(key, 0)
            BASE[key] = at + count
            return at

        SEG1 = [(0, T)]
        SEG2 = [(0, T), (T, TC)]

        def wait_tile(pe, name, u, i):
            g = G0[name] + u
            pe.wait_ge(tile_loaded[g % SLOTS], (i + g // SLOTS + 1) * 16)
            return g % SLOTS

        def pe_feature_tiles(pe, name, src, segs, n, first=0, chunks=2, nb=None):
            e0 = E0[name] + first
            nb = nb or 4 // len(segs)
            W = 4096 // nb

            def body(t, u, i):
                slot = wait_tile(pe, name, u + first, i)
                pe.wait_ge(evac_done, t + (e0 - nb + 1))
                buf = (u + first) % nb
                for j in range(chunks):
                    for s, (c0, w) in enumerate(segs):
                        o = buf * W + j * W // 2 + s * 512
                        for k in range(DC):
                            mm = pe.matmul(PS[:, o:o + w], ring[:, slot, k * 256 + j * P:k * 256 + (j + 1) * P],
                                           src[:, k, c0:c0 + w], start=k == 0, stop=k == DC - 1)
                mm.then_inc(tile_done, 1)
            over_tiles(pe, n, body)

        def act_copy_tiles(act, name, dst, segs, n, first=0, chunks=2, nb=None):
            g0 = G0[name] + first
            nb = nb or 4 // len(segs)
            W = 4096 // nb
            width = sum(w for _, w in segs)

            def body(t, u, i):
                act.wait_ge(tile_done, t + (g0 + 1))
                buf = (u + first) % nb
                act.activation(dst[:, bass.ds((t + first) * 2, chunks), 0:width],
                               PS[:, buf * W:buf * W + W].rearrange("p (j c) -> p j c", j=2)[:, 0:chunks, 0:width],
                               ACT.Copy).then_inc(evac_done, 1)
            over_tiles(act, n, body)

        def pe_token_tiles(pe, name, tokens, n, first, cols=256, nb=4):
            e0 = E0[name] + first
            W = 4096 // nb
            for t in range(n):
                slot = wait_tile(pe, name, first + t, 0)
                pe.wait_ge(evac_done, e0 + t - nb + 1)
                o = (first + t) % nb * W
                for a in range(tokens // P):
                    for k in range(DC):
                        mm = pe.matmul(PS[:, o + a * 256:o + a * 256 + cols], H[:, k, a * P:(a + 1) * P],
                                       ring[:, slot, k * 256:k * 256 + cols], start=k == 0, stop=k == DC - 1)
                mm.then_inc(tile_done, 1)

        def act_token_tiles(act, name, dst, tokens, n, first, cols=256, nb=4, col0=0):
            g0 = G0[name] + first
            W = 4096 // nb
            A = tokens // P
            for t in range(n):
                act.wait_ge(tile_done, g0 + t + 1)
                o = (first + t) % nb * W
                act.activation(dst[:, :, col0 + t * 256:col0 + t * 256 + cols],
                               PS[:, o:o + A * 256].rearrange("p (a c) -> p a c", a=A)[:, :, 0:cols],
                               ACT.Copy).then_inc(evac_done, 1)

        SPLIT, _n = {}, 0
        for _step in linear_plan():
            if _step[0].startswith(("attn", "gdn_out", "out", "up", "down")):
                SPLIT[_step[0]] = _n
                _n += _step[3]
        OWN = {_step[0]: _step[3] for _step in linear_plan()}
        NEXT = {}
        for _layer in range(4):
            for _s, _, _ in passes(_layer):
                _names = [f"{_kind}{_layer}{_s}{_half}" for _half in range(2) for _kind in ("up", "down")]
                NEXT.update(zip(_names, _names[1:]))

        def side(name):
            return COUNT[name] > OWN[name]

        def parts_of(name):
            return DOWN if name.startswith("down") else TILE

        def round_tile(act, name, u, i, m, used=None):
            g = G0[name] + u
            apart = 2 if side(name) else 1
            b = (SPLIT[name] + (u // apart if not isinstance(m, int) else m)) % 2
            act.wait_ge(tile_loaded[g % SLOTS], (i + g // SLOTS + 1) * 16)
            act.wait_ge(tile_done, used if used else i * SLOTS + (g - 2 * apart + 1))
            w = parts_of(name)
            act.activation(W_HI[:, b, 0:w], ring[:, g % SLOTS, 0:w], ACT.Copy).then_inc(sig("tile_rounded"), 1)

        def takes_rest(name):
            return "vector" if name[-2] == "1" else "gpsimd"

        def rest_tile(eng, name, u, i, m, used=None):
            g = G0[name] + u
            apart = 2 if side(name) else 1
            b = (SPLIT[name] + (u // apart if not isinstance(m, int) else m)) % 2
            eng.wait_ge(sig("tile_rounded"), m + (SPLIT[name] + 1))
            w = parts_of(name)
            eng.tensor_tensor(W_LO[:, b, 0:w], ring[:, g % SLOTS, 0:w], W_HI[:, b, 0:w].bitcast(F32),
                              ALU.subtract).then_inc(sig("tile_split"), 1)

        def over_own(eng, name, body, between=None, chain=None, steps=0):
            pairs = side(name)
            n = OWN[name]
            per = 2 if pairs else SLOTS
            apart = SLOTS // per
            rounds = (n - 1) // per
            base = chain.n if chain else 0

            def step(m, v, i):
                if pairs and between:
                    between(m, v * apart + 1, i)
                body(m, v * apart, i)
            if rounds:
                with eng.Fori(0, rounds) as i:
                    if chain:
                        chain.n = i * (per * steps) + base
                    for v in range(per):
                        step(i * per + v, v, i)
            if chain:
                chain.n = base + per * steps * rounds
            for m in range(rounds * per, n):
                step(m, m, 0)

        def next_own(eng, name, split, m, u, i):
            if split is rest_tile and takes_rest(name) == "gpsimd" and eng is not nc.gpsimd:
                return
            n = OWN[name]
            if not isinstance(m, int) or m < n - 1:
                split(eng, name, u + (2 if side(name) else 1), i, m + 1)
            elif name in NEXT:
                split(eng, NEXT[name], 0, 0, 0, G0[name] + (2 if side(name) else 1) * (n - 2) + 1)

        def pe_three(pe, o, w, hi, lo, x_hi, x_lo, n, wait=None):
            for k in range(n):
                if wait:
                    wait(k)
                pe.matmul(PS[:, o:o + w], hi(k), x_hi(k), start=k == 0, stop=False)
                pe.matmul(PS[:, o:o + w], hi(k), x_lo(k), start=False, stop=False)
                mm = pe.matmul(PS[:, o:o + w], lo(k), x_hi(k), start=False, stop=k == n - 1)
            return mm

        def wait_normed(pe):
            b = base("pe", "chunk_normed", DC)
            return lambda k: pe.wait_ge(sig("chunk_normed"), b + k + 1)

        def pe_out(pe, name, segs):
            e0 = E0[name]
            b = base("pe", "heads_split", DC)
            for m in range(OWN[name]):
                hi, lo = W_HI[:, (SPLIT[name] + m) % 2, :], W_LO[:, (SPLIT[name] + m) % 2, :]
                pe.wait_ge(sig("tile_split"), SPLIT[name] + m + 1)
                pe.wait_ge(evac_done, e0 + m - 1)
                for j in range(2):
                    for c0, w in segs:
                        col = lambda k: slice(k * 256 + j * P, k * 256 + (j + 1) * P)
                        mm = pe_three(pe, out_column(m, j, c0), w, lambda k: hi[:, col(k)], lambda k: lo[:, col(k)],
                                      lambda k: O_HI[:, k, c0:c0 + w], lambda k: O_LO[:, k, c0:c0 + w], DC,
                                      (lambda k: pe.wait_ge(sig("heads_split"), b + k + 1)) if m == j == c0 == 0 else None)
                mm.then_inc(tile_done, 1)

        def out_column(m, j, c0):
            return (m % 2) * 2048 + j * 1024 + c0

        def act_out(act, name, segs):
            width = sum(w for _, w in segs)
            round_tile(act, name, 0, 0, 0, G0[name])
            for k in range(DC):
                act.activation(O_HI[:, k, 0:width], H[:, k, 0:width], ACT.Copy).then_inc(sig("heads_rounded"), 1)
            act_round(act, name)

        def dve_out(dve, name, gate, segs):
            width = sum(w for _, w in segs)
            b = base("dve", "heads_rounded", DC)
            for k in range(DC):
                dve.wait_ge(sig("heads_rounded"), b + k + 1)
                dve.tensor_tensor(O_LO[:, k, 0:width], H[:, k, 0:width], O_HI[:, k, 0:width].bitcast(F32),
                                  ALU.subtract).then_inc(sig("heads_split"), 1)
            for m in range(OWN[name]):
                dve.wait_ge(tile_done, G0[name] + m + 1)
                for j in range(2):
                    for s, (c0, w) in enumerate(segs):
                        o, x = out_column(m, j, c0), X[:, 2 * m + j, c0:c0 + w]
                        ins = dve.scalar_tensor_tensor(out=x, in0=PS[:, o:o + w], scalar=gate[:, 2 * m + j, s:s + 1], in1=x,
                                                       op0=ALU.mult, op1=ALU.add)
                ins.then_inc(evac_done, 1)

        def pe_up(pe, layer, name, w):
            e0 = E0[name]
            normed = wait_normed(pe) if name[-1] == "0" else None

            def product(m, u, i):
                v = u // (2 if side(name) else 1)
                b = (SPLIT[name] + v) % 2
                pe.wait_ge(sig("tile_split"), m + (SPLIT[name] + 1))
                pe.wait_ge(evac_done, m + (e0 - 1))
                for j in range(2):
                    col = lambda k: slice(k * 256 + j * P, k * 256 + (j + 1) * P)
                    mm = pe_three(pe, (v % 2) * 1024 + j * 512, w, lambda k: W_HI[:, b, col(k)], lambda k: W_LO[:, b, col(k)],
                                  lambda k: H_HI[:, k, 0:w], lambda k: H_LO[:, k, 0:w], DC, normed if j == 0 else None)
                mm.then_inc(tile_done, 1)
            if side(name):
                half = int(name[-1])
                with pe.Fori(0, UP // 2) as i:
                    for v in range(2):
                        product(i * 2 + v, 2 * v, i)
                        pe_ada_tile(pe, layer + 1, i * 2 + (half * (UP + 1) + v), v)
                product(UP - 1, 2 * (UP - 1), 0)
                pe_ada_tile(pe, layer + 1, half * (UP + 1) + UP - 1, 0)
            else:
                over_own(pe, name, product)

        def act_up(act, name, w):
            g0, e0 = G0[name], E0[name]
            apart = 2 if side(name) else 1

            def body(m, u, i):
                v = u // apart % 2
                next_own(act, name, round_tile, m, u, i)
                act.wait_ge(tile_done, i * SLOTS + (g0 + u + 1))
                act.wait_ge(evac_done, m + (e0 - 1))
                act.activation(GATED[:, v, 0:w], PS[:, v * 1024:v * 1024 + w], ACT.Silu).then_inc(sig("gate_silu"), 1)
                act.wait_ge(evac_done, m + (e0 + 1))
                act.activation(HID_HI[:, bass.ds(m, 1), 0:w], HIDDEN[:, v:v + 1, 0:w], ACT.Copy).then_inc(sig("hidden_rounded"), 1)
            over_own(act, name, body)

        def dve_up(dve, layer, name, w, chain):
            apart = 2 if side(name) else 1
            b = base("dve", "gate_silu", UP)
            b2 = base("dve", "hidden_rounded", UP)

            def body(m, u, i):
                v = u // apart % 2
                next_own(dve, name, rest_tile, m, u, i)
                dve.wait_ge(sig("gate_silu"), m + (b + 1))
                dve.tensor_tensor(HIDDEN[:, v, 0:w], GATED[:, v, 0:w], PS[:, v * 1024 + 512:v * 1024 + 512 + w],
                                  ALU.mult).then_inc(evac_done, 1)
                dve.wait_ge(sig("hidden_rounded"), m + (b2 + 1))
                dve.tensor_tensor(HID_LO[:, bass.ds(m, 1), 0:w], HIDDEN[:, v:v + 1, 0:w],
                                  HID_HI[:, bass.ds(m, 1), 0:w].bitcast(F32), ALU.subtract).then_inc(sig("hidden_split"), 1)
            over_own(dve, name, body,
                     lambda m, u, i: dve_ada_tile(dve, layer + 1, name, u, i, (u // 2) % 2, chain), chain,
                     ada_steps(layer + 1) if side(name) else 0)

        def pe_down(pe, layer, name, w):
            e0 = E0[name]
            b_h = base("pe", "hidden_split", UP)

            def wait_hidden(k):
                if k in (0, UP - 1):
                    pe.wait_ge(sig("hidden_split"), b_h + (UP if k else UP - 1))

            def product(m, u, i):
                b, o = (SPLIT[name] + u) % 2, 2048 + (u % 2) * 512
                pe.wait_ge(sig("tile_split"), m + (SPLIT[name] + 1))
                pe.wait_ge(evac_done, m + (e0 - 1))
                col = lambda k: slice(k * P, (k + 1) * P)
                pe_three(pe, o, w, lambda k: W_HI[:, b, col(k)], lambda k: W_LO[:, b, col(k)],
                         lambda k: HID_HI[:, k, 0:w], lambda k: HID_LO[:, k, 0:w], UP, wait_hidden).then_inc(tile_done, 1)
            over_own(pe, name, product)
            if "after_" + name in G0:
                pe_ada_tile(pe, layer + 1, int(name[-1]) * (UP + 1) + UP, 1)

        def pool_rest(pool, name):
            if takes_rest(name) == "gpsimd":
                over_own(pool, name, lambda m, u, i: next_own(pool, name, rest_tile, m, u, i))

        def act_round(act, name):
            over_own(act, name, lambda m, u, i: next_own(act, name, round_tile, m, u, i))

        def dve_down(dve, layer, name, gate, c0, w, chain):
            g0 = G0[name]

            after = "after_" + name

            def body(m, u, i):
                next_own(dve, name, rest_tile, m, u, i)
                if after in G0 and isinstance(m, int) and m == DC - 1:
                    dve_ada_tile(dve, layer + 1, after, 0, 0, 1, chain)
                dve.wait_ge(tile_done, i * SLOTS + (g0 + u + 1))
                o = 2048 + (u % 2) * 512
                dve.scalar_tensor_tensor(out=X[:, bass.ds(m, 1), c0:c0 + w], in0=PS[:, o:o + w].rearrange("p (a c) -> p a c", a=1),
                                         scalar=gate[:, bass.ds(m, 1)], in1=X[:, bass.ds(m, 1), c0:c0 + w],
                                         op0=ALU.mult, op1=ALU.add).then_inc(evac_done, 1)
            over_own(dve, name, body)
            if after in G0 and name[-1] == "1":
                dve_ada_end(dve, layer + 1, after, chain)

        def act_split_norm(act, name, c0, w, chain, shift):
            if name in SPLIT:
                round_tile(act, name, 0, 0, 0, G0[name])
            b_mm = base("act", "split_norm_summed", DC)
            b_n = base("act", "split_norm_scaled", DC)
            for k in range(DC):
                if k >= 2:
                    act.wait_ge(sig("split_norm_summed"), b_mm + k - 1)
                act.activation(NORM_SQ[:, k % 2, 0:w], X[:, k, c0:c0 + w], ACT.Square).then_inc(sig("split_norm_squared"), 1)
            act.wait_ge(sig("split_norm_summed"), b_mm + DC)
            chain(act.activation(NORM_RSTD[:, 0:w], PS[:, 0:w], ACT.Ln, scale=1.0 / D, bias=SM[:, 0:1]))
            act.activation(NORM_RSTD[:, 0:w], NORM_RSTD[:, 0:w], ACT.Exp, scale=-0.5).then_inc(sig("split_norm_rstd"), 1)
            for k in range(DC):
                act.wait_ge(sig("split_norm_scaled"), b_n + k + 1)
                act.activation(H_HI[:, k, 0:w], NORMED[:, k, 0:w], ACT.Identity, bias=shift[:, k:k + 1]).then_inc(sig("split_norm_rounded"), 1)
            act.activation(SM[:, 45:46], SM[:, 1:2], ACT.Silu)

        def pe_split_norm(pe, w):
            b = base("pe", "split_norm_squared", DC)
            for k in range(DC):
                pe.wait_ge(sig("split_norm_squared"), b + k + 1)
                pe.matmul(PS[:, 0:w], ones, NORM_SQ[:, k % 2, 0:w], start=k == 0, stop=k == DC - 1).then_inc(sig("split_norm_summed"), 1)

        def dve_split_norm(dve, name, c0, w, gain, shift):
            if name in SPLIT and takes_rest(name) == "vector":
                rest_tile(dve, name, 0, 0, 0)
            b = base("dve", "split_norm_rstd", 1)
            b_r = base("dve", "split_norm_rounded", DC)
            b_n = base("dve", "split_norm_scaled", DC)
            dve.wait_ge(sig("split_norm_rstd"), b + 1)
            for k in range(DC):
                dve.scalar_tensor_tensor(out=NORMED[:, k, 0:w], in0=X[:, k, c0:c0 + w], scalar=gain[:, k:k + 1],
                                         in1=NORM_RSTD[:, 0:w], op0=ALU.mult, op1=ALU.mult).then_inc(sig("split_norm_scaled"), 1)
            dve.wait_ge(sig("split_norm_scaled"), b_n + DC)
            for k in range(DC):
                dve.wait_ge(sig("split_norm_rounded"), b_r + k + 1)
                dve.scalar_tensor_tensor(out=H_LO[:, k, 0:w], in0=NORMED[:, k, 0:w], scalar=shift[:, k:k + 1],
                                         in1=H_HI[:, k, 0:w].bitcast(F32), op0=ALU.add,
                                         op1=ALU.subtract).then_inc(sig("chunk_normed"), 1)

        ADA_PS = PS[:, 3072:3072 + 96].rearrange("p (n v) -> p n v", v=2)

        def vectors(layer):
            return [SC[:, 0:DC]] if layer < 2 else [SC[:, DC + v:3 * DC:2] for v in range(2)]

        def ada_steps(layer):
            return len(vectors(layer)) * DC - 1

        def dve_ada_tile(dve, layer, name, u, i, buf, chain, apart=4):
            g = G0[name] + u
            dve.wait_ge(tile_loaded[g % SLOTS], (i + g // SLOTS + 1) * 16)
            if g >= apart or not isinstance(i, int):
                dve.wait_ge(tile_done, i * SLOTS + (g - apart + 1))
            vs = vectors(layer)
            for v, c in enumerate(vs):
                for k in range(DC):
                    w, acc = ring[:, g % SLOTS, k * 256:(k + 1) * 256], ACC[:, buf, v, :]
                    if k == 0:
                        ins = dve.tensor_scalar(acc, w, c[:, 0:1], None, ALU.mult)
                    else:
                        ins = dve.scalar_tensor_tensor(out=acc, in0=w, scalar=c[:, k:k + 1], in1=acc,
                                                       op0=ALU.mult, op1=ALU.add)
                    if k < DC - 1 or v < len(vs) - 1:
                        chain(ins)
            ins.then_inc(sig("ada_weighted"), 1)

        def ada_base(layer):
            return layer * ADA

        def pe_ada_tile(pe, layer, n, buf):
            pe.wait_ge(sig("ada_weighted"), n + (ada_base(layer) + 1))
            for j in range(2):
                for v in range(len(vectors(layer))):
                    mm = pe.matmul(ADA_PS[:, bass.ds(n * 2 + j, 1), v], ACC[:, buf, v, j * P:(j + 1) * P], ones[:, 0:1],
                                   start=True, stop=True)
            mm.then_inc(tile_done, 1)

        def pe_ada0(pe):
            over_tiles(pe, ADA // 2, lambda t, u, i: pe_ada_tile(pe, 0, t, u % 2))

        def dve_ada0(dve, chain):
            def tile(u, i):
                dve_ada_tile(dve, 0, "ada0", u, i, u % 2, chain, apart=2)
            for u in range(SLOTS):
                tile(u, 0)
            base, per = chain.n, SLOTS * ada_steps(0)
            with dve.Fori(1, ADA // 2 // SLOTS) as i:
                chain.n = (i - 1) * per + base
                for u in range(SLOTS):
                    tile(u, i)
            chain.n = base + per * (ADA // 2 // SLOTS - 1)
            dve_ada_end(dve, 0, "ada0", chain, ADA // 2)

        def pe_attn_in(pe):
            e0 = E0["attn_in"]

            normed = wait_normed(pe)

            def start(m, v):
                pe.wait_ge(sig("tile_split"), m + (SPLIT["attn_in"] + 1))
                pe.wait_ge(evac_done, m + (e0 - 1))
                return W_HI[:, (SPLIT["attn_in"] + v) % 2, :], W_LO[:, (SPLIT["attn_in"] + v) % 2, :]

            def features(m, v, i):
                hi, lo = start(m, v)
                for j in range(2):
                    col = lambda k: slice(k * 256 + j * P, k * 256 + (j + 1) * P)
                    mm = pe_three(pe, v * 1024 + j * 512, T, lambda k: hi[:, col(k)], lambda k: lo[:, col(k)],
                                  lambda k: H_HI[:, k, :], lambda k: H_LO[:, k, :], DC, normed if j == 0 else None)
                mm.then_inc(tile_done, 1)
            over_pairs(pe, 8, features, lambda m, v, i: pe_ada_tile(pe, 0, m + ADA // 2, v))
            for m in range(8, 12):
                hi, lo = start(m, m % 2)
                for a in range(NT):
                    tok, col = slice(a * P, (a + 1) * P), lambda k: slice(k * 256, (k + 1) * 256)
                    mm = pe_three(pe, (m % 2) * 1024 + a * 256, 256, lambda k: H_HI[:, k, tok], lambda k: H_LO[:, k, tok],
                                  lambda k: hi[:, col(k)], lambda k: lo[:, col(k)], DC)
                mm.then_inc(tile_done, 1)
                pe_ada_tile(pe, 0, m + ADA // 2, m % 2)

        def act_attn_in(act):
            g0 = G0["attn_in"]

            def features(m, v, i):
                next_own(act, "attn_in", round_tile, m, 2 * v, i)
                act.wait_ge(tile_done, i * 4 + (g0 + 2 * v + 1))
                act.activation(QK1[:, bass.ds(m * 2, 2), :],
                               PS[:, v * 1024:(v + 1) * 1024].rearrange("p (j c) -> p j c", j=2),
                               ACT.Copy).then_inc(evac_done, 1)
            over_pairs(act, 8, features, lambda m, v, i: None)
            for m in range(8, 12):
                next_own(act, "attn_in", round_tile, m, 2 * m, 0)
                act.wait_ge(tile_done, g0 + 2 * m + 1)
                act.activation(V1[:, :, (m - 8) * 256:(m - 7) * 256],
                               PS[:, (m % 2) * 1024:(m % 2 + 1) * 1024].rearrange("p (a c) -> p a c", a=NT),
                               ACT.Copy).then_inc(evac_done, 1)

        def dve_attn_in(dve, chain):
            over_pairs(dve, 12, lambda m, v, i: dve_ada_tile(dve, 0, "attn_in", 2 * v + 1, i, v, chain),
                       lambda m, v, i: None, chain, ada_steps(0))
            dve_ada_end(dve, 0, "attn_in", chain)

        def dve_ada_end(dve, layer, name, chain, tiles=ADA):
            mod = MOD[:, layer % 2, :, :]
            n = 2 * tiles
            dve.wait_ge(tile_done, G0[name] + COUNT[name])
            bias = par("ada_b").rearrange("p (l n) -> p l n", l=4)[:, layer, :]
            for v in range(len(vectors(layer))):
                chain(dve.tensor_tensor(mod[:, 0:n, v], ADA_PS[:, 0:n, v], bias[:, 0:n], ALU.add))
                for which, row in ((0, DC), (1, 4 * DC)):
                    if row < n:
                        g = par("mix_g" if which == 0 else "ffn_g").rearrange("p (l k) -> p l k", l=4)[:, layer, :]
                        dve.scalar_tensor_tensor(out=GAIN[:, layer % 2, which, :, v], in0=mod[:, row:row + DC, v], scalar=1.0,
                                                 in1=g, op0=ALU.add, op1=ALU.mult)

        SQ = [WORK[:, 0:TA], WORK[:, TA:2 * TA]]
        RSTD = WORK[:, 2 * TA:3 * TA]

        def act_norm(act, segs, chain, shift=None):
            width = sum(w for _, w in segs)
            b_mm = base("act", "norm_summed", DC)
            for k in range(DC):
                if k >= 2:
                    act.wait_ge(sig("norm_summed"), b_mm + k - 1)
                act.activation(SQ[k % 2][:, 0:width], X[:, k, 0:width], ACT.Square).then_inc(sig("norm_squared"), 1)
            act.wait_ge(sig("norm_summed"), b_mm + DC)
            chain(act.activation(RSTD[:, 0:width], PS[:, 0:width], ACT.Ln, scale=1.0 / D, bias=SM[:, 0:1]))
            act.activation(RSTD[:, 0:width], RSTD[:, 0:width], ACT.Exp, scale=-0.5).then_inc(sig("norm_rstd"), 1)
            if shift is not None:
                b_h = base("act", "norm_scaled", DC)
                for k in range(DC):
                    act.wait_ge(sig("norm_scaled"), b_h + k + 1)
                    for s, (c0, w) in enumerate(segs):
                        act.activation(H[:, k, c0:c0 + w], H[:, k, c0:c0 + w], ACT.Identity, bias=shift[:, k, s:s + 1])

        def pe_norm(pe, segs):
            b = base("pe", "norm_squared", DC)
            for k in range(DC):
                pe.wait_ge(sig("norm_squared"), b + k + 1)
                for c0, w in segs:
                    mm = pe.matmul(PS[:, c0:c0 + w], ones, SQ[k % 2][:, c0:c0 + w], start=k == 0, stop=k == DC - 1)
                mm.then_inc(sig("norm_summed"), 1)

        def dve_norm(dve, segs, gain, dst, done):
            b = base("dve", "norm_rstd", 1)
            dve.wait_ge(sig("norm_rstd"), b + 1)
            for k in range(DC):
                for s, (c0, w) in enumerate(segs):
                    ins = dve.scalar_tensor_tensor(out=dst[:, k, c0:c0 + w], in0=X[:, k, c0:c0 + w],
                                                   scalar=gain[:, k, s:s + 1], in1=RSTD[:, c0:c0 + w],
                                                   op0=ALU.mult, op1=ALU.mult)
                ins.then_inc(sig(done), 1)

        S_SB = [[WORK[:, n * TA:(n + 1) * TA] for n in (0, 1, 2, 3)] + [WORK[:, 8192:8192 + TA]],
                [WORK[:, n * TA:(n + 1) * TA] for n in (0, 1, 2, 3, 6, 7, 8, 9)]]
        PT = [WORK[:, (4 + n) * TA:(5 + n) * TA] for n in range(2)]

        def map_list(jobs):
            return [(n, m) for n, job in enumerate(jobs) for m in range(len(job["q"]))]

        def small(n, s):
            return SM[:, 8 + n * 8 + s % 8:9 + n * 8 + s % 8]

        def attention_depth(jobs):
            return (S_SB[1], 3) if len(jobs[0]["q"]) == 2 else (S_SB[0], 3)

        def pe_attention(pe, jobs):
            S_BUF, ahead = attention_depth(jobs)
            bufs = len(S_BUF)
            maps = map_list(jobs)
            b_read = base("pe", "scores_read", len(maps))
            b_p = base("pe", "weights_ready", len(jobs))
            b_pt = base("pe", "turned_copied", len(jobs))
            b_o = base("pe", "heads_copied", len(jobs))

            def scores(s):
                n, m = maps[s]
                job = jobs[n]
                if s >= 2:
                    pe.wait_ge(sig("scores_read"), b_read + s - 1)
                for o, k in job["k"][m]:
                    a = (s % 2) * 1024 + o
                    mm = pe.matmul(PS[:, a:a + k.shape[-1]], job["q"][m], k, start=True, stop=True)
                mm.then_inc(sig("scores_ready"), 1)

            def turn(n):
                s = max(x for x, (j, _) in enumerate(maps) if j == n)
                pe.wait_ge(sig("weights_ready"), b_p + n + 1)
                if n >= 1:
                    pe.wait_ge(sig("turned_copied"), b_pt + n)
                for x in range(len(jobs[n]["v"])):
                    mm = pe.transpose(PS[:, 2048 + x * P:2048 + (x + 1) * P], S_BUF[s % bufs][:, x * P:(x + 1) * P], ident)
                mm.then_inc(sig("turned"), 1)

            def outputs(n):
                job = jobs[n]
                pe.wait_ge(sig("turned_copied"), b_pt + n + 1)
                if n >= 2:
                    pe.wait_ge(sig("heads_copied"), b_o + n - 1)
                off = job["off"]
                o = 3072 + (n % 2) * 512
                for x, v in enumerate(job["v"]):
                    mm = pe.matmul(PS[off:off + 64, o:o + P], v, PT[n % 2][:, x * P:(x + 1) * P],
                                   start=x == 0, stop=x == len(job["v"]) - 1)
                mm.then_inc(sig("heads_ready"), 1)

            per = len(jobs[0]["q"])
            made = 0
            for n in range(len(jobs)):
                for s in range(made, min((n + 1) * per + ahead + 1, len(maps))):
                    scores(s)
                    made = s + 1
                if n >= 1:
                    outputs(n - 1)
                turn(n)
            outputs(len(jobs) - 1)

        def dve_attention(dve, jobs, chain):
            maps = map_list(jobs)
            b_s = base("dve", "scores_ready", len(maps))
            b_t = base("dve", "turned", len(jobs))
            b_e = base("dve", "exps_ready", len(maps))
            S_BUF, ahead = attention_depth(jobs)
            bufs = len(S_BUF)

            def score_part(s):
                n, m = maps[s]
                job = jobs[n]
                per = len(job["q"])
                nk = len(job["v"]) * P
                S = S_BUF[s % bufs]
                dve.wait_ge(sig("scores_ready"), b_s + s + 1)
                if s >= bufs:
                    dve.wait_ge(sig("turned"), b_t + (s - bufs) // per + 1)
                pieces = job["pieces"]
                for x, (o, p0, w, mask) in enumerate(pieces):
                    src = PS[:, (s % 2) * 1024 + p0:(s % 2) * 1024 + p0 + w]
                    if mask is None:
                        ins = dve.tensor_scalar(S[:, o:o + w], src, job["scale"], None, ALU.mult)
                    else:
                        ins = dve.scalar_tensor_tensor(out=S[:, o:o + w], in0=src, scalar=job["scale"], in1=mask,
                                                       op0=ALU.mult, op1=ALU.add)
                    if x < len(pieces) - 1:
                        chain(ins)
                ins.then_inc(sig("scores_read"), 1)
                dve.wait_ge(sig("scores_read"), b_read + s + 1)
                if job["sink"] is None:
                    dve.tensor_reduce(small(0, s), S[:, 0:nk], AX_X, ALU.max,
                                      negate=True).then_inc(sig("max_ready"), 1)
                else:
                    chain(dve.tensor_reduce(small(0, s), S[:, 0:nk], AX_X, ALU.max, negate=True))
                    dve.scalar_tensor_tensor(out=small(0, s), in0=job["sink"], scalar=-1.0,
                                             in1=small(0, s), op0=ALU.mult,
                                             op1=ALU.min).then_inc(sig("max_ready"), 1)

            def weight_part(s):
                n, m = maps[s]
                job = jobs[n]
                nk = len(job["v"]) * P
                S = S_BUF[s % bufs]
                dve.wait_ge(sig("exps_ready"), b_e + s + 1)
                total, inv = small(1, s), small(2, s)
                if job["sink"] is not None:
                    chain(dve.tensor_tensor(total, total, small(3, s), ALU.add))
                chain(dve.reciprocal(inv, total))
                if m == 1:
                    chain(dve.tensor_scalar(inv, inv, job["neg_lam"], None, ALU.mult))
                    dve.scalar_tensor_tensor(out=S[:, 0:nk], in0=S[:, 0:nk], scalar=inv,
                                             in1=S_BUF[(s - 1) % bufs][:, 0:nk], op0=ALU.mult,
                                             op1=ALU.add).then_inc(sig("weights_ready"), 1)
                elif len(job["q"]) == 2:
                    chain(dve.tensor_scalar(S[:, 0:nk], S[:, 0:nk], inv, None, ALU.mult))
                else:
                    dve.tensor_scalar(S[:, 0:nk], S[:, 0:nk], inv, None, ALU.mult).then_inc(sig("weights_ready"), 1)

            b_read = base("dve", "scores_read", len(maps))
            for s in range(ahead):
                score_part(s)
            for s in range(len(maps)):
                if s + ahead < len(maps):
                    score_part(s + ahead)
                weight_part(s)

        def act_attention(act, jobs, chain):
            maps = map_list(jobs)
            b_m = base("act", "max_ready", len(maps))
            b_t = base("act", "turned", len(jobs))
            b_h = base("act", "heads_ready", len(jobs))
            S_BUF, ahead = attention_depth(jobs)
            bufs = len(S_BUF)

            def exps(s):
                n, m = maps[s]
                job = jobs[n]
                nk = len(job["v"]) * P
                S = S_BUF[s % bufs]
                act.wait_ge(sig("max_ready"), b_m + s + 1)
                if job["sink"] is not None:
                    chain(act.activation(small(3, s), job["sink"], ACT.Exp, bias=small(0, s)))
                act.activation(S[:, 0:nk], S[:, 0:nk], ACT.Exp, bias=small(0, s),
                               accum_out=small(1, s)).then_inc(sig("exps_ready"), 1)

            def copy_turned(n):
                act.wait_ge(sig("turned"), b_t + n + 1)
                if n >= 2:
                    act.wait_ge(sig("heads_ready"), b_h + n - 1)
                nk = len(jobs[n]["v"]) * P
                act.activation(PT[n % 2][:, 0:nk], PS[:, 2048:2048 + nk], ACT.Copy).then_inc(sig("turned_copied"), 1)

            def copy_heads(n):
                act.wait_ge(sig("heads_ready"), b_h + n + 1)
                job = jobs[n]
                off = job["off"]
                o = 3072 + (n % 2) * 512
                act.activation(job["out"], PS[off:off + 64, o:o + P], ACT.Copy).then_inc(sig("heads_copied"), 1)

            per = len(jobs[0]["q"])
            made = 0
            for n in range(len(jobs)):
                for s in range(made, min((n + 1) * per + ahead - 1, len(maps))):
                    exps(s)
                    made = s + 1
                copy_turned(n)
                if n >= 1:
                    copy_heads(n - 1)
            copy_heads(len(jobs) - 1)

        def pe_rope(pe, chunks):
            b = base("pe", "rotated", len(chunks))
            for n, (c, perm, _, _) in enumerate(chunks):
                if n >= 4:
                    pe.wait_ge(sig("rotated"), b + n - 3)
                pe.matmul(PS[:, (n % 4) * 512:(n % 4) * 512 + T], perm, c, start=True, stop=True).then_inc(sig("swapped"), 1)

        def dve_rope(dve, chunks, chain):
            b = base("dve", "swapped", len(chunks))
            for n, (c, _, cos, sin) in enumerate(chunks):
                dve.wait_ge(sig("swapped"), b + n + 1)
                tmp = ROPE_TMP[:, (n % 2) * T:(n % 2) * T + T]
                dve.tensor_tensor(tmp, PS[:, (n % 4) * 512:(n % 4) * 512 + T], sin, ALU.mult)
                chain(dve.tensor_tensor(c, c, cos, ALU.mult))
                dve.tensor_tensor(c, c, tmp, ALU.add).then_inc(sig("rotated"), 1)

        ROPE_TMP = WORK[:, 8192:9216]

        QK1 = BIG[:, 0:16 * T].rearrange("p (k t) -> p k t", k=16)
        V1 = BIG[:, 16 * T:24 * T].rearrange("p (a c) -> p a c", a=NT)
        COS1, SIN1, TMP1, POS = [BIG[:, n * T:(n + 1) * T] for n in range(24, 28)]

        def dve_angles(dve, chain):
            dve.wait_ge(tables_loaded, 16)
            chain(dve.tensor_copy(POS, POS.bitcast(I32)))
            chain(dve.tensor_scalar(POS, POS, const("freq"), None, ALU.mult))
            for dst, ahead in ((COS1, 0.25), (SIN1, 0.0)):
                chain(dve.tensor_scalar(TMP1, POS, 1 / TWO_PI, ahead, ALU.mult, ALU.add))
                chain(dve.tensor_scalar(TMP1, TMP1, ROUND, ROUND, ALU.add, ALU.subtract))
                chain(dve.scalar_tensor_tensor(out=dst, in0=TMP1, scalar=-PI_A, in1=POS, op0=ALU.mult, op1=ALU.add))
                chain(dve.scalar_tensor_tensor(out=dst, in0=TMP1, scalar=-PI_B, in1=dst, op0=ALU.mult, op1=ALU.add))
                chain(dve.scalar_tensor_tensor(out=dst, in0=TMP1, scalar=-PI_C, in1=dst, op0=ALU.mult, op1=ALU.add))
                if ahead:
                    chain(dve.tensor_scalar(dst, dst, np.pi / 2, None, ALU.add))
                ins = dve.tensor_scalar(dst, dst, 3.1415925, -3.1415925, ALU.min, ALU.max)
                if ahead:
                    chain(ins)
            ins.then_inc(sig("angles_ready"), 1)

        def causal_jobs():
            jobs = []
            for h in range(8):
                r = slice((h % 2) * 64, (h % 2) * 64 + 64)
                for i in range(NT):
                    pieces = [(0, 0, i * P, None)] if i else []
                    pieces.append((i * P, i * P, P, const("causal")))
                    jobs.append(dict(q=[QK1[r, h // 2, i * P:(i + 1) * P]],
                                     k=[[(0, QK1[r, 4 + h // 2, 0:(i + 1) * P])]],
                                     v=[V1[:, a, h * 64:(h + 1) * 64] for a in range(i + 1)],
                                     pieces=pieces, scale=0.125, sink=None, off=(h % 2) * 64,
                                     out=H[r, h // 2, i * P:(i + 1) * P]))
            return jobs

        OFFS = [0, 512, 1024, 896]
        SBW = 1280
        SP_ = [WORK[:, n * SBW:(n + 1) * SBW] for n in range(2)]
        SW = [WORK[:, (2 + n) * SBW:(3 + n) * SBW] for n in range(2)]

        def sb_bank(h, i):
            return (h % 2) * 1536 + OFFS[i]

        def pe_stick(pe):
            def z(h):
                if h >= 2:
                    pe.wait_ge(sig("sticks_read"), h - 1)
                r = slice((h % 2) * 64, (h % 2) * 64 + 64)
                for i in (0, 1, 3, 2):
                    a, w = sb_bank(h, i), T - i * P
                    mm = pe.matmul(PS[:, a:a + w], QK1[r, 12 + h // 2, i * P:(i + 1) * P],
                                   QK1[r, 8 + h // 2, i * P:T], start=i != 3, stop=True, skip_group_check=True)
                mm.then_inc(sig("z_ready"), 1)

            def sums(h):
                pe.wait_ge(sig("softplus_masked"), h + 1)
                for i in (0, 1, 3, 2):
                    for j in range(i, NT):
                        a = sb_bank(h, i) + (j - i) * P
                        w = T - j * P
                        mm = pe.matmul(PS[:, a:a + w], const("negtri") if j == i else const("negones"),
                                       SP_[h % 2][:, OFFS[j]:OFFS[j] + w], start=False, stop=True, skip_group_check=True)
                mm.then_inc(sig("sticks_ready"), 1)

            def outputs(h):
                pe.wait_ge(sig("sticks_masked"), h + 1)
                if h >= 2:
                    pe.wait_ge(sig("stick_heads_copied"), h - 1)
                off = (h % 2) * 64
                for i in range(NT):
                    o = 3072 + (h % 2) * 512
                    mm = pe.matmul(PS[off:off + 64, o + i * P:o + T], V1[:, i, 512 + h * 64:512 + (h + 1) * 64],
                                   SW[h % 2][:, OFFS[i]:OFFS[i] + T - i * P], start=i == 0, stop=i == NT - 1,
                                   skip_group_check=True)
                mm.then_inc(sig("stick_heads_ready"), 1)

            z(0)
            for h in range(8):
                if h + 1 < 8:
                    z(h + 1)
                sums(h)
                if h >= 1:
                    outputs(h - 1)
            outputs(7)

        def act_stick(act, chain):
            def softplus(h):
                act.wait_ge(sig("z_ready"), h + 1)
                if h >= 2:
                    act.wait_ge(sig("sticks_ready"), h - 1)
                L, a = SP_[h % 2], (h % 2) * 1536
                chain(act.activation(L, PS[:, a:a + SBW], ACT.Abs))
                chain(act.activation(L, L, ACT.Exp, scale=-1.0))
                act.activation(L, L, ACT.Ln, bias=SM[:, 1:2]).then_inc(sig("log_ready"), 1)

            def weights(h):
                act.wait_ge(sig("sticks_ready"), h + 1)
                if h >= 2:
                    act.wait_ge(sig("stick_heads_ready"), h - 1)
                a = (h % 2) * 1536
                act.activation(SW[h % 2], PS[:, a:a + SBW], ACT.Exp).then_inc(sig("sticks_read"), 1)

            def copy(h):
                off = (h % 2) * 64
                act.wait_ge(sig("stick_heads_ready"), h + 1)
                act.activation(H[off:off + 64, 4 + h // 2, 0:T], PS[off:off + 64, 3072 + (h % 2) * 512:3072 + (h % 2) * 512 + T],
                               ACT.Copy).then_inc(sig("stick_heads_copied"), 1)

            softplus(0)
            for h in range(8):
                if h + 1 < 8:
                    softplus(h + 1)
                weights(h)
                if h >= 1:
                    copy(h - 1)
            copy(7)

        def dve_stick(dve):
            for h in range(8):
                dve.wait_ge(sig("log_ready"), h + 1)
                a = (h % 2) * 1536
                dve.scalar_tensor_tensor(out=SP_[h % 2], in0=PS[:, a:a + SBW], scalar=0.0, in1=SP_[h % 2],
                                         op0=ALU.max, op1=ALU.add).then_inc(sig("softplus_ready"), 1)

        def pool_stick(pool):
            def keep_past(buf):
                for i in range(NT):
                    v = buf[:, OFFS[i]:OFFS[i] + P]
                    ins = pool.affine_select(out=v, in_=v, compare_op=ALU.is_gt, fill=0.0, base=0,
                                             pattern=[[1, P]], channel_multiplier=-1)
                return ins
            def soft(h):
                pool.wait_ge(sig("softplus_ready"), h + 1)
                keep_past(SP_[h % 2]).then_inc(sig("softplus_masked"), 1)
            soft(0)
            for h in range(8):
                if h + 1 < 8:
                    soft(h + 1)
                pool.wait_ge(sig("sticks_read"), h + 1)
                keep_past(SW[h % 2]).then_inc(sig("sticks_masked"), 1)
        def rope1_chunks():
            return [(QK1[:, x, :], const("perm_a1"), COS1, SIN1) for x in range(8)]

        FIN_G = [par("fin_g").rearrange("p (l k v) -> p l k v", l=2, v=1)[:, n, :, :] for n in range(2)]
        GQ = BIG[:, 0:32 * T].rearrange("p (k t) -> p k t", k=32)
        CONV_IN = [WORK[:, n * 1030:n * 1030 + 1030].rearrange("p (j t) -> p j t", j=2) for n in range(2)]
        CONV_OUT = [WORK[:, 2080 + n * 1024:3104 + n * 1024] for n in range(2)]
        GATES = WORK[:, 2080:2080 + T]
        HF = H[:, :, :].rearrange("p k t -> p (k t)")
        KTOK = HF[:, 0:8 * T].rearrange("p (h c d) -> p h c d", h=GH, c=NT)
        VTOK = BIG[:, 16 * T:24 * T].rearrange("p (h c d) -> p h c d", h=GH, c=NT)
        GS0 = 4096 + 4 * P + 1024
        AB = HF[:, GS0:GS0 + 64].rearrange("p (c n) -> p c n", c=NT)

        def gate_vec(n):
            return HF[:, GS0 + 64 + 32 * n:GS0 + 96 + 32 * n]
        GRAW, BETA, GCUM, NCOEF, EG, EKD, EGL, GTMP = [gate_vec(n) for n in range(8)]
        STATE = HF[:, 4096:4096 + 4 * P].rearrange("p (h e) -> p h e", h=4)
        VNEW = HF[:, 4096 + 4 * P:4096 + 8 * P]
        QEXP = HF[:, 4096 + 8 * P:4096 + 12 * P]
        SEL = lambda v, c, h: v[:, c * GH + h:c * GH + h + 1]

        def round_halves(act, t, u, i):
            g = G0["gdn_in"] + u
            for j in range(2):
                if j == 0:
                    act.wait_ge(tile_loaded[g % SLOTS], (i + g // SLOTS + 1) * 16)
                if not isinstance(t, int) or t > 0:
                    if j == 0:
                        act.wait_ge(sig("half_done"), t)
                    else:
                        act.wait_ge(tile_done, t + G0["gdn_in"])
                act.activation(U_HI[:, j, :].rearrange("p (k c) -> p k c", k=DC), half_tile(g % SLOTS, j),
                               ACT.Copy).then_inc(sig("half_rounded"), 1)

        def rest_halves(pool, t, u):
            for j in range(2):
                pool.wait_ge(sig("half_rounded"), t * 2 + (j + 1))
                pool.tensor_tensor(U_LO[:, j, :].rearrange("p (k c) -> p k c", k=DC), half_tile((G0["gdn_in"] + u) % SLOTS, j),
                                   U_HI[:, j, :].rearrange("p (k c) -> p k c", k=DC).bitcast(F32),
                                   ALU.subtract).then_inc(sig("half_split"), 1)

        def half_tile(slot, j):
            return ring[:, slot, :].rearrange("p (k c) -> p k c", k=DC)[:, :, j * P:(j + 1) * P]

        def pool_gdn_in(pool):
            over_tiles(pool, 16, lambda t, u, i: rest_halves(pool, t + 1, u + 1))

        def act_gdn_in(act):
            g0 = G0["gdn_in"]
            b = base("act", "convolved", 12)

            act.drain().then_inc(sig("conv_silu"), 2)

            def silu(t, u):
                act.wait_ge(sig("convolved"), t + (b + 9))
                act.activation(GQ[:, bass.ds(t * 2, 2), :], CONV_OUT[u % 2].rearrange("p (j c) -> p j c", j=2),
                               ACT.Silu).then_inc(sig("conv_silu"), 1)

            def body(t, u, i):
                round_halves(act, t + 1, u + 1, i)
                act.wait_ge(tile_done, t + (g0 + 1))
                act.wait_ge(sig("convolved"), t + (b + 7))
                act.activation(CONV_IN[u % 2][:, :, 3:3 + T], PS[:, (u % 4) * 1024:(u % 4 + 1) * 1024]
                               .rearrange("p (j c) -> p j c", j=2), ACT.Copy).then_inc(evac_done, 1)
                if not isinstance(t, int) or t > 0:
                    silu(t - 1, u - 1)
            for t in range(SLOTS):
                body(t, t, 0)
            with act.Fori(1, 3) as i:
                for u in range(SLOTS):
                    body(i * SLOTS + u, u, i)
            for t in range(12, 16):
                round_halves(act, t + 1, t + 1, 0)
                if t == 12:
                    silu(11, 11)
                act.wait_ge(tile_done, g0 + t + 1)
                act.activation(GQ[:, 2 * t:2 * t + 2, :], PS[:, (t - 12) * 1024:(t - 11) * 1024]
                               .rearrange("p (j c) -> p j c", j=2), ACT.Silu).then_inc(evac_done, 1)
            act.wait_ge(sig("gates_ready"), 1)
            act.activation(GATES, PS[:, 0:T], ACT.Copy).then_inc(sig("gates_copied"), 1)
            act.wait_ge(tile_done, g0 + 17)
            act.activation(AB, PS[:, 512:1024].rearrange("p (c n) -> p c n", c=NT)[:, :, 0:2 * GH], ACT.Copy).then_inc(evac_done, 1)

        def dve_gdn_in(dve, chain):
            e0 = E0["gdn_in"]
            b = 2
            dve.memset(CONV_IN[0][:, :, 0:3], 0.0)
            dve.memset(CONV_IN[1][:, :, 0:3], 0.0).then_inc(sig("convolved"), 8)
            dve.wait_ge(sig("convolved"), 8)
            w = par("gconv").rearrange("p (k n) -> p k n", k=4)

            def body(t, u, i):
                dve.wait_ge(evac_done, t + (e0 + 1))
                src = CONV_IN[u % 2]
                y2 = CONV_OUT[u % 2].rearrange("p (j c) -> p j c", j=2)
                dve.wait_ge(sig("conv_silu"), t + (b - 1))
                for tap in range(4):
                    for j in range(2):
                        y = y2[:, j:j + 1, :]
                        x = src[:, j:j + 1, tap:tap + T]
                        s = w[:, tap, bass.ds(t * 2 + j, 1)]
                        if tap == 0:
                            ins = dve.tensor_scalar(y, x, s, None, ALU.mult)
                        else:
                            ins = dve.scalar_tensor_tensor(out=y, in0=x, scalar=s, in1=y, op0=ALU.mult, op1=ALU.add)
                    if tap < 3:
                        chain(ins)
                    else:
                        ins.then_inc(sig("convolved"), 1)
            body.steps = 3
            over_tiles(dve, 12, body, chain)

        def pe_gdn_in(pe):
            e0 = E0["gdn_in"]
            normed = wait_normed(pe)

            def body(t, u, i):
                pe.wait_ge(evac_done, t + (e0 - 3))
                for j in range(2):
                    pe.wait_ge(sig("half_split"), t * 2 + (j + 1))
                    col = lambda k: slice(k * P, (k + 1) * P)
                    mm = pe_three(pe, (u % 4) * 1024 + j * 512, T, lambda k: U_HI[:, j, col(k)], lambda k: U_LO[:, j, col(k)],
                                  lambda k: H_HI[:, k, :], lambda k: H_LO[:, k, :], DC, normed if j == 0 else None)
                    mm.then_inc(tile_done if j else sig("half_done"), 1)
            over_tiles(pe, 16, body)
            pe.wait_ge(evac_done, e0 + 13)
            pe.wait_ge(sig("half_split"), 34)
            pe_three(pe, 0, T, lambda k: U_HI[:, 0, k * P:(k + 1) * P], lambda k: U_LO[:, 0, k * P:(k + 1) * P],
                     lambda k: H_HI[:, k, :], lambda k: H_LO[:, k, :], DC).then_inc(sig("gates_ready"), 1)
            pe.wait_ge(sig("gates_copied"), 1)
            for a in range(NT):
                mm = pe.transpose(PS[:, 512 + a * P:512 + (a + 1) * P], GATES[:, a * P:(a + 1) * P], ident)
            mm.then_inc(tile_done, 1)

        L2_RSTD = [WORK[:, (2 + n) * T:(3 + n) * T] for n in range(16)]

        def act_gdn_prep(act, chain):
            for n in range(16):
                act.wait_ge(sig("l2_summed"), n + 1)
                s = float(P) if n < 8 else 1.0
                act.activation(L2_RSTD[n], PS[:, (n % 2) * 512:(n % 2) * 512 + T], ACT.Ln, scale=s,
                               bias=SM[:, 2:3] if n < 8 else SM[:, 0:1]).then_inc(sig("l2_log"), 1)
            act.wait_ge(sig("l2_log"), 16)
            for n in range(16):
                act.activation(L2_RSTD[n], L2_RSTD[n], ACT.Exp, scale=-0.5).then_inc(sig("l2_rstd"), 1)
            act.wait_ge(sig("dt_added"), 1)
            a = AB[:, :, 0:GH]
            t3 = GTMP.rearrange("p (c n) -> p c n", c=NT)
            chain(act.activation(t3, a, ACT.Abs))
            chain(act.activation(GTMP, GTMP, ACT.Exp, scale=-1.0))
            chain(act.activation(GTMP, GTMP, ACT.Ln, bias=SM[:, 1:2]))
            act.activation(BETA.rearrange("p (c n) -> p c n", c=NT), AB[:, :, GH:2 * GH], ACT.Exp, scale=-1.0)
            act.activation(SM[:, 24:32], par("alog"), ACT.Exp).then_inc(sig("gate_parts"), 1)
            act.wait_ge(sig("gcum_ready"), 1)
            act.activation(EG, GCUM, ACT.Exp)
            act.activation(EKD, GTMP, ACT.Exp)
            act.activation(EGL, PS[:, 2048 + 32:2048 + 64], ACT.Exp).then_inc(sig("gate_exps"), 1)

        def pool_gdn_prep(pool):
            for n in range(16):
                if n >= 2:
                    pool.wait_ge(sig("l2_summed"), n - 1)
                pool.tensor_tensor(WORK[:, (n % 2) * T:(n % 2 + 1) * T], GQ[:, n, :], GQ[:, n, :],
                                   ALU.mult).then_inc(sig("l2_squared"), 1)

        def pe_gdn_prep(pe):
            for n in range(16):
                pe.wait_ge(sig("l2_squared"), n + 1)
                if n >= 2:
                    pe.wait_ge(sig("l2_log"), n - 1)
                pe.matmul(PS[:, (n % 2) * 512:(n % 2) * 512 + T], ones, WORK[:, (n % 2) * T:(n % 2 + 1) * T],
                          start=True, stop=True).then_inc(sig("l2_summed"), 1)
            pe.wait_ge(sig("graw_ready"), 1)
            pe.matmul(PS[:, 2048:2048 + 32], const("tri"), GRAW, start=True, stop=True)
            pe.matmul(PS[:, 2048 + 32:2048 + 64], ones, GRAW, start=True, stop=True).then_inc(sig("gsums_ready"), 1)
            for n in range(16):
                h = n % 8
                if n < 8:
                    pe.wait_ge(sig("l2_scaled"), 9 + h)
                if n >= 2:
                    pe.wait_ge(sig("tokens_copied"), n - 1)
                for c in range(NT):
                    mm = pe.transpose(PS[:, 1024 + (n % 2) * 512 + c * P:1024 + (n % 2) * 512 + (c + 1) * P],
                                      GQ[:, 8 + n, c * P:(c + 1) * P], ident)
                mm.then_inc(sig("tokens_turned"), 1)

        def dve_gdn_prep(dve, chain):
            a = AB[:, :, 0:GH]
            for c in range(NT):
                ins = dve.tensor_tensor(AB[:, c, 0:GH], AB[:, c, 0:GH], par("dtb"), ALU.add)
            ins.then_inc(sig("dt_added"), 1)
            for n in range(16):
                dve.wait_ge(sig("l2_rstd"), n + 1)
                dve.tensor_tensor(GQ[:, n, :], GQ[:, n, :], L2_RSTD[n],
                                  ALU.mult).then_inc(sig("l2_scaled"), 1)
            dve.wait_ge(sig("gate_parts"), 1)
            t3 = GTMP.rearrange("p (c n) -> p c n", c=NT)
            chain(dve.scalar_tensor_tensor(out=t3, in0=a, scalar=0.0, in1=t3, op0=ALU.max, op1=ALU.add))
            for c in range(NT):
                ins = dve.scalar_tensor_tensor(out=GRAW[:, c * GH:(c + 1) * GH], in0=GTMP[:, c * GH:(c + 1) * GH],
                                               scalar=-1.0, in1=SM[:, 24:32], op0=ALU.mult, op1=ALU.mult)
            ins.then_inc(sig("graw_ready"), 1)
            chain(dve.tensor_scalar(BETA, BETA, 1.0, None, ALU.add))
            chain(dve.reciprocal(BETA, BETA))
            dve.wait_ge(sig("gsums_ready"), 1)
            chain(dve.tensor_copy(GCUM, PS[:, 2048:2048 + 32]))
            dve.scalar_tensor_tensor(out=GTMP, in0=GCUM, scalar=-1.0, in1=PS[:, 2048 + 32:2048 + 64], op0=ALU.mult,
                                     op1=ALU.add).then_inc(sig("gcum_ready"), 1)
            dve.wait_ge(sig("gate_exps"), 1)
            dve.scalar_tensor_tensor(out=NCOEF, in0=EG, scalar=-1.0, in1=BETA, op0=ALU.mult, op1=ALU.mult)
            for n in range(16):
                h = n % 8
                dve.wait_ge(sig("tokens_turned"), n + 1)
                src = PS[:, 1024 + (n % 2) * 512:1024 + (n % 2) * 512 + T].rearrange("p (c d) -> p c d", c=NT)
                dst, by = (KTOK, EKD) if n < 8 else (VTOK, BETA)
                for c in range(NT):
                    ins = dve.tensor_scalar(dst[:, h, c, :], src[:, c, :], SEL(by, c, h), None, ALU.mult)
                ins.then_inc(sig("tokens_copied"), 1)

        def gbuf(par_, n):
            o = 4096 + par_ * 2560 + n * T
            return WORK[:, o:o + T]
        XT = [WORK[:, n * T:(n + 1) * T] for n in range(4)]
        AT = [WORK[:, (4 + n) * T:(5 + n) * T] for n in range(4)]
        LEVELS = 7

        def gps(q, n, c=None):
            o = (q * 3 + n) * 512
            return PS[:, o:o + T] if c is None else PS[:, o + c * P:o + (c + 1) * P]

        def blk(v, c):
            return v[:, c * P:(c + 1) * P]

        def pe_gdn_inverse(pe, grp):
            kT = lambda h, c: GQ[:, 8 + h, c * P:(c + 1) * P]
            for n in range(0, 4, 2):
                for q in range(2):
                    h = grp * 4 + n + q
                    N = grp * 4 + n + q
                    pe.wait_ge(sig("tri_scaled"), N + 1)
                    if N >= 2:
                        pe.wait_ge(sig("inverse_step" + str(q)), (N // 2) * LEVELS)
                    pe.matmul(gps(q, 0), ones, gbuf(q, 4), start=True, stop=True)
                    for c in range(NT):
                        pe.matmul(gps(q, 1, c), kT(h, c), kT(h, c), start=True, stop=True)
                    for c in range(NT):
                        mm = pe.matmul(gps(q, 2, c), kT(h, c), GQ[:, h, c * P:(c + 1) * P], start=True, stop=True)
                    mm.then_inc(sig("products_ready"), 1)
                for q in range(2):
                    N = grp * 4 + n + q
                    pe.wait_ge(sig("level_masked" + str(q)), (N // 2) * LEVELS + 1)
                    for c in range(NT):
                        mm = pe.transpose(gps(q, 0, c), blk(gbuf(q, 1), c), ident)
                    mm.then_inc(sig("m0_turned"), 1)
                for lv in range(1, LEVELS):
                    for q in range(2):
                        N = grp * 4 + n + q
                        X_, T_, V_, M_ = XT[n + q], gbuf(q, 3), gbuf(q, 4), gbuf(q, 1 + lv % 2)
                        pe.wait_ge(sig("inverse_step" + str(q)), (N // 2) * LEVELS + lv)
                        pe.wait_ge(sig("level_masked" + str(q)), (N // 2) * LEVELS + lv + 1)
                        for c in range(NT):
                            mm = pe.matmul(gps(q, 0, c), blk(M_, c), blk(X_, c), start=True, stop=True)
                        mm.then_inc(sig("mx_ready" + str(q)), 1)
                    for q in range(2):
                        N = grp * 4 + n + q
                        X_, T_, V_ = XT[n + q], gbuf(q, 3), gbuf(q, 4)
                        pe.wait_ge(sig("mx_copied" + str(q)), (N // 2) * (LEVELS - 1) + lv)
                        for c in range(NT):
                            mm = pe.matmul(gps(q, 1, c), blk(T_, c), blk(V_, c), start=True, stop=True)
                        if lv < LEVELS - 1:
                            for c in range(NT):
                                mm = pe.matmul(gps(q, 2, c), blk(V_, c), blk(T_, c), start=True, stop=True)
                        mm.then_inc(sig("update_ready" + str(q)), 1)

        def dve_gdn_inverse(dve, grp):
            for n in range(0, 4, 2):
                for q in range(2):
                    h = N = grp * 4 + n + q
                    if N >= 2:
                        dve.wait_ge(sig("update_ready" + str(q)), (N // 2) * (LEVELS - 1))
                    for c in range(NT):
                        ins = dve.tensor_scalar(blk(gbuf(q, 4), c), const("tri"), SEL(GRAW, c, h), None, ALU.mult)
                    ins.then_inc(sig("tri_scaled"), 1)
                for q in range(2):
                    h = N = grp * 4 + n + q
                    dve.wait_ge(sig("products_ready"), N + 1)
                    if N >= 2:
                        dve.wait_ge(sig("level_masked" + str(q)), (N // 2) * LEVELS)
                    for c in range(NT):
                        dve.tensor_scalar(blk(AT[n + q], c), gps(q, 0, c), SEL(GCUM, c, h), 0.0, ALU.subtract, ALU.min)
                        ins = dve.tensor_scalar(blk(gbuf(q, 0), c), gps(q, 0, c), SEL(GCUM, c, h), 0.0, ALU.subtract, ALU.max)
                    ins.then_inc(sig("gaps_ready"), 1)
                for q in range(2):
                    h = N = grp * 4 + n + q
                    dve.wait_ge(sig("decay_masked"), N + 1)
                    dve.tensor_tensor(AT[n + q], AT[n + q], gps(q, 2), ALU.mult)
                    for c in range(NT):
                        ins = dve.scalar_tensor_tensor(out=blk(gbuf(q, 0), c), in0=gps(q, 1, c), scalar=SEL(BETA, c, h),
                                                       in1=blk(gbuf(q, 0), c), op0=ALU.mult, op1=ALU.mult)
                    ins.then_inc(sig("lower_ready"), 1)
                for q in range(2):
                    N = grp * 4 + n + q
                    dve.wait_ge(sig("level_masked" + str(q)), (N // 2) * LEVELS + 1)
                    dve.wait_ge(sig("m0_turned"), N + 1)
                    for c in range(NT):
                        dve.tensor_tensor(blk(gbuf(q, 3), c), ident, blk(gbuf(q, 1), c), ALU.subtract)
                        ins = dve.tensor_tensor(blk(XT[n + q], c), ident, gps(q, 0, c), ALU.subtract)
                    ins.then_inc(sig("inverse_step" + str(q)), 1)
                for lv in range(1, LEVELS):
                    for q in range(2):
                        N = grp * 4 + n + q
                        dve.wait_ge(sig("update_ready" + str(q)), (N // 2) * (LEVELS - 1) + lv)
                        dve.wait_ge(sig("inverse_step" + str(q)), (N // 2) * LEVELS + lv)
                        if lv < LEVELS - 1:
                            dve.tensor_tensor(gbuf(q, 3), gbuf(q, 3), gps(q, 2), ALU.subtract)
                        dve.tensor_tensor(XT[n + q], XT[n + q], gps(q, 1), ALU.subtract).then_inc(sig("inverse_step" + str(q)), 1)

        def act_gdn_inverse(act, grp):
            for n in range(0, 4, 2):
                for q in range(2):
                    N = grp * 4 + n + q
                    act.wait_ge(sig("gaps_ready"), N + 1)
                    act.activation(AT[n + q], AT[n + q], ACT.Exp)
                    act.activation(gbuf(q, 0), gbuf(q, 0), ACT.Exp, scale=-1.0).then_inc(sig("decay_ready"), 1)
                for lv in range(1, LEVELS):
                    for q in range(2):
                        N = grp * 4 + n + q
                        act.wait_ge(sig("mx_ready" + str(q)), (N // 2) * (LEVELS - 1) + lv)
                        act.activation(gbuf(q, 4), gps(q, 0), ACT.Copy).then_inc(sig("mx_copied" + str(q)), 1)

        def pool_gdn_inverse(pool, grp):
            for n in range(0, 4, 2):
                for q in range(2):
                    N = grp * 4 + n + q
                    pool.wait_ge(sig("decay_ready"), N + 1)
                    a3 = AT[n + q].rearrange("p (c s) -> p c s", c=NT)
                    l3 = gbuf(q, 0).rearrange("p (c s) -> p c s", c=NT)
                    pool.affine_select(out=a3, in_=a3, compare_op=ALU.is_ge, fill=0.0, base=0,
                                       pattern=[[0, NT], [1, P]], channel_multiplier=-1)
                    pool.affine_select(out=l3, in_=l3, compare_op=ALU.is_gt, fill=0.0, base=0,
                                       pattern=[[0, NT], [-1, P]], channel_multiplier=1).then_inc(sig("decay_masked"), 1)
                for lv in range(LEVELS):
                    mask = const("level")[:, lv * P:(lv + 1) * P]
                    for q in range(2):
                        N = grp * 4 + n + q
                        if lv == 0:
                            pool.wait_ge(sig("lower_ready"), N + 1)
                        if lv == 2:
                            pool.wait_ge(sig("inverse_step" + str(q)), (N // 2) * LEVELS + 1)
                        if lv > 2:
                            pool.wait_ge(sig("mx_ready" + str(q)), (N // 2) * (LEVELS - 1) + lv - 2)
                        for c in range(NT):
                            ins = pool.tensor_tensor(blk(gbuf(q, 1 + lv % 2), c), blk(gbuf(q, 0), c), mask, ALU.mult)
                        ins.then_inc(sig("level_masked" + str(q)), 1)
        def bank4(n, h=None):
            return PS[:, n * 512:n * 512 + 512] if h is None else PS[:, n * 512 + h * P:n * 512 + (h + 1) * P]

        def hs(v, h):
            return v[:, h * P:(h + 1) * P]
        RHS = [WORK[:, 8192:8704], WORK[:, 8704:9216]]

        def pe_scan(pe, grp):
            for c in range(NT):
                n = grp * NT + c
                ns = grp * (NT - 1) + c
                kT = lambda h: GQ[:, 8 + grp * 4 + h, c * P:(c + 1) * P]
                qT = lambda h: GQ[:, grp * 4 + h, c * P:(c + 1) * P]
                if c:
                    pe.wait_ge(sig("state_ready"), ns)
                    for h in range(4):
                        pe.matmul(bank4(0, h), kT(h), STATE[:, h, :], start=True, stop=True)
                    for h in range(4):
                        mm = pe.matmul(bank4(1, h), qT(h), STATE[:, h, :], start=True, stop=True)
                    mm.then_inc(sig("from_state"), 1)
                    pe.wait_ge(sig("rhs_ready"), ns)
                for h in range(4):
                    rhs = hs(RHS[0], h) if c else VTOK[:, grp * 4 + h, c, :]
                    mm = pe.matmul(bank4(2, h), blk(XT[h], c), rhs, start=True, stop=True)
                mm.then_inc(sig("vnew_ready"), 1)
                pe.wait_ge(sig("vnew_copied"), n + 1)
                if c < NT - 1:
                    for h in range(4):
                        mm = pe.matmul(bank4(3, h), KTOK[:, grp * 4 + h, c, :], hs(VNEW, h), start=True, stop=True)
                    mm.then_inc(sig("state_sums"), 1)
                if n:
                    pe.wait_ge(sig("out_stored"), n)
                for h in range(4):
                    mm = pe.matmul(bank4(4, h), blk(AT[h], c), hs(VNEW, h), start=True, stop=True)
                mm.then_inc(sig("out_ready"), 1)

        def dve_scan(dve, grp):
            for c in range(NT):
                n = grp * NT + c
                ns = grp * (NT - 1) + c
                if c:
                    dve.wait_ge(sig("from_state"), ns)
                    for h in range(4):
                        ins = dve.scalar_tensor_tensor(out=hs(RHS[0], h), in0=bank4(0, h), scalar=SEL(NCOEF, c, grp * 4 + h),
                                                       in1=VTOK[:, grp * 4 + h, c, :], op0=ALU.mult, op1=ALU.add)
                    ins.then_inc(sig("rhs_ready"), 1)
                if c < NT - 1:
                    dve.wait_ge(sig("state_sums"), ns + 1)
                    for h in range(4):
                        if c:
                            ins = dve.scalar_tensor_tensor(out=STATE[:, h, :], in0=STATE[:, h, :],
                                                           scalar=SEL(EGL, c, grp * 4 + h), in1=bank4(3, h),
                                                           op0=ALU.mult, op1=ALU.add)
                        else:
                            ins = dve.tensor_copy(STATE[:, h, :], bank4(3, h))
                    ins.then_inc(sig("state_ready"), 1)
                    dve.wait_ge(sig("state_ready"), ns + 1)
                dve.wait_ge(sig("out_ready"), n + 1)
                out = VTOK[:, grp * 4:grp * 4 + 4, c, :]
                o = bank4(4).rearrange("p (h e) -> p h e", h=4)
                if c:
                    dve.wait_ge(sig("q_state_scaled"), ns)
                    ins = dve.tensor_tensor(out, QEXP.rearrange("p (h e) -> p h e", h=4), o, ALU.add)
                else:
                    ins = dve.tensor_copy(out, o)
                ins.then_inc(sig("out_stored"), 1)

        def act_scan(act, grp):
            for c in range(NT):
                n = grp * NT + c
                ns = grp * (NT - 1) + c
                if c:
                    act.wait_ge(sig("from_state"), ns)
                    act.wait_ge(sig("out_stored"), n)
                    for h in range(4):
                        ins = act.activation(hs(QEXP, h), bank4(1, h), ACT.Copy, scale=SEL(EG, c, grp * 4 + h))
                    ins.then_inc(sig("q_state_scaled"), 1)
                act.wait_ge(sig("vnew_ready"), n + 1)
                if n:
                    act.wait_ge(sig("out_ready"), n)
                act.activation(VNEW, bank4(2), ACT.Copy).then_inc(sig("vnew_copied"), 1)

        OSQ = [WORK[:, n * T:(n + 1) * T] for n in range(8)]
        O_RSTD = SM[:, 8:40]

        def act_gdn_out(act, chain):
            for h in range(GH):
                act.activation(OSQ[h].rearrange("p (c e) -> p c e", c=NT), VTOK[:, h, :, :],
                               ACT.Square).then_inc(sig("o_squared"), 1)
            act.wait_ge(sig("o_summed"), 1)
            chain(act.activation(O_RSTD, O_RSTD, ACT.Ln, scale=1.0 / P, bias=SM[:, 0:1]))
            act.activation(O_RSTD, O_RSTD, ACT.Exp, scale=-0.5).then_inc(sig("o_rstd"), 1)

        def dve_gdn_out(dve):
            for h in range(GH):
                dve.wait_ge(sig("o_squared"), h + 1)
                ins = dve.tensor_reduce(O_RSTD[:, h * NT:(h + 1) * NT], OSQ[h].rearrange("p (c e) -> p c e", c=NT), AX_X, ALU.add)
            ins.then_inc(sig("o_summed"), 1)
            dve.wait_ge(sig("o_rstd"), 1)

            def normed(h):
                for c in range(NT):
                    ins = dve.tensor_scalar(VTOK[:, h, c, :], VTOK[:, h, c, :], O_RSTD[:, h * NT + c:h * NT + c + 1], None, ALU.mult)
                ins.then_inc(sig("o_normed"), 1)
            normed(0)
            for h in range(GH):
                if h + 1 < GH:
                    normed(h + 1)
                dve.wait_ge(sig("o_turned"), h + 1)
                dve.scalar_tensor_tensor(out=H[:, h, 0:T], in0=PS[:, (h % 2) * 512:(h % 2) * 512 + T], scalar=par("gnorm"),
                                         in1=GQ[:, 24 + h, :], op0=ALU.mult, op1=ALU.mult).then_inc(sig("gated"), 1)

        def pe_gdn_out(pe):
            for h in range(GH):
                pe.wait_ge(sig("o_normed"), h + 1)
                if h >= 2:
                    pe.wait_ge(sig("gated"), h - 1)
                for c in range(NT):
                    mm = pe.transpose(PS[:, (h % 2) * 512 + c * P:(h % 2) * 512 + (c + 1) * P], VTOK[:, h, c, :], ident)
                mm.then_inc(sig("o_turned"), 1)

        Q2 = BIG[:, 0:15 * TA].rearrange("p (k t) -> p k t", k=15)
        V2 = BIG[:, 15 * TA:15 * TA + 6 * 640].rearrange("p (a c) -> p a c", a=6)
        UB, UG, QA, QC, KC, QD, KD, KA = 0, 2, 4, 6, 8, 10, 12, 14
        GW = 15 + T + 15 + 15 + TC + 15
        GLU = WORK[:, 0:2 * GW].rearrange("p (j t) -> p j t", j=2)
        YW = GW - 30
        YC = WORK[:, 2 * GW:2 * GW + 2 * YW].rearrange("p (j t) -> p j t", j=2)
        GE = WORK[:, 3300:3300 + 2 * TA].rearrange("p (j t) -> p j t", j=2)
        CTX0 = T + 30
        LAST = 3

        def in_tiles(layer):
            q = SEG1 if layer == LAST else SEG2
            return [(0, 4, 2, q), (4, 1, 2, SEG2), (5, 1, 2, q), (6, 1, 2, SEG2), (7, 1, 1, SEG2)]

        def pe_in(pe, layer):
            for first, n, chunks, segs in in_tiles(layer):
                pe_feature_tiles(pe, f"in{layer}", H, segs, n, first, chunks, nb=2)
            pe_token_tiles(pe, f"in{layer}", TA, 2, 8, nb=2)
            pe_token_tiles(pe, f"in{layer}", TA, 1, 10, cols=P, nb=2)

        def act_in(act, layer):
            for first, n, chunks, segs in in_tiles(layer):
                if first == 0:
                    act_copy_tiles(act, f"in{layer}", Q2, segs, 2, 0, chunks, nb=2)
                    act.wait_ge(evac_done, E0[f"in{layer}"] + 2)
                    w = sum(x for _, x in segs)
                    act.activation(GE[:, :, 0:w], Q2[:, UG:UG + 2, 0:w], ACT.Sigmoid).then_inc(sig("glu_gate"), 1)
                    act_copy_tiles(act, f"in{layer}", Q2, segs, 2, 2, chunks, nb=2)
                else:
                    act_copy_tiles(act, f"in{layer}", Q2, segs, n, first, chunks, nb=2)
            act_token_tiles(act, f"in{layer}", V2, TA, 2, 8, nb=2)
            act_token_tiles(act, f"in{layer}", V2, TA, 1, 10, cols=P, nb=2, col0=512)

        def dve_in(dve, layer, chain):
            l = layer - 2
            segs = SEG1 if layer == LAST else SEG2
            chain(dve.memset(WORK[:, 0:2 * GW], 0.0))
            b = base("dve", "glu_gate", 1)
            dve.wait_ge(sig("glu_gate"), b + 1)
            for (c0, x), o in zip(segs, (15, T + 45)):
                ins = dve.tensor_tensor(GLU[:, :, o:o + x], Q2[:, UB:UB + 2, c0:c0 + x], GE[:, :, c0:c0 + x], ALU.mult)
            chain(ins)
            cw = par("cw").rearrange("p (l j k) -> p l j k", l=2, j=2)
            cb = par("cb").rearrange("p (l j) -> p l j", l=2)
            yw = T if layer == LAST else YW
            for tap in range(31):
                for j in range(2):
                    y, x = YC[:, j, 0:yw], GLU[:, j, tap:tap + yw]
                    if tap == 0:
                        ins = dve.tensor_scalar(y, x, cw[:, l, j, 0:1], cb[:, l, j:j + 1], ALU.mult, ALU.add)
                    else:
                        ins = dve.scalar_tensor_tensor(out=y, in0=x, scalar=cw[:, l, j, tap:tap + 1], in1=y,
                                                       op0=ALU.mult, op1=ALU.add)
                chain(ins)

        YSQ = WORK[:, 3300:3300 + 2 * TA].rearrange("p (j t) -> p j t", j=2)
        YR = WORK[:, 4900:4900 + TA]
        TAB = WORK[:, 5700:5700 + 4 * T].rearrange("p (n t) -> p n t", n=4)

        def yseg(layer):
            return [(0, 0, T)] if layer == LAST else [(0, 0, T), (CTX0, T, TC)]

        def rope2_chunks():
            return [(Q2[:, x, 0:T], const("perm_64"), TAB[:, 0, :], TAB[:, 1, :]) for x in (QA, QA + 1, KA)] + \
                   [(Q2[:, x, 0:T], const("perm_32"), TAB[:, 2, :], TAB[:, 3, :]) for x in (QC, QC + 1, KC, KC + 1)]

        def pe_conv_norm(pe, layer):
            b2 = base("pe", "y_squared", 1)
            for y0, o, w in yseg(layer):
                for j in range(2):
                    mm = pe.matmul(PS[:, 2048 + o:2048 + o + w], ones, YC[:, j, y0:y0 + w], start=j == 0, stop=j == 1)
            mm.then_inc(sig("y_summed"), 1)
            pe_rope(pe, rope2_chunks())
            pe.wait_ge(sig("y_squared"), b2 + 1)
            for y0, o, w in yseg(layer):
                for j in range(2):
                    mm = pe.matmul(PS[:, 3072 + o:3072 + o + w], ones, YSQ[:, j, o:o + w], start=j == 0, stop=j == 1)
            mm.then_inc(sig("y_squares_summed"), 1)

        def act_conv_norm(act, layer, chain):
            b = base("act", "centered", 1)
            bs = base("act", "y_squares_summed", 1)
            bn = base("act", "y_normed", 1)
            act.wait_ge(sig("centered"), b + 1)
            for y0, o, w in yseg(layer):
                ins = act.activation(YSQ[:, :, o:o + w], YC[:, :, y0:y0 + w], ACT.Square)
            ins.then_inc(sig("y_squared"), 1)
            act.wait_ge(sig("y_squares_summed"), bs + 1)
            w = T if layer == LAST else TA
            chain(act.activation(YR[:, 0:w], PS[:, 3072:3072 + w], ACT.Ln, scale=1.0 / 256, bias=SM[:, 0:1]))
            act.activation(YR[:, 0:w], YR[:, 0:w], ACT.Exp, scale=-0.5).then_inc(sig("y_rstd"), 1)
            act.wait_ge(sig("y_normed"), bn + 1)
            act.activation(H[:, 2:4, 0:w], H[:, 2:4, 0:w], ACT.Silu)

        def dve_conv_norm(dve, layer, chain):
            l = layer - 2
            b1 = base("dve", "y_summed", 1)
            b2 = base("dve", "y_rstd", 1)
            bt = base("dve", "tables_loaded", 16)
            dve.wait_ge(sig("y_summed"), b1 + 1)
            for y0, o, w in yseg(layer):
                for j in range(2):
                    ins = dve.scalar_tensor_tensor(out=YC[:, j, y0:y0 + w], in0=PS[:, 2048 + o:2048 + o + w],
                                                   scalar=-1.0 / 256, in1=YC[:, j, y0:y0 + w], op0=ALU.mult, op1=ALU.add)
            ins.then_inc(sig("centered"), 1)
            dve.wait_ge(tables_loaded, 16 + bt + 16)
            dve_rope(dve, rope2_chunks(), chain)
            dve.wait_ge(sig("y_rstd"), b2 + 1)
            g = par("lng").rearrange("p (l j) -> p l j", l=2)
            be = par("lnb").rearrange("p (l j) -> p l j", l=2)
            for y0, o, w in yseg(layer):
                for j in range(2):
                    ins = dve.tensor_tensor(H[:, 2 + j, o:o + w], YC[:, j, y0:y0 + w], YR[:, o:o + w], ALU.mult)
            chain(ins)
            w = T if layer == LAST else TA
            for j in range(2):
                ins = dve.tensor_scalar(H[:, 2 + j, 0:w], H[:, 2 + j, 0:w], g[:, l, j:j + 1], be[:, l, j:j + 1],
                                        ALU.mult, ALU.add)
            ins.then_inc(sig("y_normed"), 1)
            lq = par("lq").rearrange("p (l n d) -> p l n d", l=2, n=4)
            for m in range(2):
                dve.tensor_tensor(LTMP[:, m, :], lq[:, l, 2 * m, :], lq[:, l, 2 * m + 1, :], ALU.mult)
            chain(dve.memset(SM[:, 42:43], 0.0))
            dve.tensor_reduce(SM[:, 40:42], LTMP, AX_X, ALU.add).then_inc(sig("lam_sums"), 1)
            bl = base("dve", "lam_exps", 1)
            dve.wait_ge(sig("lam_exps"), bl + 1)
            chain(dve.tensor_tensor(SM[:, 42:43], SM[:, 41:42], SM[:, 40:41], ALU.subtract))
            dve.tensor_scalar(SM[:, 42:43], SM[:, 42:43], -lambda_init(l), None, ALU.add)

        LTMP = WORK[:, 7800:7864].rearrange("p (m d) -> p m d", m=2)

        def lambda_init(l):
            return 0.8 - 0.6 * float(np.exp(-0.3 * l))

        def act_lambda(act):
            b = base("act", "lam_sums", 1)
            act.wait_ge(sig("lam_sums"), b + 1)
            act.activation(SM[:, 40:42], SM[:, 40:42], ACT.Exp).then_inc(sig("lam_exps"), 1)

        SLOTN = 14
        BT = WORK[:, 6 * TA:6 * TA + 4 * SLOTN * 64].rearrange("p (h s c) -> p h s c", h=4, s=SLOTN)

        def pe_bias(pe, l):
            rpb = par("rpb").rearrange("p (l h r) -> p l h r", l=2, h=4)
            hot = const("onehot")
            for rnd in range(8):
                for cc in range(8):
                    c = rnd * 8 + cc
                    for p in range(2):
                        o = rnd * 512 + cc * 56
                        mm = pe.matmul(PS[p * 64:p * 64 + 64, o:o + 4 * SLOTN].rearrange("p (h s) -> p h s", h=4),
                                       hot[0:31, 63 - c:127 - c], rpb[0:31, l, :, 1 - p:15 - p], start=True, stop=True)
                mm.then_inc(sig("bias_ready"), 1)

        def dve_bias(dve):
            b = base("dve", "bias_ready", 8)
            for rnd in range(8):
                dve.wait_ge(sig("bias_ready"), b + rnd + 1)
                src = PS[:, rnd * 512:rnd * 512 + 448].rearrange("p (c h s) -> p h s c", c=8, h=4)
                mask = const("colmask")[:, rnd * 8:rnd * 8 + 8]
                for h in range(4):
                    dve.tensor_tensor(BT[:, h, :, rnd * 8:rnd * 8 + 8], src[:, h, :, :],
                                      mask.rearrange("p (a c) -> p a c", a=1).to_broadcast([P, SLOTN, 8]), ALU.add)

        def mixer_jobs(layer):
            l = layer - 2
            singles, doubles = [], []
            sinks = par("sink").rearrange("p (l h) -> p l h", l=2)
            qtiles = range(NT if layer == LAST else TA // P)
            for h in range(4):
                g = h // 2
                r = slice(g * 64, g * 64 + 64)
                out_r = slice((h % 2) * 64, (h % 2) * 64 + 64)
                vs = lambda a: V2[:, a, 512 + g * 64:512 + g * 64 + 64]
                for i in qtiles:
                    q = Q2[r, QA + h % 2, i * P:(i + 1) * P]
                    if i < NT:
                        lo, hi = max(i - 1, 0), min(i + 1, NT - 1)
                        n1 = (hi - lo + 1) * P
                        ks = [(0, Q2[r, KA, lo * P:(hi + 1) * P]), (512, Q2[r, KA, T:TA])]
                        band = const("bands")[:, (lo - i + 1) * P:(hi - i + 2) * P]
                        pieces = [(0, 0, n1, band), (n1, 512, TC, None)]
                        v = [vs(a) for a in range(lo, hi + 1)] + [vs(4), vs(5)]
                    else:
                        ks = [(0, Q2[r, KA, T:TA])]
                        pieces = [(0, 0, TC, None)]
                        v = [vs(4), vs(5)]
                    singles.append(dict(q=[q], k=[ks], v=v, pieces=pieces, scale=0.125, sink=sinks[:, l, h:h + 1],
                                        off=(h % 2) * 64, out=H[out_r, h // 2, i * P:(i + 1) * P]))
            for h in range(4):
                r = slice((h % 2) * 64, (h % 2) * 64 + 64)
                vs = lambda a: V2[:, a, 256 + h * 64:256 + h * 64 + 64]
                for i in qtiles:
                    q = Q2[r, QD + h // 2, i * P:(i + 1) * P]
                    kv = lambda a, b: Q2[r, KD + h // 2, a:b]
                    if i < NT:
                        ks = [(0, kv(0, T)), (512, kv(T, TA))]
                        bias = BT[:, h, 6 - 2 * i:14 - 2 * i, :].rearrange("p s c -> p (s c)")
                        pieces = [(0, 0, T, bias), (T, 512, TC, None)]
                        v = [vs(a) for a in range(6)]
                    else:
                        ks, pieces, v = [(0, kv(T, TA))], [(0, 0, TC, None)], [vs(4), vs(5)]
                    singles.append(dict(q=[q], k=[ks], v=v, pieces=pieces, scale=0.125, sink=None,
                                        off=(h % 2) * 64, out=H[r, 6 + h // 2, i * P:(i + 1) * P]))
            for h in range(4):
                vs = lambda a: V2[:, a, h * 64:h * 64 + 64]
                for i in qtiles:
                    qs, ks = [], []
                    for m in range(2):
                        r = slice((h % 2) * 64 + m * 32, (h % 2) * 64 + m * 32 + 32)
                        qs.append(Q2[r, QC + h // 2, i * P:(i + 1) * P])
                        kv = lambda a, b: Q2[r, KC + h // 2, a:b]
                        ks.append([(0, kv(0, T)), (512, kv(T, TA))] if i < NT else [(0, kv(T, TA))])
                    full = i < NT
                    r = slice((h % 2) * 64, (h % 2) * 64 + 64)
                    doubles.append(dict(q=qs, k=ks, v=[vs(a) for a in (range(6) if full else (4, 5))],
                                        pieces=[(0, 0, TA if full else TC, None)], scale=32 ** -0.5, sink=None,
                                        neg_lam=SM[:, 42:43], off=(h % 2) * 64, out=H[r, 4 + h // 2, i * P:(i + 1) * P]))
            return singles, doubles

        def act_sub_norm(act, layer, chain):
            w = T if layer == LAST else TA
            b = base("act", "heads_summed", 2)
            for n in range(2):
                act.activation(WORK[:, n * TA:n * TA + w], H[:, 4 + n, 0:w], ACT.Square).then_inc(sig("heads_squared"), 1)
            for n in range(2):
                act.wait_ge(sig("heads_summed"), b + n + 1)
                R = WORK[:, (2 + n) * TA:(2 + n) * TA + w]
                chain(act.activation(R, PS[:, n * 1024:n * 1024 + w], ACT.Ln, scale=1.0 / 64, bias=SM[:, 0:1]))
                act.activation(R, R, ACT.Exp, scale=-0.5).then_inc(sig("heads_rstd"), 1)

        def pe_sub_norm(pe, layer):
            b = base("pe", "heads_squared", 2)
            for n in range(2):
                pe.wait_ge(sig("heads_squared"), b + n + 1)
                for c0, w in SEG1 if layer == LAST else SEG2:
                    mm = pe.matmul(PS[:, n * 1024 + c0:n * 1024 + c0 + w], const("half64"), WORK[:, n * TA + c0:n * TA + c0 + w],
                                   start=True, stop=True)
                mm.then_inc(sig("heads_summed"), 1)

        def dve_sub_norm(dve, layer, chain):
            l = layer - 2
            w = T if layer == LAST else TA
            b = base("dve", "heads_rstd", 2)
            chain(dve.tensor_scalar(SM[:, 43:44], par("subg")[:, l:l + 1], 1.0 - lambda_init(l), None, ALU.mult))
            for n in range(2):
                dve.wait_ge(sig("heads_rstd"), b + n + 1)
                dve.scalar_tensor_tensor(out=H[:, 4 + n, 0:w], in0=H[:, 4 + n, 0:w], scalar=SM[:, 43:44],
                                         in1=WORK[:, (2 + n) * TA:(2 + n) * TA + w], op0=ALU.mult, op1=ALU.mult)
        OUTPUT = ("attn_out", "gdn_out", "out2", "out3")
        block = ctx.enter_context(nc.Block())

        @block.sync
        def _(sp):
            sp.dma_start(PR[:, :], params).then_inc(params_loaded, 16)
            def read_off(name, u, i):
                if name in SPLIT and not (side(name) and u % 2):
                    apart = 2 if side(name) else 1
                    return sig("tile_split"), i * (SLOTS // apart) + (SPLIT[name] + u // apart + 1)
                return tile_done, i * SLOTS + (G0[name] + u + 1)

            order = [(name, t) for name, _, n, _, _, _ in linear_plan() for t in range(n)]
            for name, kind, n, _, step, _ in linear_plan():
                src, width = (w_tiles, TILE) if kind == "w" else (d_tiles, DOWN)

                def load(u, i, last):
                    if last:
                        sp.wait_ge(*read_off(*last))
                    slot = (G0[name] + u) % SLOTS
                    sp.dma_start(ring[:, slot:slot + 1, 0:width],
                                 src[bass.ds((i * SLOTS + u) * step + FROM[name], 1), :, :]
                                 .rearrange("a p c -> p a c")).then_inc(tile_loaded[slot], 16)

                def load_one(t):
                    g = G0[name] + t
                    load(t, 0, (*order[g - SLOTS], 0) if g >= SLOTS else None)
                for t in range(min(n, SLOTS)):
                    load_one(t)
                if name == "ada0":
                    sp.dma_start(CN[:, :], consts).then_inc(consts_loaded, 16)
                    sp.dma_start(X[:, :, 0:T], xT).then_inc(x_loaded, 16)
                    sp.dma_start(X[:, :, T:TA], ctxT).then_inc(x_loaded, 16)
                    sp.dma_start(POS.bitcast(I32), positions.to_broadcast([P, T])).then_inc(tables_loaded, 16)
                rounds = n // SLOTS
                if rounds > 1:
                    with sp.Fori(1, rounds) as i:
                        for u in range(SLOTS):
                            load(u, i, (name, u, i - 1))
                for t in range(max(rounds, 1) * SLOTS, n):
                    load_one(t)
            for k in range(DC):
                sp.wait_ge(sig("out_normed"), k + 1)
                sp.dma_start(outT[:, k, :], H[:, k, 0:T]).then_inc(stored, 16)
            sp.wait_ge(stored, 16 * DC)

        @block.tensor
        def _(pe):
            ph = Phase()
            pe.wait_ge(consts_loaded, 16)
            for layer in range(4):
                segs = SEG1 if layer < 2 or layer == LAST else SEG2
                if layer == 0:
                    pe_ada0(pe)
                    ph.end(pe)
                if layer < 2:
                    pe_split_norm(pe, T)
                else:
                    pe_norm(pe, SEG2)
                    ph.end(pe)
                if layer == 0:
                    pe_attn_in(pe)
                    ph.end(pe)
                    pe_rope(pe, rope1_chunks())
                    ph.end(pe)
                    pe_attention(pe, causal_jobs())
                    ph.end(pe)
                    pe_stick(pe)
                    ph.end(pe)
                    pe_out(pe, "attn_out", SEG1)
                elif layer == 1:
                    pe_gdn_in(pe)
                    ph.end(pe)
                    pe_gdn_prep(pe)
                    ph.end(pe)
                    for grp in range(2):
                        pe_gdn_inverse(pe, grp)
                        ph.end(pe)
                        pe_scan(pe, grp)
                        ph.end(pe)
                    pe_gdn_out(pe)
                    ph.end(pe)
                    pe_out(pe, "gdn_out", SEG1)
                else:
                    pe_in(pe, layer)
                    ph.end(pe)
                    pe_conv_norm(pe, layer)
                    ph.end(pe)
                    pe_bias(pe, layer - 2)
                    ph.end(pe)
                    singles, doubles = mixer_jobs(layer)
                    pe_attention(pe, singles)
                    ph.end(pe)
                    pe_attention(pe, doubles)
                    ph.end(pe)
                    pe_sub_norm(pe, layer)
                    ph.end(pe)
                    pe_out(pe, f"out{layer}", segs)
                ph.end(pe)
                for s, c0, w in passes(layer):
                    pe_split_norm(pe, w)
                    for half in range(2):
                        pe_up(pe, layer, f"up{layer}{s}{half}", w)
                        pe_down(pe, layer, f"down{layer}{s}{half}", w)
                    ph.end(pe)
                if layer in (1, 3):
                    pe_norm(pe, SEG1)
                    ph.end(pe)

        @block.scalar
        def _(act):
            ph = Phase()
            chain = Chain(act, act_chain)
            act.wait_ge(params_loaded, 16)
            act.activation(SC[:, :], PR[:, 0:3 * DC], ACT.Silu).then_inc(sig("c_silu"), 1)
            act.drain().then_inc(evac_done, 8)
            for layer in range(4):
                segs = SEG1 if layer < 2 or layer == LAST else SEG2
                if layer == 0:
                    act.wait_ge(x_loaded, 32)
                    ph.end(act)
                mod = MOD[:, layer % 2, :, :]
                if layer < 2:
                    if layer == 1:
                        round_halves(act, 0, 0, 0)
                    act_split_norm(act, ("attn_in", "gdn_in")[layer], 0, T, chain, mod[:, 0:DC, 0])
                else:
                    act_norm(act, SEG2, chain, mod[:, 0:DC, :])
                    ph.end(act)
                if layer == 0:
                    act_attn_in(act)
                    ph.end(act)
                    act.wait_ge(sig("angles_ready"), 1)
                    act.activation(QK1[:, 8:12, :], QK1[:, 8:12, :], ACT.Copy, scale=0.125)
                    chain(act.activation(COS1, COS1, ACT.Sin))
                    chain(act.activation(SIN1, SIN1, ACT.Sin))
                    act.activation(SIN1, SIN1, ACT.Copy, scale=const("sign")).then_inc(sig("angles_done"), 1)
                    ph.end(act)
                    act_attention(act, causal_jobs(), chain)
                    ph.end(act)
                    act_stick(act, chain)
                    ph.end(act)
                elif layer == 1:
                    act_gdn_in(act)
                    ph.end(act)
                    act_gdn_prep(act, chain)
                    ph.end(act)
                    for grp in range(2):
                        act_gdn_inverse(act, grp)
                        ph.end(act)
                        act_scan(act, grp)
                        ph.end(act)
                    act_gdn_out(act, chain)
                    ph.end(act)
                else:
                    act_in(act, layer)
                    ph.end(act)
                    act.dma_start(TAB, rope_tables).then_inc(tables_loaded, 16)
                    act_conv_norm(act, layer, chain)
                    act_lambda(act)
                    ph.end(act)
                    ph.end(act)
                    singles, doubles = mixer_jobs(layer)
                    act_attention(act, singles, chain)
                    ph.end(act)
                    act_attention(act, doubles, chain)
                    ph.end(act)
                    act_sub_norm(act, layer, chain)
                    ph.end(act)
                act_out(act, OUTPUT[layer], segs)
                ph.end(act)
                for s, c0, w in passes(layer):
                    act_split_norm(act, f"up{layer}{s}0", c0, w, chain, mod[:, 3 * DC:4 * DC, s])
                    for half in range(2):
                        act_up(act, f"up{layer}{s}{half}", w)
                        act_round(act, f"down{layer}{s}{half}")
                    ph.end(act)
                if layer in (1, 3):
                    act_norm(act, SEG1, chain)
                    ph.end(act)

        @block.vector
        def _(dve):
            ph = Phase()
            chain = Chain(dve, dve_chain)
            dve.memset(SM[:, 0:1], EPS)
            dve.memset(SM[:, 1:2], 1.0)
            dve.memset(SM[:, 2:3], P * EPS)
            dve.wait_ge(sig("c_silu"), 1)
            for layer in range(4):
                segs = SEG1 if layer < 2 or layer == LAST else SEG2
                if layer == 0:
                    dve_ada0(dve, chain)
                    ph.end(dve)
                mod = MOD[:, layer % 2, :, :]
                if layer < 2:
                    dve_split_norm(dve, ("attn_in", "gdn_in")[layer], 0, T, GAIN[:, layer, 0, :, 0], mod[:, 0:DC, 0])
                else:
                    dve_norm(dve, SEG2, GAIN[:, layer % 2, 0, :, :], H, "norm_scaled")
                    ph.end(dve)
                if layer == 0:
                    dve_angles(dve, chain)
                    dve_attn_in(dve, chain)
                    ph.end(dve)
                    dve.wait_ge(sig("angles_done"), 1)
                    dve_rope(dve, rope1_chunks(), chain)
                    ph.end(dve)
                    dve_attention(dve, causal_jobs(), chain)
                    ph.end(dve)
                    dve_stick(dve)
                    ph.end(dve)
                    dve_out(dve, "attn_out", mod[:, 2 * DC:3 * DC, :], SEG1)
                elif layer == 1:
                    dve_gdn_in(dve, chain)
                    ph.end(dve)
                    dve_gdn_prep(dve, chain)
                    ph.end(dve)
                    for grp in range(2):
                        dve_gdn_inverse(dve, grp)
                        ph.end(dve)
                        dve_scan(dve, grp)
                        ph.end(dve)
                    dve_gdn_out(dve)
                    ph.end(dve)
                    dve_out(dve, "gdn_out", mod[:, 2 * DC:3 * DC, :], SEG1)
                else:
                    dve_in(dve, layer, chain)
                    ph.end(dve)
                    dve_conv_norm(dve, layer, chain)
                    ph.end(dve)
                    dve_bias(dve)
                    ph.end(dve)
                    singles, doubles = mixer_jobs(layer)
                    dve_attention(dve, singles, chain)
                    ph.end(dve)
                    dve_attention(dve, doubles, chain)
                    ph.end(dve)
                    dve_sub_norm(dve, layer, chain)
                    ph.end(dve)
                    dve_out(dve, f"out{layer}", mod[:, 2 * DC:3 * DC, :], segs)
                ph.end(dve)
                for s, c0, w in passes(layer):
                    dve_split_norm(dve, f"up{layer}{s}0", c0, w, GAIN[:, layer % 2, 1, :, s], mod[:, 3 * DC:4 * DC, s])
                    for half in range(2):
                        dve_up(dve, layer, f"up{layer}{s}{half}", w, chain)
                        dve_down(dve, layer, f"down{layer}{s}{half}", mod[:, 5 * DC:6 * DC, s], c0, w, chain)
                    ph.end(dve)
                if layer in (1, 3):
                    dve_norm(dve, SEG1, FIN_G[layer // 2], *((X, "block_normed") if layer == 1 else (H, "out_normed")))
                    ph.end(dve)

        @block.gpsimd
        def _(pool):
            ph = Phase()
            for layer in range(4):
                if layer == 0:
                    ph.end(pool)
                    rest_tile(pool, "attn_in", 0, 0, 0)
                    pool_rest(pool, "attn_in")
                    ph.end(pool)
                elif layer == 1:
                    rest_halves(pool, 0, 0)
                    pool_gdn_in(pool)
                    ph.end(pool)
                else:
                    ph.end(pool)
                    ph.end(pool)
                if layer == 0:
                    ph.end(pool)
                    ph.end(pool)
                    pool_stick(pool)
                    ph.end(pool)
                elif layer == 1:
                    pool_gdn_prep(pool)
                    ph.end(pool)
                    for grp in range(2):
                        pool_gdn_inverse(pool, grp)
                        ph.end(pool)
                        ph.end(pool)
                    ph.end(pool)
                else:
                    for _ in range(5):
                        ph.end(pool)
                rest_tile(pool, OUTPUT[layer], 0, 0, 0)
                pool_rest(pool, OUTPUT[layer])
                ph.end(pool)
                for s, _, _ in passes(layer):
                    if takes_rest(f"up{layer}{s}0") == "gpsimd":
                        rest_tile(pool, f"up{layer}{s}0", 0, 0, 0)
                    for half in range(2):
                        pool_rest(pool, f"up{layer}{s}{half}")
                        pool_rest(pool, f"down{layer}{s}{half}")
                    ph.end(pool)
                if layer in (1, 3):
                    ph.end(pool)


def constants():
    c = np.zeros((P, CONST_W), np.float32)

    def put(name, v):
        a, w = CONST[name]
        c[:v.shape[0], a:a + w] = v
    i, j = np.arange(P)[:, None], np.arange(P)[None, :]
    put("ident", np.eye(P))
    put("ones", np.ones((P, P)))
    put("tri", i <= j)
    put("negtri", -1.0 * (i >= j))
    put("negones", -np.ones((P, P)))

    def swap(width, half):
        m = np.zeros((P, P))
        for x in range(P):
            y = x % width
            if y < 2 * half:
                m[x + half if y < half else x - half, x] = 1
        return m
    put("perm_a1", swap(64, 8))
    put("perm_64", swap(64, 32))
    put("perm_32", swap(32, 16))
    put("causal", np.where(j <= i, 0, NEG))
    put("bands", np.concatenate([np.where(j >= i, 0, NEG), np.zeros((P, P)), np.where(j <= i, 0, NEG)], 1))
    levels = []
    for lv in range(7):
        s = 1 << lv
        levels.append((i // (2 * s) == j // (2 * s)) & (i % (2 * s) >= s) & (j % (2 * s) < s))
    put("level", np.concatenate(levels, 1))
    put("onehot", (np.arange(31)[:, None] == 78 - j).astype(np.float32))
    q, k = np.arange(64)[:, None], np.arange(64)[None, :]
    start = np.clip(q - 8, 0, 48)
    put("colmask", np.tile(np.where((k >= start) & (k < start + 16), 0, NEG), (2, 1)))
    put("half64", i // 64 == j // 64)
    freq = np.float32(500000.0) ** (-np.arange(8, dtype=np.float32) * np.float32(2.0) / np.float32(16))
    f, s = np.zeros((P, 1)), np.zeros((P, 1))
    for x in range(P):
        if x % 64 < 16:
            f[x] = freq[x % 8]
            s[x] = -1 if x % 64 < 8 else 1
    put("freq", f)
    put("sign", s)
    return c


def axial_tables():
    out = np.zeros((P, 4, T), np.float32)
    t = np.arange(T)
    row, col = (t // 64).astype(np.float32), (t % 64).astype(np.float32)
    for n, dim in enumerate((64, 32)):
        nf = dim // 4
        inv = np.float32(10000.0) ** (-np.arange(nf, dtype=np.float32) / np.float32(nf))
        ang = np.concatenate([row[:, None] * inv, col[:, None] * inv], -1)
        for x in range(P):
            y = x % dim
            a = ang[:, y % (dim // 2)]
            out[x, 2 * n] = np.cos(a)
            out[x, 2 * n + 1] = np.sin(a) * (-1 if y < dim // 2 else 1)
    return out


def column_tiles(w):
    n = w.shape[1] // 256
    return w.reshape(DC, P, n, 256).transpose(2, 1, 0, 3).reshape(n, P, TILE)


def padded(w, width=256):
    return np.pad(w, ((0, 0), (0, width - w.shape[1])))


def up_tiles(gate, up):
    g, u = gate.reshape(D, FC, P), up.reshape(D, FC, P)
    return column_tiles(np.stack([g, u], 2).reshape(D, 2 * F))


def down_tiles(w):
    return w.reshape(2, FC // 2, P, DC, P).transpose(0, 3, 2, 1, 4).reshape(2 * DC, P, DOWN)


def in_turn(a, b):
    return np.stack([a, b], 1).reshape(2 * len(a), P, TILE)


def in_halves(up, ada):
    return [in_turn(up[:UP], ada[:UP]), ada[UP:UP + 1], in_turn(up[UP:], ada[UP + 1:2 * UP + 1]), ada[2 * UP + 1:]]


def weight_tiles(i):
    w, d = [], []
    ada = [column_tiles(i["ada_w"][0]), column_tiles(i["ada_w"][1]), column_tiles(i["w_ada_2"][0]), column_tiles(i["w_ada_2"][1])]
    for layer in range(4):
        if layer < 2:
            if layer == 0:
                w.append(ada[0][:ADA // 2])
                a = i["attn_w_in"][0]
                tiles = column_tiles(np.concatenate([a[:, 0:1024], a[:, 1536:2560], a[:, 1024:1536], a[:, 2560:3072]], 1))
                w.append(in_turn(tiles, ada[0][ADA // 2:]))
                w.append(column_tiles(i["attn_w_out"][0]))
            else:
                a = i["gdn_w_in"][0]
                w.append(column_tiles(np.concatenate([a[:, 0:4096], padded(a[:, 4096:])], 1)))
                w.append(column_tiles(i["gdn_w_out"][0]))
            a = i["ffn_w_in"][layer]
            w += in_halves(up_tiles(a[:, 0:F], a[:, F:]), ada[layer + 1])
            d.append(down_tiles(i["ffn_w_out"][layer]))
        else:
            l = layer - 2
            a = i["w_in_2"][l]
            qa, ka, va, ub, qc, kc, vc, qd, kd, vd = np.split(a, np.cumsum([256, 128, 128, 512, 256, 256, 256, 256, 256]), 1)
            qa = qa[:, np.r_[0:64, 128:192, 64:128, 192:256]]
            w.append(column_tiles(np.concatenate([ub, qa, qc, kc, qd, kd, padded(ka), vc, vd, padded(va)], 1)))
            w.append(column_tiles(i["w_out_2"][l]))
            up = up_tiles(i["w_gate_2"][l], i["w_up_2"][l])
            w += in_halves(up, ada[3]) if layer == 2 else [up]
            d.append(down_tiles(i["w_down_2"][l]))
    return np.concatenate(w), np.concatenate(d)


def parameters(i):
    p = np.zeros((P, PARAM_W), np.float32)

    def put(name, v):
        a, w = PARAM[name]
        p[:v.shape[0], a:a + w] = v.reshape(v.shape[0], w)

    def cols(v):
        v = np.asarray(v)
        return v.reshape(-1, P).T
    put("c1", cols(i["c"]))
    put("c2", np.stack([cols(i["c_2"]), cols(i["c_ctx_2"])], 2))
    put("ada_b", np.concatenate([cols(i["ada_b"]), cols(i["b_ada_2"])], 1))
    put("mix_g", np.concatenate([cols(i["norm_mix_g"]), cols(i["norm1_g_2"])], 1))
    put("ffn_g", np.concatenate([cols(i["norm_ffn_g"]), cols(i["norm2_g_2"])], 1))
    put("fin_g", np.concatenate([cols(i["final_norm_g"]), cols(i["final_g_2"])], 1))
    put("gconv", cols(i["gdn_conv_w"][0]))
    put("gnorm", cols(i["gdn_norm_g"]))
    put("alog", np.broadcast_to(i["gdn_a_log"], (P, GH)))
    put("dtb", np.broadcast_to(i["gdn_dt_bias"], (P, GH)))
    put("sink", np.broadcast_to(i["attn_sink_2"].reshape(1, 8), (P, 8)))
    put("cw", i["conv_w_2"].reshape(2, 31, 2, P).transpose(3, 0, 2, 1))
    put("cb", cols(i["conv_b_2"]))
    put("lng", cols(i["conv_ln_g_2"]))
    put("lnb", cols(i["conv_ln_b_2"]))
    lq = np.stack([i["diff_lq1_2"], i["diff_lk1_2"], i["diff_lq2_2"], i["diff_lk2_2"]], 1)
    put("lq", np.broadcast_to(lq.reshape(1, 256), (P, 256)))
    put("subg", np.concatenate([i["diff_subln_g_2"].T, i["diff_subln_g_2"].T], 0))
    put("rpb", i["na_rpb_2"].transpose(3, 0, 1, 2))
    return p


def kernel(**inputs):
    import concourse.bacc as bacc
    from concourse.bass_utils import run_bass_kernel_spmd

    i = {name: np.asarray(v) for name, v in inputs.items()}
    w, d = weight_tiles(i)
    arrays = {
        "w_tiles": w, "d_tiles": d,
        "xT": np.ascontiguousarray(i["x"][0].T.reshape(DC, P, T).transpose(1, 0, 2)),
        "ctxT": np.ascontiguousarray(i["ctx_2"][0].T.reshape(DC, P, TC).transpose(1, 0, 2)),
        "positions": i["positions"], "consts": constants(), "params": parameters(i), "rope_tables": axial_tables(),
    }
    nc = bacc.Bacc("TRN2", target_bir_lowering=False, num_devices=1)
    args = [nc.dram_tensor(name, a.shape, mybir.dt.from_np(a.dtype), kind="ExternalInput").ap() for name, a in arrays.items()]
    args.append(nc.dram_tensor("outT", (P, DC, T), F32, kind="ExternalOutput").ap())
    build_program(nc, *args)
    r = run_bass_kernel_spmd(nc, [arrays], core_ids=[0])
    out = r.results[0]["outT"]
    return np.ascontiguousarray(out.transpose(1, 0, 2).reshape(1, D, T).transpose(0, 2, 1))
```
